# Optimizing a Trainium2 kernel written in Bass

```python
import math
import jax, jax.numpy as jnp
from jax import lax
import numpy as np

D_MODEL = 1024
BATCH = 1
SEQ = 256
DEPTH = 1

HG_HEADS = 4
HG_DK = 128
HG_DV = 128
HG_W = HG_HEADS * HG_DV
HG_CHUNK = 64
HG_F_MIN = 1e-6
DA_HEADS = 4
DA_DQK = 64
DA_DV = 2 * DA_DQK
DA_W = DA_HEADS * DA_DV
DA_QBLOCK = 128
MASK_VALUE = -1e30
RW_HEADS = 8
RW_DH = 64
RW_W = RW_HEADS * RW_DH
RW_LORA_W = 64
RW_LORA_A = 64
RW_LORA_G = 128
RW_IN_SIZES = (RW_W, RW_W, RW_W, RW_LORA_W, RW_LORA_A, RW_LORA_G)
RW_IN_W = 1792
RW_GN_EPS = 64e-5
IN_SIZES = (HG_HEADS * HG_DK, HG_HEADS * HG_DK, HG_W, HG_W,
            DA_HEADS * 2 * DA_DQK, DA_HEADS * 2 * DA_DQK, DA_W, RW_IN_W)
IN_W = 5376
N_BRANCH = 3
MIX_W = HG_W + DA_W + RW_W
N_EXPERTS = 16
N_GROUPS = 4
EXPERTS_PER_GROUP = 4
TOP_K = 2
D_EXPERT = 512
ALPHA = (2.0 * DEPTH) ** 0.25
BETA = (8.0 * DEPTH) ** -0.25
LN_EPS = 1e-5
RMS_EPS = 1e-6

kernel_name = "hybrid_hgrn2_diffattn_rwkv7_groupmoe_deepnorm"

def _split_points(sizes):
    return [int(s) for s in np.cumsum(np.asarray(sizes))[:-1]]

def layer_norm(x, g, b):
    xf = x.astype(jnp.float32)
    mu = jnp.mean(xf, axis=-1, keepdims=True)
    var = jnp.mean(jnp.square(xf - mu), axis=-1, keepdims=True)
    return ((xf - mu) * lax.rsqrt(var + LN_EPS) * g.astype(jnp.float32) + b.astype(jnp.float32)).astype(x.dtype)

def rms_norm(x, g):
    xf = x.astype(jnp.float32)
    return xf * lax.rsqrt(jnp.mean(jnp.square(xf), axis=-1, keepdims=True) + RMS_EPS) * g.astype(jnp.float32)

def _token_shift(a):
    return jnp.pad(a, ((0, 0), (1, 0), (0, 0)))[:, :-1]

def _alibi_slopes(n):
    return jnp.asarray([2.0 ** (-8.0 * (h + 1) / n) for h in range(n)], jnp.float32)

def hgrn2_mixer(q, f_pre, i, og, lb, norm_g):
    B, T, _ = q.shape
    n = T // HG_CHUNK
    z = f_pre.astype(jnp.float32)
    lb = lb.astype(jnp.float32)
    f = lb + (1.0 - lb) * jax.nn.sigmoid(z)
    log_f = jnp.log(jnp.maximum(f, HG_F_MIN))
    k = (1.0 - lb) * jax.nn.sigmoid(-z)

    def to_chunks(a, d):
        return a.reshape(B, n, HG_CHUNK, HG_HEADS, d).transpose(1, 0, 3, 2, 4)

    qc = to_chunks(q.astype(jnp.float32), HG_DK)
    kc = to_chunks(k, HG_DK)
    vc = to_chunks(i.astype(jnp.float32), HG_DV)
    gc = to_chunks(log_f, HG_DK)
    causal = jnp.tril(jnp.ones((HG_CHUNK, HG_CHUNK), bool))[:, :, None]

    def step(S, inp):
        qb, kb, vb, gb = inp
        b = jnp.cumsum(gb, axis=2)
        diff = b[:, :, :, None, :] - b[:, :, None, :, :]
        decay = jnp.where(causal, jnp.exp(jnp.minimum(diff, 0.0)), 0.0)
        a = jnp.einsum('bhtk,bhtsk,bhsk->bhts', qb, decay, kb)
        o = jnp.einsum('bhts,bhsv->bhtv', a, vb) + jnp.einsum('bhtk,bhkv->bhtv', qb * jnp.exp(b), S)
        b_last = b[:, :, -1:, :]
        S = jnp.exp(b_last[:, :, 0, :])[..., None] * S + jnp.einsum('bhsk,bhsv->bhkv', kb * jnp.exp(b_last - b), vb)
        return S, o

    S0 = jnp.zeros((B, HG_HEADS, HG_DK, HG_DV), jnp.float32)
    _, o = lax.scan(step, S0, (qc, kc, vc, gc))
    o = o.transpose(1, 0, 3, 2, 4).reshape(B, T, HG_HEADS, HG_DV)
    o = rms_norm(o, norm_g) * jax.nn.silu(og.reshape(B, T, HG_HEADS, HG_DV).astype(jnp.float32))
    return o.reshape(B, T, HG_W).astype(q.dtype)

def diff_attention(q, k, v, lam, lam_init, subln_g):
    B, T, _ = q.shape
    q = q.reshape(B, T, DA_HEADS, 2, DA_DQK).transpose(0, 3, 2, 1, 4) * (DA_DQK ** -0.5)
    k = k.reshape(B, T, DA_HEADS, 2, DA_DQK).transpose(0, 3, 2, 1, 4)
    v = v.reshape(B, T, DA_HEADS, DA_DV).transpose(0, 2, 1, 3)
    slopes = _alibi_slopes(DA_HEADS)
    outs = []
    for blk in range(T // DA_QBLOCK):
        q0, q1 = blk * DA_QBLOCK, (blk + 1) * DA_QBLOCK
        s = jnp.einsum('bmhqd,bmhkd->bmhqk', q[:, :, :, q0:q1], k[:, :, :, :q1]).astype(jnp.float32)
        dist = (jnp.arange(q0, q1)[:, None] - jnp.arange(q1)[None, :]).astype(jnp.float32)
        s = jnp.where(dist >= 0, s - slopes[:, None, None] * dist, MASK_VALUE)
        p = jax.nn.softmax(s, axis=-1)
        p = p[:, 0] - lam * p[:, 1]
        outs.append(jnp.einsum('bhqk,bhkd->bhqd', p.astype(v.dtype), v[:, :, :q1]))
    o = jnp.concatenate(outs, axis=2)
    o = rms_norm(o, subln_g) * (1.0 - lam_init)
    return o.transpose(0, 2, 1, 3).reshape(B, T, DA_W).astype(v.dtype)

def rwkv7_mixer(xs, mu, w0, w_up, a0, a_up, g_up, k_k, k_a, r_k, gn_g, gn_b):
    B, T, _ = xs.shape
    mu, w0, w_up, a0, a_up, g_up, k_k, k_a, r_k, gn_g, gn_b = [
        p.astype(jnp.float32) for p in (mu, w0, w_up, a0, a_up, g_up, k_k, k_a, r_k, gn_g, gn_b)]
    xs = xs.astype(jnp.float32)
    xs = xs + (_token_shift(xs) - xs) * mu
    r, k, v, wd, ad, gd = jnp.split(xs, _split_points(RW_IN_SIZES), axis=-1)
    w_log = -jax.nn.softplus(-(w0 + jnp.tanh(wd) @ w_up)) - 0.5
    decay = jnp.exp(-jnp.exp(w_log))
    a = jax.nn.sigmoid(a0 + ad @ a_up)
    g = jax.nn.sigmoid(gd) @ g_up

    def hd(t):
        return t.reshape(B, T, RW_HEADS, RW_DH)

    kk = hd(k * k_k)
    kk = kk * lax.rsqrt(jnp.maximum(jnp.sum(jnp.square(kk), axis=-1, keepdims=True), 1e-12))
    k = k * (1.0 + (a - 1.0) * k_a)
    r, decay, k, v, a = hd(r), hd(decay), hd(k), hd(v), hd(a)

    def step(S, inp):
        r_t, w_t, k_t, v_t, a_t, b_t = inp
        S = (S * w_t[:, :, None, :]
             + jnp.einsum('bhvk,bhk->bhv', S, a_t)[..., None] * b_t[:, :, None, :]
             + v_t[..., None] * k_t[:, :, None, :])
        return S, jnp.einsum('bhvk,bhk->bhv', S, r_t)

    def tm(t):
        return jnp.swapaxes(t, 0, 1)

    S0 = jnp.zeros((B, RW_HEADS, RW_DH, RW_DH), jnp.float32)
    _, o = lax.scan(step, S0, (tm(r), tm(decay), tm(k), tm(v), tm(-kk), tm(kk * a)))
    o = tm(o)
    m = jnp.mean(o, axis=-1, keepdims=True)
    var = jnp.mean(jnp.square(o - m), axis=-1, keepdims=True)
    o = (o - m) * lax.rsqrt(var + RW_GN_EPS) * gn_g.reshape(RW_HEADS, RW_DH) + gn_b.reshape(RW_HEADS, RW_DH)
    o = o + jnp.sum(r * k * r_k, axis=-1, keepdims=True) * v
    return o.reshape(B, T, RW_W) * g

def hybrid_mixer(u, w_in, hg_lb, hg_norm_g, lam, lam_init, da_subln_g,
                 rw_mu, rw_w0, rw_w_up, rw_a0, rw_a_up, rw_g_up, rw_k_k, rw_k_a, rw_r_k, rw_gn_g, rw_gn_b,
                 w_merge, b_merge, w_branch, w_out):
    hg_q, hg_f, hg_i, hg_og, da_q, da_k, da_v, rw_x = jnp.split(
        jnp.einsum('btd,de->bte', u, w_in), _split_points(IN_SIZES), axis=-1)
    o_hg = hgrn2_mixer(hg_q, hg_f, hg_i, hg_og, hg_lb, hg_norm_g)
    o_da = diff_attention(da_q, da_k, da_v, lam, lam_init, da_subln_g)
    o_rw = rwkv7_mixer(rw_x, rw_mu, rw_w0, rw_w_up, rw_a0, rw_a_up, rw_g_up,
                       rw_k_k, rw_k_a, rw_r_k, rw_gn_g, rw_gn_b)
    wb_hg, wb_da, wb_rw = jnp.split(w_branch, _split_points((HG_W, DA_W, RW_W)), axis=0)
    merged = jnp.zeros_like(u)
    for br, (o, wb) in enumerate(((o_hg, wb_hg), (o_da, wb_da), (o_rw, wb_rw))):
        gate = jax.nn.sigmoid(u @ w_merge[br] + b_merge[br])
        merged = merged + gate * (o.astype(u.dtype) @ wb)
    return merged @ w_out

def grouped_moe(u, w_router, router_bias, w_gate, w_up, w_down):
    B, T, D = u.shape
    t = u.reshape(B * T, D)
    scores = jax.nn.softmax((t @ w_router).astype(jnp.float32), axis=-1)
    sel = scores + router_bias.astype(jnp.float32)
    grp_score = jnp.sum(lax.top_k(sel.reshape(-1, N_GROUPS, EXPERTS_PER_GROUP), TOP_K)[0], axis=-1)
    gmask = jax.nn.one_hot(jnp.argmax(grp_score, axis=-1), N_GROUPS, dtype=jnp.bool_)
    emask = jnp.repeat(gmask, EXPERTS_PER_GROUP, axis=-1)
    _, idx = lax.top_k(jnp.where(emask, sel, MASK_VALUE), TOP_K)
    w = jnp.take_along_axis(scores, idx, axis=-1)
    w = w / jnp.sum(w, axis=-1, keepdims=True)
    combine = jnp.sum(jax.nn.one_hot(idx, N_EXPERTS, dtype=jnp.float32) * w[..., None], axis=1).astype(t.dtype)
    y = jnp.zeros_like(t)
    for e in range(N_EXPERTS):
        h = jax.nn.silu(t @ w_gate[e]) * (t @ w_up[e])
        y = y + combine[:, e:e + 1] * (h @ w_down[e])
    return y.reshape(B, T, D)

def setup_inputs(seed: int = 0) -> dict:
    key = jax.random.key(seed)
    ks = iter(jax.random.split(key, 40))
    L, D = DEPTH, D_MODEL

    def nrm(shape, std):
        return std * jax.random.normal(next(ks), shape, jnp.float32)

    return {
        "x": nrm((BATCH, SEQ, D), 1.0),
        "c": nrm((BATCH, D), 1.0),
        "w_ada": nrm((L, D, 6 * D), 0.5 * D ** -0.5),
        "b_ada": nrm((L, 6 * D), 0.02),
        "w_in": nrm((L, D, IN_W), D ** -0.5),
        "hg_lb_logits": nrm((L, HG_HEADS * HG_DK), 1.0),
        "hg_norm_g": 1.0 + nrm((L, HG_DV), 0.02),
        "da_lambda": nrm((L, 4, DA_DQK), 0.1),
        "da_subln_g": 1.0 + nrm((L, DA_DV), 0.02),
        "rw_mu": jax.random.uniform(next(ks), (L, RW_IN_W), jnp.float32),
        "rw_w0": -1.0 + nrm((L, RW_W), 0.5),
        "rw_w_up": nrm((L, RW_LORA_W, RW_W), 0.1),
        "rw_a0": nrm((L, RW_W), 0.1),
        "rw_a_up": nrm((L, RW_LORA_A, RW_W), RW_LORA_A ** -0.5),
        "rw_g_up": nrm((L, RW_LORA_G, RW_W), RW_LORA_G ** -0.5),
        "rw_k_k": 0.85 + nrm((L, RW_W), 0.02),
        "rw_k_a": 1.0 + nrm((L, RW_W), 0.02),
        "rw_r_k": nrm((L, RW_HEADS, RW_DH), 0.1),
        "rw_gn_g": 1.0 + nrm((L, RW_W), 0.02),
        "rw_gn_b": nrm((L, RW_W), 0.02),
        "w_merge": nrm((L, N_BRANCH, D, D), D ** -0.5),
        "b_merge": nrm((L, N_BRANCH, D), 0.02),
        "w_branch": nrm((L, MIX_W, D), BETA * HG_W ** -0.5),
        "w_out": nrm((L, D, D), BETA * D ** -0.5),
        "ln_g": 1.0 + nrm((L, 2, D), 0.02),
        "ln_b": nrm((L, 2, D), 0.02),
        "w_router": nrm((D, N_EXPERTS), D ** -0.5),
        "router_bias": nrm((N_EXPERTS,), 0.01),
        "w_exp_gate": nrm((L, N_EXPERTS, D, D_EXPERT), D ** -0.5),
        "w_exp_up": nrm((L, N_EXPERTS, D, D_EXPERT), D ** -0.5),
        "w_exp_down": nrm((L, N_EXPERTS, D_EXPERT, D), BETA * D_EXPERT ** -0.5),
    }

def reference(x, c, w_ada, b_ada, w_in, hg_lb_logits, hg_norm_g, da_lambda, da_subln_g,
              rw_mu, rw_w0, rw_w_up, rw_a0, rw_a_up, rw_g_up, rw_k_k, rw_k_a, rw_r_k, rw_gn_g, rw_gn_b,
              w_merge, b_merge, w_branch, w_out, ln_g, ln_b, w_router, router_bias,
              w_exp_gate, w_exp_up, w_exp_down):
    sm = jax.nn.softmax(hg_lb_logits.astype(jnp.float32), axis=0)
    hg_lb = jnp.cumsum(sm, axis=0) - sm[0:1]
    cond = jax.nn.silu(c)
    for l in range(DEPTH):
        mod = (cond @ w_ada[l] + b_ada[l])[:, None, :]
        sh1, sc1, g1, sh2, sc2, g2 = jnp.split(mod, 6, axis=-1)
        lq1, lk1, lq2, lk2 = da_lambda[l].astype(jnp.float32)
        lam_init = 0.8 - 0.6 * math.exp(-0.3 * l)
        lam = jnp.exp(jnp.sum(lq1 * lk1)) - jnp.exp(jnp.sum(lq2 * lk2)) + lam_init
        u = x * (1.0 + sc1) + sh1
        mix = hybrid_mixer(u, w_in[l], hg_lb[l], hg_norm_g[l], lam, lam_init, da_subln_g[l],
                           rw_mu[l], rw_w0[l], rw_w_up[l], rw_a0[l], rw_a_up[l], rw_g_up[l],
                           rw_k_k[l], rw_k_a[l], rw_r_k[l], rw_gn_g[l], rw_gn_b[l],
                           w_merge[l], b_merge[l], w_branch[l], w_out[l])
        x = layer_norm(ALPHA * x + (1.0 + g1) * mix, ln_g[l, 0], ln_b[l, 0])
        u = x * (1.0 + sc2) + sh2
        ffn = grouped_moe(u, w_router, router_bias, w_exp_gate[l], w_exp_up[l], w_exp_down[l])
        x = layer_norm(ALPHA * x + (1.0 + g2) * ffn, ln_g[l, 1], ln_b[l, 1])
    return x


_drawn_inputs = setup_inputs


def setup_inputs(seed=0):
    import zlib

    import numpy as np

    out = dict(_drawn_inputs(seed))
    spreads = {}
    factors = {'hg_norm_g': 3.818,
     'da_lambda': 2.688,
     'da_subln_g': 3.991,
     'rw_k_k': 8.0,
     'rw_k_a': 3.735,
     'rw_gn_g': 8.0,
     'rw_gn_b': 8.0,
     'b_merge': 4.056}
    for name, (base, spread) in spreads.items():
        noise = np.random.default_rng([zlib.crc32(name.encode()), seed]).standard_normal(out[name].shape)
        drawn = base * np.exp(spread * noise) if base else spread * noise
        out[name] = __import__('jax').numpy.asarray(drawn.astype(out[name].dtype))
    for name, factor in factors.items():
        out[name] = (out[name] * factor).astype(out[name].dtype)
    return out
```

```python
import concourse.bass as bass
from concourse import mybir
from contextlib import ExitStack
import math

F32 = mybir.dt.float32
I32 = mybir.dt.int32
ALU = mybir.AluOpType
ACT = mybir.ActivationFunctionType
AX = mybir.AxisListType

P = 128
T = 256
D = 1024
KT = D // P
NB = T // P
C = 64
NCH = T // C
H4 = 4
E = 16
FE = 512
CAP = 64
PASSES = T // CAP
PAIRS = E // 2
ALPHA = 2.0 ** 0.25
LN_EPS, RMS_EPS, GN_EPS = 1e-5, 1e-6, 64e-5
LAM_INIT = 0.8 - 0.6 * math.exp(-0.3 * 0)
DECAY = math.exp(-0.5)
UNIT = 4096
FRONT_SLOTS, MOE_SLOTS = 3, 6

LEVELS = (1, 2, 4, 8, 16, 32, 64)
MATS = ["ident", "ones_d", "ones_dv", "pair", "pair_mean", "ones"] + [f"lev{b}" for b in LEVELS] + [
    "quad", "strict", "incl", "before"]
MAT_COLS = P * len(MATS)
DIST0 = MAT_COLS
IOTA0 = DIST0 + 3 * P
TIE0 = IOTA0 + CAP
CONST_COLS = TIE0 + 16

VECS = [("c", 8), ("b_ada", 48), ("hg_lb", 4), ("hg_norm", 1), ("da_subln", 1), ("mu", 14), ("w0", 4),
        ("a0", 4), ("k_k", 4), ("k_a", 4), ("r_k", 4), ("gn_g", 4), ("gn_b", 4), ("b_merge", 24),
        ("ln_g", 16), ("ln_b", 16)]
VEC_AT, _n = {}, 0
for _name, _w in VECS:
    VEC_AT[_name] = (_n, _w)
    _n += _w
VEC_COLS = _n


class Groups:

    def __init__(self, nc, ctx, what, banks, names):
        self.banks, self.names = banks, {n: i for i, n in enumerate(names)}
        assert len(self.names) == len(names)
        self.full = [ctx.enter_context(nc.semaphore(f"{what}_full{i}")) for i in range(len(banks))]
        self.free = [ctx.enter_context(nc.semaphore(f"{what}_read{i}")) for i in range(len(banks))]

    def at(self, name):
        i = self.names[name]
        b, k = i % len(self.banks), i // len(self.banks)
        return self.banks[b], self.full[b], self.free[b], k

    def claim(self, pe, name):
        t, full, free, k = self.at(name)
        if k:
            pe.wait_ge(free, k)
        return t, full

    def wait_full(self, eng, name):
        t, full, free, k = self.at(name)
        eng.wait_ge(full, k + 1)
        return t, free, k + 1

    def wait_read(self, eng, name):
        t, full, free, k = self.at(name)
        eng.wait_ge(free, k + 1)


def build(nc, xt, w_ada, w_in, w_merge, w_branch, w_out, w_router, w_gate, w_up, w_down,
          vecs, consts, lam_row, rbias_row, rw_w_up, rw_a_up, rw_g_up, out):
    ctx = ExitStack()
    with ctx:
        def sem(name):
            return ctx.enter_context(nc.semaphore(name))

        total = 53200
        A = ctx.enter_context(nc.sbuf_tensor("arena", [P, total], F32))
        flag_i = ctx.enter_context(nc.sbuf_tensor("overflow_flag", [1, 1], I32))
        bank = [ctx.enter_context(nc.psum_tensor(f"bank{i}", [P, 512], F32)) for i in range(8)]
        place = [0]

        def take(width):
            at = place[0]
            place[0] += width
            assert place[0] <= total, place[0]
            return A[:, at:at + width]

        def tiles(ap, n):
            return ap.rearrange("p (n t) -> p n t", n=n)

        ring = [take(UNIT) for _ in range(MOE_SLOTS)]
        place[0] = FRONT_SLOTS * UNIT
        a_rw, g_rw, bonus, at_f, kt_f, rt_f = [take(1024) for _ in range(6)]
        late = place[0]
        sig_w, cs0, cs1, g_inv, kk, kk_sq = [take(1024) for _ in range(6)]
        assert place[0] == MOE_SLOTS * UNIT
        cst = take(CONST_COLS)
        vec = take(VEC_COLS)
        xT, uT = take(2048), take(2048)
        o_hg, o_da = take(1024), take(1024)
        rwx_a = take(14 * (T + 1))
        work0 = place[0]
        hk, hb0, hb1, hv, hog, dk_, dv_ = [take(1024) for _ in range(7)]
        o_rw = take(1024)
        gates = [take(2048) for _ in range(3)]
        small = take(700)
        modc = small[:, 0:48]
        sc1p, g1p, sc2p, g2p = [small[:, 48 + 8 * i:56 + 8 * i] for i in range(4)]
        condc = small[:, 80:88]
        lbv, oml = small[:, 88:92], small[:, 92:96]
        lam4 = small[:, 96:104]
        smx = small[:, 104:168]
        gend = small[:, 168:184]
        wr = small[:, 192:320]
        route = small[:, 320:700]
        condb, modrow = take(256), take(512)
        lora_wa = gates[2][:, 0:512]
        lora_g = gates[2][:, 512:1024]
        lam_sb = gates[1][:, 0:256]
        lam_t = gates[1][:, 256:384]
        rwx = rwx_a.rearrange("p (n t) -> p n t", n=14)

        def M(name):
            i = MATS.index(name)
            return cst[:, i * P:(i + 1) * P]

        def V(name, i=0, n=1):
            return vec[:, VEC_AT[name][0] + i:VEC_AT[name][0] + i + n]

        def over(m, n):
            return m.unsqueeze(1).to_broadcast([P, n, m.shape[-1]])

        proj_names = (["ada0", "adaT0"] + [f"rw{i}" for i in (6, 2, 3, 0, 1)] + ["hgf0", "hgf1", "hgq0", "hgq1", "rw4", "rw5"]
                      + ["hgv0", "hgv1", "hog0", "hog1", "daq0", "daq1", "dak0", "dak1", "dav0", "dav1"]
                      + [f"gate{b}_{i}" for b in range(3) for i in range(4)]
                      + [f"br{b}_{i}" for b in range(3) for i in range(4)]
                      + [f"out{i}" for i in range(4)] + ["ln1m", "ln1v", "logit", "logitT", "rank"]
                      + [f"u2t{i}" for i in range(4)])
        PJ = Groups(nc, ctx, "proj", bank[0:2], proj_names)
        lev_names = [f"a{b}_{i}" for b in (64, 32, 16, 8, 4, 0) for i in range(2)]
        lev_names.insert(2, "a128")
        HD = Groups(nc, ctx, "mix", bank[6:8], lev_names + ["hgo0", "hgo1", "hgs0", "hgs1"]
                    + [f"s{h}_{m}" for h in range(4) for m in range(2)] + [f"pT{i}" for i in range(3)]
                    + ["dao0", "dao1", "das0", "das1", "ada1", "adaT1", "ada2", "adaT2"])
        rw_names = [f"lw{i}" for i in range(2)] + [f"la{i}" for i in range(2)] + [f"lg{i}" for i in range(2)]
        rw_names += ["kk0", "kk1", "bo0", "bo1"]
        for hf in range(2):
            rw_names += [f"{hf}tok{i}" for i in range(4)]
            rw_names += [f"{hf}m{m}_{hp}" for m in range(4) for hp in range(2)]
            rw_names += [f"{hf}x1_{hp}" for hp in range(2)]
            for b in LEVELS[1:6]:
                rw_names += [f"{hf}y{b}_{hp}" for hp in range(2)]
                rw_names += [f"{hf}xt{b}_{hp}" for hp in range(2)]
                if b < 32:
                    rw_names += [f"{hf}xx{b}_{hp}" for hp in range(2)]
            rw_names += [f"{hf}y0_{hp}" for hp in range(2)] + [f"{hf}up_{hp}" for hp in range(2)] + [f"{hf}wat"]
            for c in range(NCH):
                if c:
                    rw_names.append(f"{hf}u{c}")
                if c < NCH - 1:
                    rw_names.append(f"{hf}s{c}")
            rw_names += [f"{hf}o", f"{hf}gm", f"{hf}gv"]
        RW = Groups(nc, ctx, "rwkv", bank[2:6], rw_names)

        units = []
        for r in range(1):
            units += [("ada", r, q, f"ada{r}") for q in range(4)]
        in_units = [(5120, 256, "rw6"), (4096, 512, "rw3"), (3584, 512, "rw1"), (512, 512, "hgf1"), (0, 512, "hgq1"),
                    (4608, 512, "rw5"), (1024, 512, "hgv1"), (1536, 512, "hog1"), (2048, 512, "daq1"),
                    (2560, 512, "dak1"), (3072, 512, "dav1")]
        units += [("in", c0, w, last) for c0, w, last in in_units]
        for what in "g00 g01 g10 a10 a11 g11 a12 a13 g20 a20 a21 g21 a22 a23".split():
            x, y = int(what[1]), int(what[2])
            units.append(("ada", x, y, f"ada{x}") if what[0] == "a" else ("gate", x, y, f"gate{x}_{2 * y + 1}"))
        units += [("br", b, 0, f"br{b}_3") for b in range(3)]
        units += [("out", 0, i, f"out{2 * i + 1}") for i in range(2)]
        UIDX = {}
        for i, u in enumerate(units):
            UIDX[u[:3]] = i
        front_uses = [sum(1 for i in range(len(units)) if i % FRONT_SLOTS == s) for s in range(FRONT_SLOTS)]
        front_uses += [0] * (MOE_SLOTS - FRONT_SLOTS)
        slot_in = [sem(f"weights_in_slot{i}") for i in range(MOE_SLOTS)]
        ada_used = sem("ada_unit_used")

        def unit(eng, *key):
            i = UIDX[key]
            eng.wait_ge(slot_in[i % FRONT_SLOTS], 16 * (i // FRONT_SLOTS + 1))
            return ring[i % FRONT_SLOTS]

        const_in, vec_in, x_in, lora_in, row_in = sem("consts_in"), sem("vectors_in"), sem("x_in"), sem("lora_in"), sem("rows_in")
        out_done = sem("out_written")
        cond_sig, lb_exp, lb_in, ln2_sum = sem("cond_sigmoid"), sem("lower_bound_exp"), sem("lower_bound_in"), sem("ln2_sum")
        cond_ready, u_ready = sem("cond_ready"), sem("u_ready")
        modrow_ready, mod_ready = sem("modrow_ready"), sem("mod_ready")
        pad_ready, xs_ready = sem("pad_ready"), sem("shifted_ready")
        lora_act = sem("lora_act_ready")
        lora_done = sem("lora_gates_ready")
        kk_ready, kk_sqd, kk_n = sem("kk_ready"), sem("kk_squared"), sem("kk_norm_ready")
        cs_ready, dec_ready = sem("cumsum_ready"), sem("decays_ready")
        rk_ready, rwf_ready = sem("rk_ready"), sem("rwkv_factors_ready")
        sg_ready = sem("hg_sigmoids_ready")
        f_ready, logf_ready, kq_ready = sem("hg_forget_ready"), sem("hg_logf_ready"), sem("hg_k_ready")
        hcs_ready, dec_in, dec_out = sem("hg_cumsum_ready"), sem("hg_exponent_ready"), sem("hg_decay_ready")
        lev_ready = sem("hg_level_ready")
        at_ready = sem("hg_scores_ready")
        osq_ready, rms_ready = sem("out_squared"), sem("rstd_ready")
        o_ready = sem("branch_out_ready")
        s_ready, nmax_ready, e_ready, p_ready = sem("scores_ready"), sem("negmax_ready"), sem("exp_ready"), sem("probs_ready")
        lam_ready, lam_exp = sem("lambda_sums_ready"), sem("lambda_exp_ready")
        m_ready, xt_ready, nl_ready = sem("rw_matrices_ready"), sem("rw_inverse_started"), sem("rw_level_mask_ready")
        pool_ch, dq_ready, head_ready = sem("pool_chain"), sem("attention_q_ready"), sem("head_factors_ready")
        st_ready = sem("rw_state_ready")
        go_sq, go_ln, go_d = sem("gn_squared"), sem("gn_rstd"), sem("gn_centred")
        orw_copied = sem("rw_out_copied")
        merged_ready = sem("merged_ready")
        y1_ready, lnd, lnsq, lnr = sem("ln_in_ready"), sem("ln_centred"), sem("ln_squared"), sem("ln_rstd")
        u2_ready = sem("u2_ready")
        lg_exp_in, lg_exp = sem("router_shifted"), sem("router_exp")
        chosen_ready = sem("chosen_ready")
        flag_ready = sem("flag_ready")
        dve_ch, act_ch = sem("dve_chain"), sem("act_chain")
        x2_ready = sem("result_ready")

        pick_ready = sem("picks_ready")
        pw_full, pw_copied = sem("pick_transposes_done"), sem("pick_transposes_copied")
        xg_full, xg_ready = sem("gather_done"), sem("gathered_ready")
        gate_full, up_full = sem("gate_done"), sem("up_done")
        sig_ready, h_ready = sem("silu_ready"), sem("hidden_ready")
        hT_full, hT_ready = sem("hidden_transposed"), sem("hidden_t_ready")
        y_full, y_ready = sem("down_done"), sem("y_ready")
        comb_full, comb_added = sem("combine_done"), sem("combine_added")
        moe_ch = sem("moe_dve_chain")
        blk_ch = sem("moe_pass_chain")

        XG = rwx_a[:, 0:1024]
        HM = rwx_a[:, 1024:1536]
        HH = rwx_a[:, 1536:2048]
        HT_ = rwx_a[:, 2048:2560]
        SG = rwx_a[:, 2560:3072]
        place[0] = work0
        U2K = take(2048)
        PK = take(2048)
        PWT = take(2048)
        Y = take(1024)
        PW = gates[2]
        ACC = gates[0]
        LNT = gates[1]

        lvE, lvK, lvQ = [A[:, late + i * 1024:late + (i + 1) * 1024] for i in range(3)]
        scoresT = A[:, late + 3072:late + 4608]
        lvX = gates[0][:, 0:1024]
        dq_map = [gates[1][:, 1024:2048], gates[2][:, 1024:2048]]
        hog_s = gates[1][:, 0:1024]
        att = A[:, late:late + 3072]
        probsT = A[:, late + 3072:late + 4608]
        daSq = A[:, late + 4608:late + 5632]
        daR = hb1
        RB = route[:, 0:E]
        rt2 = route[:, 16:20]
        scores, chosen = route[:, 20:52], route[:, 52:84]
        slot = route[:, 196:228]
        lgT = LNT[:, 256:512]

        def rw_mats(hf):
            lt = [A[:, late + i * 1024:late + (i + 1) * 1024] for i in range(6)]
            wk = [A[:, work0 + i * 1024:work0 + (i + 1) * 1024] for i in range(7)]
            NT, X, XT, YY = lt[0:4]
            NL = lt[4:6]
            AKT, RBT, RKT = wk[0:3]
            tok = [A[:, work0 + 3072 + i * 512:work0 + 3584 + i * 512] for i in range(4)]
            UP, WAT = [A[:, work0 + 5120 + i * 512:work0 + 5632 + i * 512] for i in range(2)]
            ST = rwx_a[:, 0:1024]
            Y0 = rwx_a[:, 1536:2048]
            return NT, X, XT, YY, NL, AKT, RBT, RKT, tok, Y0, UP, WAT, ST

        def kk_gn(hf):
            return rwx_a[:, 1024:1536]

        block = ctx.enter_context(nc.Block())

        @block.sync
        def _(sp):
            sp.dma_start(vec, vecs).then_inc(vec_in, 16)
            n_ada = [0]

            def load(i):
                u = units[i]
                s = i % FRONT_SLOTS
                if i >= FRONT_SLOTS:
                    prev = units[i - FRONT_SLOTS]
                    if prev[0] == "ada":
                        sp.wait_ge(ada_used, 4 * prev[1] + prev[2] + 1)
                    else:
                        t, full, free, k = PJ.at(prev[3])
                        sp.wait_ge(full, k + 1)
                if u[0] == "ada":
                    src = w_ada[:, u[2] * 2:u[2] * 2 + 2, u[1] * 2048:(u[1] + 1) * 2048]
                    dst = ring[s].rearrange("p (k c) -> p k c", k=2)
                elif u[0] == "in":
                    src = w_in[:, :, u[1]:u[1] + u[2]]
                    dst = ring[s][:, 0:KT * u[2]].rearrange("p (k c) -> p k c", k=KT)
                elif u[0] == "gate":
                    src = w_merge[:, u[1], :, u[2] * 512:(u[2] + 1) * 512]
                    dst = ring[s].rearrange("p (k c) -> p k c", k=KT)
                elif u[0] == "br":
                    src = w_branch[:, u[1] * 4:u[1] * 4 + 4, :]
                    dst = ring[s].rearrange("p (k c) -> p k c", k=4)
                else:
                    src = w_out[:, :, u[2] * 512:(u[2] + 1) * 512]
                    dst = ring[s].rearrange("p (k c) -> p k c", k=KT)
                sp.dma_start(dst, src).then_inc(slot_in[s], 16)

            load(0)
            sp.dma_start(cst, consts).then_inc(const_in, 16)
            sp.dma_start(tiles(xT, KT), xt).then_inc(x_in, 16)
            load(1)
            load(2)
            sp.dma_start(lora_wa[0:64, :], rw_w_up).then_inc(lora_in, 16)
            sp.dma_start(lora_wa[64:128, :], rw_a_up).then_inc(lora_in, 16)
            sp.dma_start(lora_g, rw_g_up).then_inc(lora_in, 16)
            sp.dma_start(lam_sb, lam_row.to_broadcast([P, 256])).then_inc(row_in, 16)
            sp.dma_start(wr.rearrange("p (k e) -> p k e", k=KT), w_router).then_inc(row_in, 16)
            sp.dma_start(route[:, 0:E], rbias_row.to_broadcast([P, E])).then_inc(row_in, 16)
            for i in range(3, len(units)):
                load(i)

            def expert_load(s, e2):
                w, kt = ((w_gate, KT), (w_up, KT), (w_down, FE // P))[s // 2]
                src = w[bass.ds(e2 + s % 2, 1), :, :, :].rearrange("e p k c -> p (e k) c")
                sp.dma_start(ring[s].rearrange("p (k c) -> p k c", k=kt), src).then_inc(slot_in[s], 16)

            def next_pair(e2, n):
                for s in range(MOE_SLOTS):
                    if s < 4:
                        sp.wait_ge((gate_full, up_full)[s // 2], n)
                    else:
                        sp.wait_ge(y_full, 2 * n)
                    expert_load(s, e2)

            sp.wait_ge(merged_ready, 4)
            for s in range(FRONT_SLOTS, MOE_SLOTS):
                expert_load(s, 0)
            nu = len(units)
            for i in range(nu - FRONT_SLOTS, nu):
                t, full, free, k = PJ.at(units[i][3])
                sp.wait_ge(full, k + 1)
                expert_load(i % FRONT_SLOTS, 0)
            with sp.Fori(1, PAIRS) as p:
                next_pair(2 * p, p)
            sp.wait_ge(flag_ready, 1)
            over_ = sp.value_load(flag_i[0:1, 0:1], min_val=0, max_val=1)
            with sp.If(over_ > 0):
                with sp.Fori(1, PASSES) as b:
                    with sp.Fori(0, PAIRS) as p:
                        next_pair(2 * p, b * PAIRS + p)
            for i in range(4):
                sp.wait_ge(x2_ready, i + 1)
                sp.dma_start(out[:, 2 * i:2 * i + 2, :], tiles(uT, KT)[:, 2 * i:2 * i + 2, :]).then_inc(out_done, 16)
            sp.wait_ge(out_done, 64)

        @block.gpsimd
        def _(pool):
            n = [0]

            def link(ins):
                n[0] += 1
                ins.then_inc(pool_ch, 1)
                pool.wait_ge(pool_ch, n[0])

            nc.gpsimd.memset(rwx[:, :, 0:1], 0.0).then_inc(pad_ready, 1)
            pool.wait_ge(const_in, 16)

            def one_head(dst, src, head, *more):
                return nc.gpsimd.tensor_scalar(dst, src, M("pair")[:, head * 64:head * 64 + 1], *more)

            PJ.wait_read(pool, "daq0")
            PJ.wait_read(pool, "daq1")
            for m in range(2):
                one_head(dq_map[m], o_da, m, 0.125, ALU.mult, ALU.mult).then_inc(dq_ready, 1)
            pool.wait_ge(o_ready, 2)
            for hf in range(2):
                NT, X, _, YY, NL = rw_mats(hf)[0:5]
                if hf:
                    RW.wait_full(pool, "0xt32_1")
                    RW.wait_full(pool, "0xt32_0")
                for src, dst in ((a_rw, X), (kt_f, YY)):
                    for hp in range(2):
                        one_head(dst[:, hp * 512:(hp + 1) * 512], src[:, hf * 512:(hf + 1) * 512], hp, None,
                                 ALU.mult).then_inc(head_ready, 1)
                pool.wait_ge(m_ready, 8 * hf + 2)
                for i, b in enumerate(LEVELS[1:6]):
                    if i >= 2:
                        RW.wait_full(pool, f"{hf}y{LEVELS[i - 1]}_1")
                    nc.gpsimd.tensor_tensor(tiles(NL[i % 2], 8), tiles(NT, 8), over(M(f"lev{b}"), 8),
                                            ALU.mult).then_inc(nl_ready, 1)
                    pool.wait_ge(nl_ready, 5 * hf + i + 1)

        @block.tensor
        def _(pe):
            mm = nc.tensor.matmul

            def mod_rows(r, q):
                G = HD if r else PJ
                if q == 0:
                    G.claim(pe, f"ada{r}")
                t, full, free, n = G.at(f"ada{r}")
                w = unit(pe, "ada", r, q).rearrange("p (k c) -> p k c", k=2)
                for k in range(2):
                    for g in range(4):
                        last = mm(t[32 * g:32 * g + 32, :], condb[:, (2 * q + k) * 32:(2 * q + k) * 32 + 32],
                                  w[:, k, g * 512:(g + 1) * 512], start=(q + k == 0), stop=(q == 3 and k == 1))
                if q == 3:
                    last.then_inc(full, 1)
                    G.wait_full(pe, f"ada{r}")
                    pe.nop().then_inc(ada_used, 1)
                else:
                    last.then_inc(ada_used, 1)

            def mod_cols(r):
                pe.wait_ge(modrow_ready, r + 1)
                t, full = (HD if r else PJ).claim(pe, f"adaT{r}")
                for i in range(4):
                    last = nc.tensor.transpose(t[:, i * P:(i + 1) * P], modrow[:, i * P:(i + 1) * P], M("ident"))
                last.then_inc(full, 1)

            uv = tiles(uT, KT)

            def project(name, w, m0, rhs=uv, kt=KT):
                t, full = PJ.claim(pe, name)
                for i in range(2):
                    for k in range(kt):
                        last = mm(t[:, i * T:(i + 1) * T], w[:, k, (m0 + i) * P:(m0 + i + 1) * P], rhs[:, k, :],
                                  start=(k == 0), stop=(k == kt - 1))
                last.then_inc(full, 1)

            def project_tokens(name, w, b):
                t, full = PJ.claim(pe, name)
                for k in range(KT):
                    last = mm(t[:, :], uv[:, k, b * P:(b + 1) * P], w[:, k, :], start=(k == 0), stop=(k == KT - 1))
                last.then_inc(full, 1)

            def gate_group(b, i):
                w = unit(pe, "gate", b, i // 2).rearrange("p (k c) -> p k c", k=KT)
                project(f"gate{b}_{i}", w, 2 * (i % 2))

            pe.wait_ge(cond_ready, 1)
            for q in range(4):
                mod_rows(0, q)
            pe.wait_ge(const_in, 16)
            mod_cols(0)
            pe.wait_ge(u_ready, 1)

            def in_group(name, c0, i, w_=512):
                w = unit(pe, "in", c0, w_)[:, 0:KT * w_].rearrange("p (k c) -> p k c", k=KT)
                project(name, w, 2 * i)

            def in_tokens(name, c0, i):
                project_tokens(name, unit(pe, "in", c0, 512).rearrange("p (k c) -> p k c", k=KT), i)

            in_group("rw6", 5120, 0, 256)
            in_group("rw2", 4096, 0)
            in_group("rw3", 4096, 1)

            pe.wait_ge(lora_in, 48)
            pe.wait_ge(lora_act, 2)
            for what, lhs, rhs in (("lw", lora_wa[0:64, :], rwx[0:64, 12, 1:]), ("la", lora_wa[64:128, :], rwx[64:128, 12, 1:]),
                                   ("lg", lora_g, rwx[:, 13, 1:])):
                for i in range(2):
                    t, full = RW.claim(pe, f"{what}{i}")
                    for j in range(2):
                        m = 2 * i + j
                        last = mm(t[:, j * T:(j + 1) * T], lhs[:, m * P:(m + 1) * P], rhs, start=True, stop=True)
                    last.then_inc(full, 1)
            in_group("rw0", 3584, 0)
            in_group("rw1", 3584, 1)

            def head_sums(what):
                for i in range(2):
                    t, full = RW.claim(pe, f"{what}{i}")
                    mm(t[:, :], M("pair"), kk_sq[:, i * 512:(i + 1) * 512], start=True, stop=True).then_inc(full, 1)

            pe.wait_ge(kk_sqd, 1)
            head_sums("kk")
            in_group("hgf0", 512, 0)
            in_group("hgf1", 512, 1)
            in_group("hgq0", 0, 0)
            in_group("hgq1", 0, 1)
            in_group("rw4", 4608, 0)
            in_group("rw5", 4608, 1)
            pe.wait_ge(rk_ready, 1)
            head_sums("bo")

            q3, k3 = tiles(lvQ, 4), tiles(lvK, 4)

            def level(name, n, sk, sq, kk_=None, qq_=None):
                pe.wait_ge(lev_ready, n)
                t, full = HD.claim(pe, name)
                for h in range(H4):
                    last = mm(t[:, h * P:(h + 1) * P], (kk_ or k3)[:, h, sk:sk + P], (qq_ or q3)[:, h, sq:sq + P],
                              start=True, stop=True)
                last.then_inc(full, 1)

            in_tokens("hgv0", 1024, 0)
            in_tokens("hgv1", 1024, 1)
            in_group("hog0", 1536, 0)
            level("a64_0", 1, 0, 0)
            level("a64_1", 1, P, P)
            level("a128", 2, 0, 0, tiles(lvX, 8)[:, 0:4, :], tiles(lvX, 8)[:, 4:8, :])
            in_group("hog1", 1536, 1)
            for i, b in enumerate((32, 16, 8, 4, 0)):
                for s in range(2):
                    level(f"a{b}_{s}", 3 + i, s * P, s * P)
                if i < 4:
                    what, c0 = (("daq", 2048), ("dak", 2560))[i // 2]
                    in_group(f"{what}{i % 2}", c0, i % 2)
            in_tokens("dav0", 3072, 0)
            pe.wait_ge(at_ready, 1)
            hv3, A4 = tiles(hv, 2), scoresT.rearrange("p (a h t) -> p a h t", a=3, h=H4)
            for s in range(2):
                t, full = HD.claim(pe, f"hgo{s}")
                for h in range(H4):
                    o = t[:, h * P:(h + 1) * P]
                    if s == 0:
                        last = mm(o, hv3[:, 0, h * P:(h + 1) * P], A4[:, 0, h, :], start=True, stop=True)
                    else:
                        mm(o, hv3[:, 0, h * P:(h + 1) * P], A4[:, 2, h, :], start=True, stop=False)
                        last = mm(o, hv3[:, 1, h * P:(h + 1) * P], A4[:, 1, h, :], start=False, stop=True)
                last.then_inc(full, 1)
            in_tokens("dav1", 3072, 1)
            for s in range(2):
                pe.wait_ge(osq_ready, s + 1)
                t, full = HD.claim(pe, f"hgs{s}")
                mm(t[:, :], M("ones_dv"), lvE[:, s * 512:(s + 1) * 512], start=True, stop=True).then_inc(full, 1)

            dk3, dv3 = tiles(dk_, 4), tiles(dv_, 2)
            PJ.wait_read(pe, "dak1")
            pe.wait_ge(dq_ready, 2)
            for h in range(H4):
                for m in range(2):
                    dq = tiles(dq_map[m], 4)
                    t, full = HD.claim(pe, f"s{h}_{m}")
                    mm(t[:, 0:P], dq[:, h, 0:P], dk3[:, h, 0:P], start=True, stop=True)
                    mm(t[:, P:3 * P], dq[:, h, P:T], dk3[:, h, :], start=True, stop=True).then_inc(full, 1)
            gate_group(0, 0)
            gate_group(0, 1)
            pe.wait_ge(p_ready, 1)
            S8 = tiles(att, 8)
            for i in range(3):
                t, full = HD.claim(pe, f"pT{i}")
                for h in range(H4):
                    last = nc.tensor.transpose(t[:, h * P:(h + 1) * P], S8[:, 2 * h, i * P:(i + 1) * P], M("ident"))
                last.then_inc(full, 1)
            gate_group(0, 2)
            PJ.wait_read(pe, "dav1")
            HD.wait_read(pe, "pT2")
            HD.wait_read(pe, "pT1")
            pT3 = probsT.rearrange("p (a h t) -> p a h t", a=3, h=H4)
            for s in range(2):
                t, full = HD.claim(pe, f"dao{s}")
                for h in range(H4):
                    o = t[:, h * P:(h + 1) * P]
                    if s == 0:
                        last = mm(o, dv3[:, 0, h * P:(h + 1) * P], pT3[:, 0, h, :], start=True, stop=True)
                    else:
                        mm(o, dv3[:, 0, h * P:(h + 1) * P], pT3[:, 1, h, :], start=True, stop=False)
                        last = mm(o, dv3[:, 1, h * P:(h + 1) * P], pT3[:, 2, h, :], start=False, stop=True)
                last.then_inc(full, 1)
            gate_group(0, 3)
            for s in range(2):
                pe.wait_ge(osq_ready, 2 + s + 1)
                t, full = HD.claim(pe, f"das{s}")
                mm(t[:, :], M("ones_dv"), daSq[:, s * 512:(s + 1) * 512], start=True, stop=True).then_inc(full, 1)

            af, bf, kf, rf = [tiles(x, 4) for x in (at_f, a_rw, kt_f, rt_f)]
            vf = rwx[:, 8:12, 1:]
            pe.wait_ge(rwf_ready, 1)
            for hf in range(2):
                NT, X, XT, YY, NL, AKT, RBT, RKT, tok, Y0, UP, WAT, ST = rw_mats(hf)
                j0 = 2 * hf

                def q_of(hp, jj, s):
                    return slice(((hp * 2 + jj) * 2 + s) * P, ((hp * 2 + jj) * 2 + s + 1) * P)

                for n, src in enumerate((af, bf, kf, vf)):
                    t, full = RW.claim(pe, f"{hf}tok{n}")
                    for s in range(2):
                        for jj in range(2):
                            o = (s * 2 + jj) * P
                            last = nc.tensor.transpose(t[:, o:o + P], src[:, j0 + jj, s * P:(s + 1) * P], M("ident"))
                    last.then_inc(full, 1)
                pe.wait_ge(head_ready, 4 * hf + 4)
                for n, (lh, rh) in enumerate(((X, af), (YY, af), (X, rf), (YY, rf))):
                    for hp in range(2):
                        lh3 = tiles(lh, 4)[:, 2 * hp:2 * hp + 2, :]
                        t, full = RW.claim(pe, f"{hf}m{n}_{hp}")
                        for jj in range(2):
                            for s in range(2):
                                o = (jj * 2 + s) * P
                                last = mm(t[:, o:o + P], lh3[:, jj, s * P:(s + 1) * P], rh[:, j0 + jj, s * P:(s + 1) * P],
                                          start=True, stop=True)
                        last.then_inc(full, 1)
                gate_group(1 + hf, 0)
                pe.wait_ge(xt_ready, hf + 1)
                for hp in range(2):
                    t, full = RW.claim(pe, f"{hf}x1_{hp}")
                    for i in range(4):
                        q = (hp * 4 + i) * P
                        last = nc.tensor.transpose(t[:, i * P:(i + 1) * P], XT[:, q:q + P], M("ident"))
                    last.then_inc(full, 1)
                for i, b in enumerate(LEVELS[1:6]):
                    pe.wait_ge(nl_ready, 5 * hf + i + 1)
                    for hp in range(2):
                        if i:
                            RW.wait_read(pe, f"{hf}xx{LEVELS[i]}_{hp}")
                        else:
                            RW.wait_read(pe, f"{hf}x1_{hp}")
                        t, full = RW.claim(pe, f"{hf}y{b}_{hp}")
                        for n in range(4):
                            q = (hp * 4 + n) * P
                            last = mm(t[:, n * P:(n + 1) * P], NL[i % 2][:, q:q + P], X[:, q:q + P], start=True, stop=True)
                        last.then_inc(full, 1)
                    if i % 2:
                        gate_group(1 + hf, 1 + i // 2)
                    else:
                        mod_rows(1 + hf, i // 2)
                    for hp in range(2):
                        RW.wait_read(pe, f"{hf}y{b}_{hp}")
                        if i:
                            RW.wait_read(pe, f"{hf}xt{LEVELS[i]}_{hp}")
                        t, full = RW.claim(pe, f"{hf}xt{b}_{hp}")
                        for n in range(4):
                            q = (hp * 4 + n) * P
                            last = mm(t[:, n * P:(n + 1) * P], YY[:, q:q + P], XT[:, q:q + P], start=True, stop=True)
                        last.then_inc(full, 1)
                    if b < 32:
                        for hp in range(2):
                            RW.wait_read(pe, f"{hf}xt{b}_{hp}")
                            t, full = RW.claim(pe, f"{hf}xx{b}_{hp}")
                            for n in range(4):
                                q = (hp * 4 + n) * P
                                last = nc.tensor.transpose(t[:, n * P:(n + 1) * P], XT[:, q:q + P], M("ident"))
                            last.then_inc(full, 1)
                mod_rows(1 + hf, 3)
                RW.wait_read(pe, f"{hf}tok3")
                pe.wait_ge(m_ready, 8 * hf + 8)
                for hp in range(2):
                    t, full = RW.claim(pe, f"{hf}y0_{hp}")
                    for jj in range(2):
                        for s in range(2):
                            o = (jj * 2 + s) * P
                            last = mm(t[:, o:o + P], AKT[:, q_of(hp, jj, s)], tok[3][:, (s * 2 + jj) * P:(s * 2 + jj + 1) * P],
                                      start=True, stop=True)
                    last.then_inc(full, 1)
                RW.wait_read(pe, f"{hf}y0_1")
                RW.wait_read(pe, f"{hf}y0_0")
                RW.wait_read(pe, f"{hf}xt32_0")
                RW.wait_read(pe, f"{hf}xt32_1")
                for hp in range(2):
                    t, full = RW.claim(pe, f"{hf}up_{hp}")
                    for jj in range(2):
                        for s in range(2):
                            o = (jj * 2 + s) * P
                            last = mm(t[:, o:o + P], XT[:, q_of(hp, jj, s)], Y0[:, o:o + P], start=True, stop=True)
                    last.then_inc(full, 1)
                t, full = RW.claim(pe, f"{hf}wat")
                for jj in range(2):
                    for s in range(2):
                        for hp in range(2):
                            o = (jj * 2 + s) * P
                            a0 = (s * 2 + jj) * P + hp * 64
                            last = mm(t[hp * 64:hp * 64 + 64, o:o + P], tok[0][:, a0:a0 + 64], XT[:, q_of(hp, jj, s)],
                                      start=True, stop=True)
                last.then_inc(full, 1)
                RW.wait_read(pe, f"{hf}wat")
                RW.wait_read(pe, f"{hf}up_0")
                RW.wait_read(pe, f"{hf}up_1")
                for c in range(NCH):
                    s, r = c // 2, slice((c % 2) * 64, (c % 2) * 64 + 64)
                    if c:
                        pe.wait_ge(st_ready, 3 * hf + c)
                        t, full = RW.claim(pe, f"{hf}u{c}")
                        for jj in range(2):
                            o = (jj * 2 + s) * P + (c % 2) * 64
                            last = mm(t[r, jj * P:(jj + 1) * P], WAT[:, o:o + 64], ST[:, (c * 2 + jj) * P:(c * 2 + jj + 1) * P],
                                      start=True, stop=True)
                        last.then_inc(full, 1)
                        RW.wait_read(pe, f"{hf}u{c}")
                    if c < NCH - 1:
                        t, full = RW.claim(pe, f"{hf}s{c}")
                        for jj in range(2):
                            a0, u0 = (s * 2 + jj) * P, (jj * 2 + s) * P
                            mm(t[:, jj * P:(jj + 1) * P], tok[1][r, a0:a0 + P], UP[r, u0:u0 + P], start=True, stop=False)
                            last = mm(t[:, jj * P:(jj + 1) * P], tok[2][r, a0:a0 + P], tok[3][r, a0:a0 + P],
                                      start=False, stop=True)
                        last.then_inc(full, 1)
                    if c == 1:
                        gate_group(1 + hf, 3)
                    elif c == 2:
                        mod_cols(1 + hf)
                t, full = RW.claim(pe, f"{hf}o")
                for jj in range(2):
                    for s in range(2):
                        o, a0 = (jj * 2 + s) * P, (s * 2 + jj) * P
                        heads = [(hp, slice(hp * 64, hp * 64 + 64), hp * 64) for hp in range(2)]
                        for hp, rr, hh in heads:
                            mm(t[rr, o:o + P], UP[:, o + hh:o + hh + 64], RBT[:, q_of(hp, jj, s)], start=True, stop=False)
                        for hp, rr, hh in heads:
                            mm(t[rr, o:o + P], tok[3][:, a0 + hh:a0 + hh + 64], RKT[:, q_of(hp, jj, s)], start=False, stop=False)
                        for c in (2 * s, 2 * s + 1):
                            for hp, rr, hh in heads:
                                s0 = (c * 2 + jj) * P + hh
                                last = mm(t[rr, o + (c % 2) * 64:o + (c % 2) * 64 + 64], ST[:, s0:s0 + 64],
                                          rf[:, j0 + jj, c * 64:(c + 1) * 64], start=False, stop=(c % 2 == 1))
                last.then_inc(full, 1)
                pe.wait_ge(orw_copied, hf + 1)
                t, full = RW.claim(pe, f"{hf}gm")
                mm(t[:, :], M("pair_mean"), o_rw[:, hf * 512:(hf + 1) * 512], start=True, stop=True).then_inc(full, 1)
                pe.wait_ge(go_sq, hf + 1)
                t, full = RW.claim(pe, f"{hf}gv")
                mm(t[:, :], M("pair_mean"), kk_gn(hf), start=True, stop=True).then_inc(full, 1)

            for b, src in enumerate((o_hg, o_da, o_rw)):
                pe.wait_ge(o_ready, (1, 2, 4)[b])
                w = unit(pe, "br", b, 0).rearrange("p (k c) -> p k c", k=4)
                for i in range(4):
                    project(f"br{b}_{i}", w, 2 * i, rhs=tiles(src, 4), kt=4)
            mg = tiles(gates[0], KT)
            pe.wait_ge(merged_ready, 4)
            for i in range(4):
                w = unit(pe, "out", 0, i // 2).rearrange("p (k c) -> p k c", k=KT)
                project(f"out{i}", w, 2 * (i % 2), rhs=mg)

            def norm_sum(name, src):
                t, full = PJ.claim(pe, name)
                for k in range(KT):
                    last = mm(t[:, 0:T], M("ones_d"), tiles(src, KT)[:, k, :], start=(k == 0), stop=(k == KT - 1))
                last.then_inc(full, 1)

            pe.wait_ge(y1_ready, 1)
            norm_sum("ln1m", xT)
            pe.wait_ge(lnsq, 1)
            norm_sum("ln1v", LNT)
            pe.wait_ge(u2_ready, 1)
            pe.wait_ge(row_in, 48)
            t, full = PJ.claim(pe, "logit")
            for k in range(KT):
                last = mm(t[0:E, 0:T], wr[:, k * E:(k + 1) * E], uv[:, k, :], start=(k == 0), stop=(k == KT - 1))
            last.then_inc(full, 1)
            PJ.wait_read(pe, "logit")
            t, full = PJ.claim(pe, "logitT")
            for s in range(2):
                last = nc.tensor.transpose(t[:, s * E:(s + 1) * E], lgT[0:E, s * P:(s + 1) * P], M("ident")[0:E, 0:E])
            last.then_inc(full, 1)
            pe.wait_ge(chosen_ready, 1)
            t, full = PJ.claim(pe, "rank")
            ch = chosen.rearrange("p (b e) -> p b e", b=2)
            mm(t[:, 0:E], M("before"), ch[:, 0, :], start=True, stop=True)
            mm(t[:, E:2 * E], M("before"), ch[:, 1, :], start=True, stop=False)
            mm(t[:, E:2 * E], M("ones"), ch[:, 0, :], start=False, stop=True)
            mm(t[:, 2 * E:3 * E], M("ones"), ch[:, 0, :], start=True, stop=False)
            mm(t[:, 2 * E:3 * E], M("ones"), ch[:, 1, :], start=False, stop=True).then_inc(full, 1)
            for i in range(4):
                t, full = PJ.claim(pe, f"u2t{i}")
                for j in range(4):
                    m = (i % 2) * 4 + j
                    last = nc.tensor.transpose(t[:, j * P:(j + 1) * P], uv[:, m, (i // 2) * P:(i // 2 + 1) * P], M("ident"))
                last.then_inc(full, 1)

            PWv = PW.rearrange("p (b n s) -> p b n s", b=2, n=PAIRS)

            def picks(b):
                pe.wait_ge(pick_ready, b + 1)
                for f in range(4):
                    for j in range(2):
                        for s in range(2):
                            o = (2 * j + s) * P
                            last = nc.tensor.transpose(bank[2 + f][:, o:o + P], PWv[:, s, 2 * f + j, :], M("ident"))
                    last.then_inc(pw_full, 1)
                pe.wait_ge(pw_copied, 4 * b + 4)

            def gather(p, n):
                if not isinstance(n, int) or n > 0:
                    pe.wait_ge(xg_ready, 2 * n)
                for half in range(2):
                    for j in range(4):
                        m = half * 4 + j
                        for s in range(2):
                            last = mm(bank[half][:, j * P:(j + 1) * P], U2K[:, s * D + m * P:s * D + (m + 1) * P],
                                      PK[:, bass.ds(s * 1024 + p * P, P)], start=(s == 0), stop=(s == 1))
                    last.then_inc(xg_full, 1)

            xg3, hT3 = tiles(XG, KT), tiles(HT_, 4)

            def pair(p, n, more):
                pe.wait_ge(xg_ready, 2 * n + 2)
                pe.wait_ge(comb_added, 4 * n + 1)
                for what, bk, done_ in ((0, 2, gate_full), (1, 3, up_full)):
                    for j in range(2):
                        s = 2 * what + j
                        pe.wait_ge(slot_in[s], 16 * n + 16 * (front_uses[s] + 1))
                    for k in range(KT):
                        for j in range(2):
                            w = ring[2 * what + j].rearrange("p (k c) -> p k c", k=KT)
                            last = mm(bank[bk][j * 64:j * 64 + 64, :], xg3[:, k, j * 64:j * 64 + 64], w[:, k, :],
                                      start=(k == 0), stop=(k == KT - 1))
                    last.then_inc(done_, 1)
                if more:
                    gather(p + 1, n + 1)
                pe.wait_ge(h_ready, n + 1)
                for k in range(4):
                    last = nc.tensor.transpose(bank[4][:, k * P:(k + 1) * P], HH[:, k * P:(k + 1) * P], M("ident"))
                last.then_inc(hT_full, 1)
                pe.wait_ge(hT_ready, n + 1)
                for j in range(2):
                    pe.wait_ge(slot_in[4 + j], 16 * n + 16 * (front_uses[4 + j] + 1))
                for half in range(2):
                    for k in range(4):
                        for j in range(2):
                            w = ring[4 + j].rearrange("p (k c) -> p k c", k=4)
                            last = mm(bank[5 + half][j * 64:j * 64 + 64, :], hT3[:, k, j * 64:j * 64 + 64],
                                      w[:, k, half * 512:(half + 1) * 512], start=(k == 0), stop=(k == 3))
                    last.then_inc(y_full, 1)
                pe.wait_ge(y_ready, 2 * n + 2)
                for i in range(4):
                    if i >= 2:
                        pe.wait_ge(comb_added, 4 * n + i)
                    bk = bank[7] if i % 2 == 0 else bank[2]
                    for j in range(2):
                        m = 2 * i + j
                        last = mm(bk[:, j * T:(j + 1) * T], Y[:, m * P:(m + 1) * P], PWT[:, bass.ds(p * T, T)],
                                  start=True, stop=True)
                    last.then_inc(comb_full, 1)

            def one_pass(b, n0):
                picks(b)
                gather(0, n0)
                with pe.Fori(0, PAIRS - 1) as p:
                    pair(p, n0 + p, True)
                pair(PAIRS - 1, n0 + PAIRS - 1, False)

            one_pass(0, 0)
            pe.wait_ge(flag_ready, 1)
            over_ = pe.value_load(flag_i[0:1, 0:1], min_val=0, max_val=1)
            with pe.If(over_ > 0):
                with pe.Fori(1, PASSES) as b:
                    one_pass(b, b * PAIRS)

            pe.wait_ge(y1_ready, 2)
            for k in range(KT):
                last = mm(bank[0][:, 0:T], M("ones_d"), tiles(xT, KT)[:, k, :], start=(k == 0), stop=(k == KT - 1))
            last.then_inc(ln2_sum, 1)
            pe.wait_ge(lnsq, 2)
            for k in range(KT):
                last = mm(bank[1][:, 0:T], M("ones_d"), tiles(LNT, KT)[:, k, :], start=(k == 0), stop=(k == KT - 1))
            last.then_inc(ln2_sum, 1)

        @block.scalar
        def _(act):
            n = [0]

            def link(ins):
                n[0] += 1
                ins.then_inc(act_ch, 1)
                act.wait_ge(act_ch, n[0])

            def done(ins, s, v):
                ins.then_inc(s, 1)
                act.wait_ge(s, v)

            def fn(out_, in_, f, **kw):
                return nc.scalar.activation(out_, in_, f, **kw)

            act.wait_ge(vec_in, 16)
            done(fn(condc, V("c", 0, 8), ACT.Sigmoid), cond_sig, 1)

            act.wait_ge(lb_in, 1)
            done(fn(lbv, lbv, ACT.Exp), lb_exp, 1)

            act.wait_ge(pad_ready, 1)
            def shift_in(*groups):
                for g in groups:
                    t, free, k = PJ.wait_full(act, f"rw{g}")
                    done(fn(rwx[:, 2 * g:2 * g + 2, 1:], tiles(t[:, :], 2), ACT.Copy), free, k)

            def copy_in(name, g, dst):
                t, free, k = PJ.wait_full(act, f"{name}{g}")
                done(fn(dst[:, g * 512:(g + 1) * 512], t[:, :], ACT.Copy), free, k)

            shift_in(6, 2)
            act.wait_ge(xs_ready, 1)
            done(fn(rwx[0:64, 12, 1:], rwx[0:64, 12, 1:], ACT.Tanh), lora_act, 1)
            done(fn(rwx[:, 13, 1:], rwx[:, 13, 1:], ACT.Sigmoid), lora_act, 2)
            shift_in(3)
            for what, dst, v in (("lw", sig_w, "w0"), ("la", a_rw, "a0")):
                for i in range(2):
                    t, free, k = RW.wait_full(act, f"{what}{i}")
                    for j in range(2):
                        m = 2 * i + j
                        ins = fn(dst[:, m * T:(m + 1) * T], t[:, j * T:(j + 1) * T], ACT.Sigmoid, bias=V(v, m))
                        if j:
                            done(ins, free, k)
                        else:
                            link(ins)
            act.nop().then_inc(lora_done, 1)
            for i in range(2):
                t, free, k = RW.wait_full(act, f"lg{i}")
                done(fn(g_rw[:, i * 512:(i + 1) * 512], t[:, :], ACT.Copy), free, k)
            act.wait_ge(kk_ready, 1)
            done(fn(kk_sq, kk, ACT.Square), kk_sqd, 1)
            shift_in(0, 1)
            act.wait_ge(cs_ready, 1)
            link(fn(g_inv, cs0, ACT.Exp, scale=DECAY))
            link(fn(cs0, cs0, ACT.Exp, scale=-DECAY))
            done(fn(sig_w, sig_w, ACT.Exp, scale=-DECAY), dec_ready, 1)
            act.wait_ge(kk_n, 1)
            link(fn(kk_sq, kk_sq, ACT.Ln))
            done(fn(kk_sq, kk_sq, ACT.Exp, scale=-0.5), kk_n, 2)
            for g in range(2):
                t, free, k = PJ.wait_full(act, f"hgf{g}")
                link(fn(hb0[:, g * 512:(g + 1) * 512], t[:, :], ACT.Sigmoid))
                done(fn(hk[:, g * 512:(g + 1) * 512], t[:, :], ACT.Sigmoid, scale=-1.0), free, k)
            for g in range(2):
                copy_in("hgq", g, o_hg)
            shift_in(4, 5)
            act.wait_ge(lam_ready, 1)
            done(fn(lam4[:, 2:4], lam4[:, 0:2], ACT.Exp), lam_exp, 1)
            def out_gate(g):
                t, free, k = PJ.wait_full(act, f"hog{g}")
                link(fn(hog_s[:, g * 512:(g + 1) * 512], t[:, :], ACT.Sigmoid))
                done(fn(hog[:, g * 512:(g + 1) * 512], t[:, :], ACT.Copy), free, k)

            copy_in("hgv", 0, hv)
            act.wait_ge(f_ready, 1)
            done(fn(hb0, hb0, ACT.Ln), logf_ready, 1)
            copy_in("hgv", 1, hv)
            out_gate(0)
            act.wait_ge(dec_in, 1)
            link(fn(lvE, lvE, ACT.Exp, scale=-1.0))
            done(fn(lvQ, hb0, ACT.Exp), dec_out, 1)
            act.wait_ge(dec_in, 2)
            done(fn(small[:, 184:192], small[:, 184:192], ACT.Exp), dec_out, 2)

            def level_decay(i):
                act.wait_ge(dec_in, 3 + i)
                done(fn(lvE, lvE, ACT.Exp, scale=-1.0), dec_out, 3 + i)

            level_decay(0)
            out_gate(1)
            level_decay(1)
            copy_in("daq", 0, o_da)
            level_decay(2)
            copy_in("daq", 1, o_da)
            level_decay(3)
            copy_in("dak", 0, dk_)
            act.wait_ge(dec_in, 7)
            link(fn(lvQ, lvE, ACT.Exp))
            done(fn(lvE, lvE, ACT.Exp, scale=-1.0), dec_out, 7)
            copy_in("dak", 1, dk_)
            copy_in("dav", 0, dv_)
            for s in range(2):
                t, free, k = HD.wait_full(act, f"hgo{s}")
                link(fn(tiles(o_hg, 4)[:, :, s * P:(s + 1) * P], tiles(t[:, :], 4), ACT.Copy))
                done(fn(lvE[:, s * 512:(s + 1) * 512], t[:, :], ACT.Square), free, k)
                act.nop().then_inc(osq_ready, 1)
            copy_in("dav", 1, dv_)
            for s in range(2):
                t, free, k = HD.wait_full(act, f"hgs{s}")
                link(fn(lvK[:, s * 512:(s + 1) * 512], t[:, :], ACT.Ln, bias=RMS_EPS))
                done(fn(lvK[:, s * 512:(s + 1) * 512], lvK[:, s * 512:(s + 1) * 512], ACT.Exp, scale=-0.5), free, k)
            def gate_sig(b, i):
                t, free, k = PJ.wait_full(act, f"gate{b}_{i}")
                for j in range(2):
                    m = 2 * i + j
                    ins = fn(gates[b][:, m * T:(m + 1) * T], t[:, j * T:(j + 1) * T], ACT.Sigmoid, bias=V("b_merge", b * 8 + m))
                    if j:
                        done(ins, free, k)
                    else:
                        link(ins)

            S8 = tiles(att, 8)
            act.wait_ge(nmax_ready, 1)
            for i in range(8):
                link(fn(S8[:, i, 0:P], S8[:, i, 0:P], ACT.Exp, bias=smx[:, i:i + 1], accum_out=smx[:, 16 + i:17 + i]))
                ins = fn(S8[:, i, P:3 * P], S8[:, i, P:3 * P], ACT.Exp, bias=smx[:, 8 + i:9 + i],
                         accum_out=smx[:, 24 + i:25 + i])
                done(ins, e_ready, i + 1)
            gate_sig(0, 0)
            gate_sig(0, 1)
            for i in range(3):
                t, free, k = HD.wait_full(act, f"pT{i}")
                done(fn(probsT[:, i * 512:(i + 1) * 512], t[:, :], ACT.Copy), free, k)
            gate_sig(0, 2)
            for s in range(2):
                t, free, k = HD.wait_full(act, f"dao{s}")
                link(fn(tiles(o_da, 4)[:, :, s * P:(s + 1) * P], tiles(t[:, :], 4), ACT.Copy))
                done(fn(daSq[:, s * 512:(s + 1) * 512], t[:, :], ACT.Square), free, k)
                act.nop().then_inc(osq_ready, 1)
            gate_sig(0, 3)
            for s in range(2):
                t, free, k = HD.wait_full(act, f"das{s}")
                link(fn(daR[:, s * 512:(s + 1) * 512], t[:, :], ACT.Ln, bias=RMS_EPS))
                done(fn(daR[:, s * 512:(s + 1) * 512], daR[:, s * 512:(s + 1) * 512], ACT.Exp, scale=-0.5), free, k)
            act.wait_ge(o_ready, 2)
            for hf in range(2):
                NT, X, XT, YY, NL, AKT, RBT, RKT, tok, Y0, UP, WAT, ST = rw_mats(hf)
                for i in range(4):
                    t, free, k = RW.wait_full(act, f"{hf}tok{i}")
                    done(fn(tok[i], t[:, :], ACT.Copy), free, k)
                gate_sig(1 + hf, 0)
                for hp in range(2):
                    t, free, k = RW.wait_full(act, f"{hf}x1_{hp}")
                    done(fn(X[:, hp * 512:(hp + 1) * 512], t[:, :], ACT.Copy), free, k)
                for i, b in enumerate(LEVELS[1:6]):
                    for hp in range(2):
                        t, free, k = RW.wait_full(act, f"{hf}y{b}_{hp}")
                        done(fn(YY[:, hp * 512:(hp + 1) * 512], t[:, :], ACT.Copy), free, k)
                    if i % 2:
                        gate_sig(1 + hf, 1 + i // 2)
                    if b < 32:
                        for hp in range(2):
                            t, free, k = RW.wait_full(act, f"{hf}xx{b}_{hp}")
                            done(fn(X[:, hp * 512:(hp + 1) * 512], t[:, :], ACT.Copy), free, k)
                for hp in range(2):
                    t, free, k = RW.wait_full(act, f"{hf}y0_{hp}")
                    done(fn(tiles(Y0, 4)[:, :, hp * 64:hp * 64 + 64], tiles(t[:, :], 4)[:, :, hp * 64:hp * 64 + 64],
                            ACT.Copy), free, k)
                for hp in range(2):
                    t, free, k = RW.wait_full(act, f"{hf}up_{hp}")
                    done(fn(tiles(UP, 4)[:, :, hp * 64:hp * 64 + 64], tiles(t[:, :], 4)[:, :, hp * 64:hp * 64 + 64],
                            ACT.Copy), free, k)
                t, free, k = RW.wait_full(act, f"{hf}wat")
                done(fn(WAT, t[:, :], ACT.Copy), free, k)
                gate_sig(1 + hf, 3)
                t, free, k = RW.wait_full(act, f"{hf}o")
                done(fn(o_rw[:, hf * 512:(hf + 1) * 512], t[:, :], ACT.Copy), free, k)
                act.nop().then_inc(orw_copied, 1)
                act.wait_ge(go_d, hf + 1)
                done(fn(kk_gn(hf), o_rw[:, hf * 512:(hf + 1) * 512], ACT.Square), go_sq, hf + 1)
                t, free, k = RW.wait_full(act, f"{hf}gv")
                link(fn(kk_gn(hf), t[:, :], ACT.Ln, bias=GN_EPS))
                done(fn(kk_gn(hf), kk_gn(hf), ACT.Exp, scale=-0.5), free, k)
            act.wait_ge(lnd, 1)
            done(fn(LNT, xT, ACT.Square), lnsq, 1)
            t, free, k = PJ.wait_full(act, "ln1v")
            link(fn(LNT[:, 0:T], t[:, 0:T], ACT.Ln, bias=LN_EPS))
            done(fn(LNT[:, 0:T], LNT[:, 0:T], ACT.Exp, scale=-0.5), free, k)
            t, free, k = PJ.wait_full(act, "logit")
            done(fn(lgT[0:E, :], t[0:E, 0:T], ACT.Copy), free, k)
            act.wait_ge(lg_exp_in, 1)
            done(fn(scores, scores, ACT.Exp), lg_exp, 1)
            for i in range(4):
                t, free, k = PJ.wait_full(act, f"u2t{i}")
                done(fn(U2K[:, i * 512:(i + 1) * 512], t[:, :], ACT.Copy), free, k)

            def picks(b):
                for f in range(4):
                    act.wait_ge(pw_full, 4 * b + f + 1)
                    done(fn(PWT[:, f * 512:(f + 1) * 512], bank[2 + f][:, :], ACT.Copy), pw_copied, 4 * b + f + 1)

            def gathered(n):
                for half in range(2):
                    act.wait_ge(xg_full, 2 * n + half + 1)
                    done(fn(XG[:, half * 512:(half + 1) * 512], bank[half][:, :], ACT.Copy), xg_ready, 2 * n + half + 1)

            def pair(n, more):
                act.wait_ge(gate_full, n + 1)
                done(fn(SG, bank[2][:, :], ACT.Sigmoid), sig_ready, n + 1)
                if more:
                    act.wait_ge(up_full, n + 1)
                    gathered(n + 1)
                act.wait_ge(hT_full, n + 1)
                done(fn(HT_, bank[4][:, :], ACT.Copy), hT_ready, n + 1)
                for half in range(2):
                    act.wait_ge(y_full, 2 * n + half + 1)
                    done(fn(Y[:, half * 512:(half + 1) * 512], bank[5 + half][:, :], ACT.Copy), y_ready, 2 * n + half + 1)

            def one_pass(b, n0):
                picks(b)
                gathered(n0)
                with act.Fori(0, PAIRS - 1) as p:
                    pair(n0 + p, True)
                pair(n0 + PAIRS - 1, False)

            one_pass(0, 0)
            act.wait_ge(flag_ready, 1)
            over_ = act.value_load(flag_i[0:1, 0:1], min_val=0, max_val=1)
            with act.If(over_ > 0):
                with act.Fori(1, PASSES) as b:
                    one_pass(b, b * PAIRS)
            act.wait_ge(lnd, 2)
            done(fn(LNT, xT, ACT.Square), lnsq, 2)
            act.wait_ge(ln2_sum, 2)
            link(fn(LNT[:, 0:T], bank[1][:, 0:T], ACT.Ln, bias=LN_EPS))
            done(fn(LNT[:, 0:T], LNT[:, 0:T], ACT.Exp, scale=-0.5), lnr, 1)

        @block.vector
        def _(dve):
            n = [0]
            v = nc.vector

            def link(ins):
                n[0] += 1
                ins.then_inc(dve_ch, 1)
                dve.wait_ge(dve_ch, n[0])

            def done(ins, s, val):
                ins.then_inc(s, 1)
                dve.wait_ge(s, val)

            def tick(s):
                dve.nop().then_inc(s, 1)

            dve.wait_ge(vec_in, 16)
            dve.wait_ge(cond_sig, 1)
            link(v.tensor_tensor(condc, condc, V("c", 0, 8), ALU.mult))
            done(v.tensor_copy(condb.rearrange("p (k r) -> p k r", k=KT), condc.unsqueeze(2).to_broadcast([P, KT, 32])),
                 cond_ready, 1)
            done(v.tensor_tensor(lbv, V("hg_lb", 0, 4), V("hg_lb", 0, 4), ALU.subtract), lb_in, 1)
            dve.wait_ge(lb_exp, 1)
            link(v.reciprocal(oml, lbv))
            link(v.tensor_tensor(oml, oml, lbv, ALU.mult))
            link(v.tensor_tensor(lbv, oml, oml, ALU.subtract))
            link(v.tensor_scalar(oml, lbv, -1.0, 1.0, ALU.mult, ALU.add))

            def mod_row(r):
                t, free, k = (HD if r else PJ).wait_full(dve, f"ada{r}")
                done(v.tensor_copy(modrow, t[:, :]), free, k)
                tick(modrow_ready)

            def mod_cols(r):
                t, free, k = (HD if r else PJ).wait_full(dve, f"adaT{r}")
                src = t[:, :].rearrange("p (i g x) -> p g i x", i=4, g=4)[:, :, :, 0]
                dst = modc[:, 16 * r:16 * r + 16].rearrange("p (g i) -> p g i", g=4)
                done(v.tensor_tensor(dst, src, V("b_ada", 16 * r, 16).rearrange("p (g i) -> p g i", g=4), ALU.add), free, k)

            mod_row(0)
            mod_cols(0)
            link(v.tensor_scalar(sc1p, modc[:, 8:16], 1.0, None, ALU.add))
            dve.wait_ge(x_in, 16)
            x3, u3 = tiles(xT, KT), tiles(uT, KT)
            for m in range(KT):
                link(v.tensor_scalar(u3[:, m, :], x3[:, m, :], sc1p[:, m:m + 1], modc[:, m:m + 1], ALU.mult, ALU.add))
            tick(u_ready)

            dve.wait_ge(row_in, 48)
            l4 = tiles(lam_sb, 4)
            link(v.tensor_tensor(tiles(lam_t, 2), l4[:, 0:4:2, :], l4[:, 1:4:2, :], ALU.mult))
            done(v.tensor_reduce(lam4[:, 0:2], tiles(lam_t, 2), axis=AX.X, op=ALU.add), lam_ready, 1)

            def shift(*ms):
                for m in ms:
                    PJ.wait_read(dve, f"rw{m // 2}")
                    link(v.tensor_tensor(hb1[:, 0:T], rwx[:, m, 0:T], rwx[:, m, 1:], ALU.subtract))
                    link(v.scalar_tensor_tensor(rwx[:, m, 1:], hb1[:, 0:T], V("mu", m), rwx[:, m, 1:], ALU.mult, ALU.add))

            shift(12, 13)
            tick(xs_ready)
            r3, k3, v3 = [rwx[:, 4 * i:4 * i + 4, 1:] for i in range(3)]
            shift(4, 5, 6, 7)
            kk3, sq3 = tiles(kk, 4), tiles(kk_sq, 4)
            for j in range(4):
                link(v.tensor_scalar(kk3[:, j, :], k3[:, j, :], V("k_k", j), None, ALU.mult))
            tick(kk_ready)

            def cumsum(a, b, save=None):
                for i in range(6):
                    d = 1 << i
                    s_, t_ = (a, b) if i % 2 == 0 else (b, a)
                    sv, tv = [x.rearrange("p (n c) -> p n c", c=C) for x in (s_, t_)]
                    link(v.tensor_tensor(tv[:, :, d:C], sv[:, :, d:C], sv[:, :, 0:C - d], ALU.add))
                    link(v.tensor_copy(tv[:, :, 0:d], sv[:, :, 0:d]))

            dve.wait_ge(lora_done, 1)
            link(v.tensor_copy(cs0, sig_w))
            cumsum(cs0, cs1)
            done(v.tensor_tensor(sig_w, cs0, sig_w, ALU.subtract), cs_ready, 1)
            for j in range(4):
                link(v.tensor_scalar(cs1[:, j * T:(j + 1) * T], a_rw[:, j * T:(j + 1) * T], -1.0, V("k_a", j), ALU.add, ALU.mult))
            link(v.scalar_tensor_tensor(k3, tiles(cs1, 4), 1.0, k3, ALU.add, ALU.mult))
            shift(0, 1, 2, 3)
            for i in range(2):
                t, free, k = RW.wait_full(dve, f"kk{i}")
                done(v.tensor_scalar(kk_sq[:, i * 512:(i + 1) * 512], t[:, :], 1e-12, None, ALU.max), free, k)
            tick(kk_n)
            dve.wait_ge(kk_n, 2)
            link(v.tensor_tensor(kk, kk, kk_sq, ALU.mult))
            link(v.tensor_tensor(sq3, r3, k3, ALU.mult))
            for j in range(4):
                link(v.tensor_scalar(sq3[:, j, :], sq3[:, j, :], V("r_k", j), None, ALU.mult))
            tick(rk_ready)
            dve.wait_ge(dec_ready, 1)
            link(v.scalar_tensor_tensor(at_f, kk, -1.0, sig_w, ALU.mult, ALU.mult))
            link(v.tensor_tensor(a_rw, a_rw, kk, ALU.mult))
            link(v.tensor_tensor(a_rw, a_rw, g_inv, ALU.mult))
            link(v.tensor_tensor(tiles(kt_f, 4), k3, tiles(g_inv, 4), ALU.mult))
            link(v.tensor_tensor(tiles(rt_f, 4), r3, tiles(cs0, 4), ALU.mult))
            link(v.tensor_copy(gend.rearrange("p (n c) -> p n c", c=1), cs0.rearrange("p (n c) -> p n c", c=C)[:, :, C - 1:C]))
            shift(8, 9, 10, 11)
            for i in range(2):
                t, free, k = RW.wait_full(dve, f"bo{i}")
                done(v.tensor_tensor(tiles(bonus, 4)[:, 2 * i:2 * i + 2, :], tiles(t[:, :], 2), v3[:, 2 * i:2 * i + 2, :],
                                     ALU.mult), free, k)
            tick(rwf_ready)

            PJ.wait_read(dve, "hgf1")
            hb03, hk3 = tiles(hb0, 4), tiles(hk, 4)
            for h in range(H4):
                link(v.tensor_scalar(hb03[:, h, :], hb03[:, h, :], oml[:, h:h + 1], lbv[:, h:h + 1], ALU.mult, ALU.add))
                link(v.tensor_scalar(hk3[:, h, :], hk3[:, h, :], oml[:, h:h + 1], None, ALU.mult))
            done(v.tensor_scalar(hb0, hb0, 1e-6, None, ALU.max), f_ready, 1)
            dve.wait_ge(logf_ready, 1)
            cumsum(hb0, hb1)
            PJ.wait_read(dve, "hgq1")
            hcs = hb0.rearrange("p (n c) -> p n c", c=C)
            ev = lvE.rearrange("p (n c) -> p n c", c=C)
            done(v.tensor_tensor(ev, hcs, hcs[:, :, C - 1:C].to_broadcast([P, 16, C]), ALU.subtract), dec_in, 1)
            far = small[:, 184:192]
            ends = hcs[:, :, C - 1:C].rearrange("p (h c) x -> p h (c x)", h=4)[:, :, 1:3]
            link(v.tensor_copy(far.rearrange("p (h c) -> p h c", h=4), ends))
            dve.wait_ge(dec_out, 1)
            tick(dec_in)
            link(v.tensor_tensor(lvK, hk, lvE, ALU.mult))
            link(v.tensor_tensor(lvQ, o_hg, lvQ, ALU.mult))
            tick(lev_ready)
            dve.wait_ge(dec_out, 2)
            K128, Q128 = tiles(lvX, 8)[:, 0:4, :], tiles(lvX, 8)[:, 4:8, :]
            f3 = far.rearrange("p (h c) -> p h c", h=4)
            Kl, Ql = tiles(lvK, 4), tiles(lvQ, 4)
            link(v.tensor_tensor(K128[:, :, 0:C], Kl[:, :, 0:C], f3[:, :, 0:1].to_broadcast([P, 4, C]), ALU.mult))
            link(v.tensor_copy(K128[:, :, C:P], Kl[:, :, C:P]))
            link(v.tensor_copy(Q128[:, :, 0:C], Ql[:, :, P:P + C]))
            link(v.tensor_tensor(Q128[:, :, C:P], Ql[:, :, P + C:T], f3[:, :, 1:2].to_broadcast([P, 4, C]), ALU.mult))
            tick(lev_ready)
            A4 = scoresT.rearrange("p (a h t) -> p a h t", a=3, h=H4)

            def take_scores(b, first):
                for s in range(2):
                    t, free, k = HD.wait_full(dve, f"a{b}_{s}")
                    m = over(M(f"lev{b}" if b else "quad"), 4)
                    if first:
                        done(v.tensor_tensor(A4[:, s], tiles(t[:, :], 4), m, ALU.mult), free, k)
                    else:
                        done(v.tensor_tensor(tiles(hb1[:, 0:512], 4), tiles(t[:, :], 4), m, ALU.mult), free, k)
                        link(v.tensor_tensor(A4[:, s], A4[:, s], tiles(hb1[:, 0:512], 4), ALU.add))

            take_scores(64, True)
            t, free, k = HD.wait_full(dve, "a128")
            done(v.tensor_copy(A4[:, 2], tiles(t[:, :], 4)), free, k)
            prev = None
            for i, b in enumerate((32, 16, 8, 4, 0)):
                w = 2 * b if b else 4
                nn = 1024 // w
                bv, e_ = [x.rearrange("p (n c) -> p n c", c=w) for x in (hb0, lvE)]
                if not b:
                    take_scores(prev, False)
                if b:
                    ref = bv[:, :, b - 1:b].to_broadcast([P, nn, b])
                    link(v.tensor_tensor(e_[:, :, 0:b], bv[:, :, 0:b], ref, ALU.subtract))
                    done(v.tensor_tensor(e_[:, :, b:w], ref, bv[:, :, b:w], ALU.subtract), dec_in, 3 + i)
                else:
                    ref = bv[:, :, 1:2].to_broadcast([P, nn, w])
                    done(v.tensor_tensor(e_, bv, ref, ALU.subtract), dec_in, 3 + i)
                if i and b:
                    take_scores(prev, False)
                prev = b
                dve.wait_ge(dec_out, 3 + i)
                link(v.tensor_tensor(lvK, hk, lvE, ALU.mult))
                link(v.tensor_tensor(lvQ, o_hg, lvE if b else lvQ, ALU.mult))
                tick(lev_ready)
            take_scores(0, False)
            PJ.wait_read(dve, "hgv1")
            tick(at_ready)
            PJ.wait_read(dve, "hog1")
            link(v.tensor_tensor(hog, hog, hog_s, ALU.mult))
            HD.wait_read(dve, "hgo1")
            HD.wait_read(dve, "hgo0")
            for s in range(2):
                HD.wait_read(dve, f"hgs{s}")
                o = tiles(o_hg, 4)[:, :, s * P:(s + 1) * P]
                link(v.scalar_tensor_tensor(o, o, V("hg_norm"), tiles(lvK[:, s * 512:(s + 1) * 512], 4), ALU.mult, ALU.mult))
                link(v.tensor_tensor(o, o, tiles(hog, 4)[:, :, s * P:(s + 1) * P], ALU.mult))
            tick(o_ready)

            S8 = tiles(att, 8)
            dist = cst[:, DIST0:DIST0 + 3 * P]
            for h in range(H4):
                slope = 2.0 ** (-8.0 * (h + 1) / H4)
                for m in range(2):
                    t, free, k = HD.wait_full(dve, f"s{h}_{m}")
                    done(v.scalar_tensor_tensor(S8[:, 2 * h + m, :], dist, -slope, t[:, 0:3 * P], ALU.mult, ALU.add), free, k)
            link(v.tensor_reduce(smx[:, 32:40], S8[:, :, 0:P], axis=AX.X, op=ALU.max))
            link(v.tensor_reduce(smx[:, 40:48], S8[:, :, P:3 * P], axis=AX.X, op=ALU.max))
            done(v.tensor_scalar(smx[:, 0:16], smx[:, 32:48], -1.0, None, ALU.mult), nmax_ready, 1)
            dve.wait_ge(lam_exp, 1)
            link(v.tensor_tensor(lam4[:, 4:5], lam4[:, 2:3], lam4[:, 3:4], ALU.subtract))
            link(v.tensor_scalar(lam4[:, 5:6], lam4[:, 4:5], LAM_INIT, -1.0, ALU.add, ALU.mult))
            dve.wait_ge(e_ready, 8)
            link(v.reciprocal(smx[:, 48:64], smx[:, 16:32]))
            link(v.tensor_scalar(smx[:, 49:64:2], smx[:, 49:64:2], lam4[:, 5:6], None, ALU.mult))
            for h in range(H4):
                for (c0, c1, o) in ((0, P, 48), (P, 3 * P, 56)):
                    link(v.tensor_scalar(S8[:, 2 * h, c0:c1], S8[:, 2 * h, c0:c1], smx[:, o + 2 * h:o + 2 * h + 1], None, ALU.mult))
                    link(v.scalar_tensor_tensor(S8[:, 2 * h, c0:c1], S8[:, 2 * h + 1, c0:c1], smx[:, o + 2 * h + 1:o + 2 * h + 2],
                                                S8[:, 2 * h, c0:c1], ALU.mult, ALU.add))
            tick(p_ready)
            link(v.tensor_scalar(lam4[:, 6:7], V("da_subln"), 1.0 - LAM_INIT, None, ALU.mult))
            HD.wait_read(dve, "dao1")
            HD.wait_read(dve, "dao0")
            for s in range(2):
                HD.wait_read(dve, f"das{s}")
                o = tiles(o_da, 4)[:, :, s * P:(s + 1) * P]
                link(v.scalar_tensor_tensor(o, o, lam4[:, 6:7], tiles(daR[:, s * 512:(s + 1) * 512], 4), ALU.mult, ALU.mult))
            tick(o_ready)

            for hf in range(2):
                NT, X, XT, YY, NL, AKT, RBT, RKT, tok, Y0, UP, WAT, ST = rw_mats(hf)
                for i, (dst, mask) in enumerate(((NT, "strict"), (AKT, "strict"), (RBT, "incl"), (RKT, "incl"))):
                    if i == 1:
                        link(v.tensor_tensor(tiles(XT, 8), tiles(NT, 8), over(M("lev1"), 8), ALU.mult))
                        done(v.tensor_tensor(tiles(XT, 8), tiles(XT, 8), over(M("ident"), 8), ALU.add), xt_ready, hf + 1)
                    for hp in range(2):
                        t, free, k = RW.wait_full(dve, f"{hf}m{i}_{hp}")
                        done(v.tensor_tensor(tiles(dst[:, hp * 512:(hp + 1) * 512], 4), tiles(t[:, :], 4), over(M(mask), 4),
                                             ALU.mult), free, k)
                        tick(m_ready)
                link(v.memset(ST[:, 0:2 * P], 0.0))
                for i, b in enumerate(LEVELS[1:6]):
                    for hp in range(2):
                        t, free, k = RW.wait_full(dve, f"{hf}xt{b}_{hp}")
                        d_ = XT[:, hp * 512:(hp + 1) * 512]
                        done(v.tensor_tensor(d_, d_, t[:, :], ALU.add), free, k)
                mod_row(1 + hf)
                RW.wait_read(dve, f"{hf}up_0")
                RW.wait_read(dve, f"{hf}up_1")
                U4 = UP.rearrange("p (j s d) -> p j s d", j=2, s=2)
                for c in range(NCH):
                    s, r = c // 2, slice((c % 2) * 64, (c % 2) * 64 + 64)
                    if c:
                        t, free, k = RW.wait_full(dve, f"{hf}u{c}")
                        done(v.tensor_tensor(U4[r, :, s, :], U4[r, :, s, :], tiles(t[:, 0:256], 2)[r], ALU.add), free, k)
                    if c < NCH - 1:
                        t, free, k = RW.wait_full(dve, f"{hf}s{c}")
                        nxt = tiles(ST[:, (c + 1) * 256:(c + 2) * 256], 2)
                        done(v.tensor_tensor(nxt, tiles(t[:, 0:256], 2), over(M("pair"), 2), ALU.mult), free, k)
                        link(v.tensor_tensor(nxt, nxt, tiles(ST[:, c * 256:(c + 1) * 256], 2), ALU.add))
                        for jj in range(2):
                            g = (2 * hf + jj) * 4 + c
                            ins = v.tensor_scalar(nxt[:, jj, :], nxt[:, jj, :], gend[:, g:g + 1], None, ALU.mult)
                            if jj:
                                done(ins, st_ready, 3 * hf + c + 1)
                            else:
                                link(ins)
                mod_cols(1 + hf)
                dve.wait_ge(orw_copied, hf + 1)
                o = o_rw[:, hf * 512:(hf + 1) * 512]
                t, free, k = RW.wait_full(dve, f"{hf}gm")
                done(v.tensor_tensor(o, o, t[:, :], ALU.subtract), free, k)
                tick(go_d)
                RW.wait_read(dve, f"{hf}gv")
                link(v.tensor_tensor(o, o, kk_gn(hf), ALU.mult))
                for jj in range(2):
                    j = 2 * hf + jj
                    link(v.tensor_scalar(o_rw[:, j * T:(j + 1) * T], o_rw[:, j * T:(j + 1) * T], V("gn_g", j), V("gn_b", j),
                                         ALU.mult, ALU.add))
                link(v.tensor_tensor(o, o, bonus[:, hf * 512:(hf + 1) * 512], ALU.add))
                link(v.tensor_tensor(o, o, g_rw[:, hf * 512:(hf + 1) * 512], ALU.mult))
                tick(o_ready)

            link(v.tensor_scalar(g1p, modc[:, 16:24], 1.0, None, ALU.add))
            link(v.tensor_scalar(sc2p, modc[:, 32:40], 1.0, None, ALU.add))
            link(v.tensor_scalar(g2p, modc[:, 40:48], 1.0, None, ALU.add))

            for b in range(3):
                for i in range(4):
                    PJ.wait_read(dve, f"gate{b}_{i}")
                    t, free, k = PJ.wait_full(dve, f"br{b}_{i}")
                    g = gates[b][:, i * 512:(i + 1) * 512]
                    done(v.tensor_tensor(g, g, t[:, :], ALU.mult), free, k)
                    if b:
                        m_ = gates[0][:, i * 512:(i + 1) * 512]
                        link(v.tensor_tensor(m_, m_, g, ALU.add))
                    if b == 2:
                        tick(merged_ready)
            for i in range(4):
                t, free, k = PJ.wait_full(dve, f"out{i}")
                for j in range(2):
                    m = 2 * i + j
                    ins = v.tensor_scalar(gates[1][:, m * T:(m + 1) * T], t[:, j * T:(j + 1) * T], g1p[:, m:m + 1], None, ALU.mult)
                    if j:
                        done(ins, free, k)
                    else:
                        link(ins)
                sl = slice(i * 512, (i + 1) * 512)
                link(v.scalar_tensor_tensor(xT[:, sl], xT[:, sl], ALPHA, gates[1][:, sl], ALU.mult, ALU.add))
            tick(y1_ready)

            t, free, k = PJ.wait_full(dve, "ln1m")
            done(v.tensor_tensor(x3, x3, over(t[:, 0:T], KT), ALU.subtract), free, k)
            tick(lnd)
            PJ.wait_read(dve, "ln1v")
            link(v.tensor_tensor(x3, x3, over(LNT[:, 0:T], KT), ALU.mult))
            for m in range(KT):
                link(v.tensor_scalar(x3[:, m, :], x3[:, m, :], V("ln_g", m), V("ln_b", m), ALU.mult, ALU.add))
                link(v.tensor_scalar(u3[:, m, :], x3[:, m, :], sc2p[:, m:m + 1], modc[:, 24 + m:25 + m], ALU.mult, ALU.add))
            tick(u2_ready)
            done(v.memset(ACC, 0.0), comb_added, 1)

            s3 = scores.rearrange("p (b e) -> p b e", b=2)
            t, free, k = PJ.wait_full(dve, "logitT")
            done(v.tensor_copy(scores, t[:, 0:2 * E]), free, k)
            link(v.tensor_reduce(rt2[:, 0:2], s3, axis=AX.X, op=ALU.max))
            done(v.tensor_tensor(s3, s3, rt2[:, 0:2].unsqueeze(2).to_broadcast([P, 2, E]), ALU.subtract), lg_exp_in, 1)
            dve.wait_ge(lg_exp, 1)
            link(v.tensor_reduce(rt2[:, 0:2], s3, axis=AX.X, op=ALU.add))
            link(v.reciprocal(rt2[:, 2:4], rt2[:, 0:2]))
            link(v.tensor_tensor(s3, s3, rt2[:, 2:4].unsqueeze(2).to_broadcast([P, 2, E]), ALU.mult))
            sel = route[:, 84:116]
            link(v.tensor_tensor(sel.rearrange("p (b e) -> p b e", b=2), s3, RB.unsqueeze(1).to_broadcast([P, 2, E]), ALU.add))
            s4 = sel.rearrange("p (n j) -> p n j", j=4)
            big, big2 = LNT[:, 0:128], LNT[:, 128:256]
            tie = cst[:, TIE0:TIE0 + 16].rearrange("p (j i) -> p j i", j=4)

            def ranks(vals, nn, out_):
                w = nn * 16
                b3 = big[:, 0:w].rearrange("p (n j i) -> p n j i", j=4, i=4)
                c3 = big2[:, 0:w].rearrange("p (n j i) -> p n j i", j=4, i=4)
                vi = vals.unsqueeze(2).to_broadcast([P, nn, 4, 4])
                vj = vals.unsqueeze(3).to_broadcast([P, nn, 4, 4])
                link(v.tensor_tensor(b3, vi, vj, ALU.is_gt))
                link(v.tensor_tensor(c3, vi, vj, ALU.is_equal))
                link(v.tensor_tensor(c3, c3, tie.unsqueeze(1).to_broadcast([P, nn, 4, 4]), ALU.mult))
                link(v.tensor_tensor(b3, b3, c3, ALU.add))
                link(v.tensor_reduce(out_, b3, axis=AX.X, op=ALU.add))

            rk = route[:, 116:148]
            ranks(s4, 8, rk.rearrange("p (n j) -> p n j", j=4))
            top2 = route[:, 148:180]
            link(v.tensor_scalar(top2, rk, 2.0, None, ALU.is_lt))
            gs = route[:, 180:188]
            link(v.tensor_tensor(rk, top2, sel, ALU.mult))
            link(v.tensor_reduce(gs, rk.rearrange("p (n j) -> p n j", j=4), axis=AX.X, op=ALU.add))
            grk = route[:, 188:196]
            ranks(gs.rearrange("p (n j) -> p n j", j=4), 2, grk.rearrange("p (n j) -> p n j", j=4))
            link(v.tensor_scalar(grk, grk, 1.0, None, ALU.is_lt))
            done(v.tensor_tensor(chosen.rearrange("p (n j) -> p n j", j=4), top2.rearrange("p (n j) -> p n j", j=4),
                                 grk.unsqueeze(2).to_broadcast([P, 8, 4]), ALU.mult), chosen_ready, 1)
            link(v.tensor_tensor(scores, scores, chosen, ALU.mult))
            link(v.tensor_reduce(rt2[:, 0:2], s3, axis=AX.X, op=ALU.add))
            link(v.reciprocal(rt2[:, 2:4], rt2[:, 0:2]))
            link(v.tensor_tensor(s3, s3, rt2[:, 2:4].unsqueeze(2).to_broadcast([P, 2, E]), ALU.mult))
            t, free, k = PJ.wait_full(dve, "rank")
            link(v.tensor_reduce(rt2[:, 0:1], t[:, 2 * E:3 * E], axis=AX.X, op=ALU.max))
            done(v.scalar_tensor_tensor(slot, t[:, 0:2 * E], 1.0, chosen, ALU.add, ALU.mult), free, k)
            link(v.tensor_scalar(slot, slot, -1.0, None, ALU.add))
            done(v.tensor_scalar(flag_i[0:1, 0:1], rt2[0:1, 0:1], float(CAP), None, ALU.is_gt), flag_ready, 1)

            iota = cst[:, IOTA0:IOTA0 + CAP]

            def picks(b):
                for s in range(2):
                    pk = PK[:, s * 1024:(s + 1) * 1024].rearrange("p (e j) -> p e j", e=E)
                    pw = PW[:, s * 1024:(s + 1) * 1024].rearrange("p (e j) -> p e j", e=E)
                    sl = slot[:, s * E:(s + 1) * E].unsqueeze(2).to_broadcast([P, E, CAP])
                    wt = scores[:, s * E:(s + 1) * E].unsqueeze(2).to_broadcast([P, E, CAP])
                    done(v.tensor_tensor(pk, over(iota, E), sl, ALU.is_equal), blk_ch, 5 * b + 2 * s + 1)
                    done(v.tensor_tensor(pw, pk, wt, ALU.mult), blk_ch, 5 * b + 2 * s + 2)
                done(v.tensor_scalar(slot, slot, -float(CAP), None, ALU.add), blk_ch, 5 * b + 5)
                tick(pick_ready)

            def pair(n_):
                dve.wait_ge(sig_ready, n_ + 1)
                done(v.tensor_tensor(HM, bank[2][:, :], SG, ALU.mult), moe_ch, n_ + 1)
                dve.wait_ge(up_full, n_ + 1)
                done(v.tensor_tensor(HH, bank[3][:, :], HM, ALU.mult), h_ready, n_ + 1)
                for i in range(4):
                    dve.wait_ge(comb_full, 4 * n_ + i + 1)
                    a_ = ACC[:, i * 512:(i + 1) * 512]
                    bk = bank[7] if i % 2 == 0 else bank[2]
                    done(v.tensor_tensor(a_, a_, bk[:, :], ALU.add), comb_added, 4 * n_ + i + 2)

            def one_pass(b, n0):
                picks(b)
                with dve.Fori(0, PAIRS) as p:
                    pair(n0 + p)

            one_pass(0, 0)
            over_ = dve.value_load(flag_i[0:1, 0:1], min_val=0, max_val=1)
            with dve.If(over_ > 0):
                with dve.Fori(1, PASSES) as b:
                    one_pass(b, b * PAIRS)

            a3 = tiles(ACC, KT)
            for m in range(KT):
                link(v.tensor_scalar(a3[:, m, :], a3[:, m, :], g2p[:, m:m + 1], None, ALU.mult))
            link(v.scalar_tensor_tensor(xT, xT, ALPHA, ACC, ALU.mult, ALU.add))
            tick(y1_ready)
            dve.wait_ge(ln2_sum, 1)
            link(v.tensor_tensor(x3, x3, over(bank[0][:, 0:T], KT), ALU.subtract))
            tick(lnd)
            dve.wait_ge(lnr, 1)
            for i in range(4):
                link(v.tensor_tensor(x3[:, 2 * i:2 * i + 2, :], x3[:, 2 * i:2 * i + 2, :], over(LNT[:, 0:T], 2), ALU.mult))
                for m in (2 * i, 2 * i + 1):
                    ins = v.tensor_scalar(u3[:, m, :], x3[:, m, :], V("ln_g", 8 + m), V("ln_b", 8 + m), ALU.mult, ALU.add)
                    if m % 2:
                        done(ins, x2_ready, i + 1)
                    else:
                        link(ins)


_INS = ["xt", "w_ada", "w_in", "w_merge", "w_branch", "w_out", "w_router", "w_gate", "w_up", "w_down",
        "vecs", "consts", "lam_row", "rbias_row", "rw_w_up", "rw_a_up", "rw_g_up"]


def _constants():
    import numpy as np
    i = np.arange(P)
    s, t = i[:, None], i[None, :]
    same = lambda w: (s // w) == (t // w)
    m = {"ident": s == t, "ones_d": np.full((P, P), 1.0 / D), "ones_dv": np.full((P, P), 1.0 / P),
         "pair": same(64), "pair_mean": same(64) / 64.0, "ones": np.ones((P, P)),
         "quad": same(4) & (s <= t), "strict": same(C) & (s < t), "incl": same(C) & (s <= t), "before": s < t}
    for b in LEVELS:
        m[f"lev{b}"] = same(2 * b) & (s % (2 * b) < b) & (t % (2 * b) >= b)
    own = np.where(s >= t, s - t, 1e33)
    dist = np.concatenate([own, s - t + P, own], 1)
    iota = np.broadcast_to(np.arange(CAP), (P, CAP))
    j4 = np.arange(4)
    tie = np.broadcast_to((j4[None, :] < j4[:, None]).reshape(1, 16), (P, 16))
    return np.concatenate([np.asarray(m[n], np.float32) for n in MATS] + [dist, iota, tie], 1).astype(np.float32)


def kernel(**inputs):
    import numpy as np
    import concourse.bacc as bacc
    from concourse.bass_utils import run_bass_kernel_spmd

    a = {k: np.asarray(x) for k, x in inputs.items()}

    def by_channel(w):
        return w.reshape(-1, P, w.shape[-1])

    cols = lambda x: x.reshape(-1, P).T
    parts = {"c": a["c"], "b_ada": a["b_ada"], "hg_lb": a["hg_lb_logits"], "hg_norm": a["hg_norm_g"],
             "da_subln": a["da_subln_g"], "mu": a["rw_mu"], "w0": a["rw_w0"], "a0": a["rw_a0"], "k_k": a["rw_k_k"],
             "k_a": a["rw_k_a"], "r_k": a["rw_r_k"], "gn_g": a["rw_gn_g"], "gn_b": a["rw_gn_b"],
             "b_merge": a["b_merge"], "ln_g": a["ln_g"], "ln_b": a["ln_b"]}
    arrays = {
        "xt": by_channel(a["x"][0].T), "w_ada": by_channel(a["w_ada"][0]), "w_in": by_channel(a["w_in"][0]),
        "w_merge": a["w_merge"][0].reshape(3, KT, P, D), "w_branch": by_channel(a["w_branch"][0]),
        "w_out": by_channel(a["w_out"][0]), "w_router": by_channel(a["w_router"]),
        "w_gate": a["w_exp_gate"][0].reshape(E, KT, P, FE), "w_up": a["w_exp_up"][0].reshape(E, KT, P, FE),
        "w_down": a["w_exp_down"][0].reshape(E, FE // P, P, D),
        "vecs": np.concatenate([cols(parts[n]) for n, _ in VECS], 1), "consts": _constants(),
        "lam_row": a["da_lambda"].reshape(1, 256), "rbias_row": a["router_bias"].reshape(1, E),
        "rw_w_up": a["rw_w_up"][0], "rw_a_up": a["rw_a_up"][0], "rw_g_up": a["rw_g_up"][0],
    }
    arrays = {k: np.ascontiguousarray(x) for k, x in arrays.items()}
    nc = bacc.Bacc("TRN2", target_bir_lowering=False, num_devices=1)
    d = {n: nc.dram_tensor(f"in_{n}", arrays[n].shape, mybir.dt.from_np(arrays[n].dtype), kind="ExternalInput").ap()
         for n in _INS}
    for n in ("xt", "w_ada", "w_in", "w_branch", "w_out", "w_router"):
        d[n] = d[n].rearrange("k p c -> p k c")
    d["w_merge"] = d["w_merge"].rearrange("b k p c -> p b k c")
    for n in ("w_gate", "w_up", "w_down"):
        d[n] = d[n].rearrange("e k p c -> e p k c")
    out = nc.dram_tensor("out_t", (KT, P, T), F32, kind="ExternalOutput").ap().rearrange("k p c -> p k c")
    build(nc, out=out, **d)
    r = run_bass_kernel_spmd(nc, [{f"in_{n}": arrays[n] for n in _INS}], core_ids=[0])
    return np.ascontiguousarray(r.results[0]["out_t"].reshape(D, T).T).reshape(1, T, D)
```

```python
import concourse.bass as bass
from concourse import mybir
from contextlib import ExitStack
import math

F32 = mybir.dt.float32
I32 = mybir.dt.int32
ALU = mybir.AluOpType
ACT = mybir.ActivationFunctionType
AX = mybir.AxisListType

P = 128
T = 256
D = 1024
KT = D // P
NB = T // P
C = 64
NCH = T // C
H4 = 4
E = 16
FE = 512
CAP = 64
PASSES = T // CAP
PAIRS = E // 2
ALPHA = 2.0 ** 0.25
LN_EPS, RMS_EPS, GN_EPS = 1e-5, 1e-6, 64e-5
LAM_INIT = 0.8 - 0.6 * math.exp(-0.3 * 0)
DECAY = math.exp(-0.5)
UNIT = 4096
FRONT_SLOTS, RING_SLOTS, MOE_SLOTS = 3, 6, 8

LEVELS = (1, 2, 4, 8, 16, 32, 64)
MATS = ["ident", "ones_d", "ones_dv", "pair", "pair_mean", "ones"] + [f"lev{b}" for b in LEVELS] + [
    "quad", "strict", "incl", "before"]
MAT_COLS = P * len(MATS)
DIST0 = MAT_COLS
IOTA0 = DIST0 + 3 * P
TIE0 = IOTA0 + CAP
CONST_COLS = TIE0 + 16

VECS = [("c", 8), ("b_ada", 48), ("hg_lb", 4), ("hg_norm", 1), ("da_subln", 1), ("mu", 14), ("w0", 4),
        ("a0", 4), ("k_k", 4), ("k_a", 4), ("r_k", 4), ("gn_g", 4), ("gn_b", 4), ("b_merge", 24),
        ("ln_g", 16), ("ln_b", 16)]
VEC_AT, _n = {}, 0
for _name, _w in VECS:
    VEC_AT[_name] = (_n, _w)
    _n += _w
VEC_COLS = _n


class Groups:

    def __init__(self, nc, ctx, what, banks, names):
        self.banks, self.names = banks, {n: i for i, n in enumerate(names)}
        assert len(self.names) == len(names)
        self.full = [ctx.enter_context(nc.semaphore(f"{what}_full{i}")) for i in range(len(banks))]
        self.free = [ctx.enter_context(nc.semaphore(f"{what}_read{i}")) for i in range(len(banks))]

    def at(self, name):
        i = self.names[name]
        b, k = i % len(self.banks), i // len(self.banks)
        return self.banks[b], self.full[b], self.free[b], k

    def claim(self, pe, name):
        t, full, free, k = self.at(name)
        if k:
            pe.wait_ge(free, k)
        return t, full

    def wait_full(self, eng, name):
        t, full, free, k = self.at(name)
        eng.wait_ge(full, k + 1)
        return t, free, k + 1

    def wait_read(self, eng, name):
        t, full, free, k = self.at(name)
        eng.wait_ge(free, k + 1)


def build(nc, xt, w_ada, w_in, w_merge, w_branch, w_out, w_router, w_gate, w_up, w_down,
          vecs, consts, lam_row, rbias_row, rw_w_up, rw_a_up, rw_g_up, out):
    ctx = ExitStack()
    with ctx:
        def sem(name):
            return ctx.enter_context(nc.semaphore(name))

        total = 53200
        A = ctx.enter_context(nc.sbuf_tensor("arena", [P, total], F32))
        flag_i = ctx.enter_context(nc.sbuf_tensor("overflow_flag", [1, 1], I32))
        bank = [ctx.enter_context(nc.psum_tensor(f"bank{i}", [P, 512], F32)) for i in range(8)]
        place = [0]

        def take(width):
            at = place[0]
            place[0] += width
            assert place[0] <= total, place[0]
            return A[:, at:at + width]

        def tiles(ap, n):
            return ap.rearrange("p (n t) -> p n t", n=n)

        ring = [take(UNIT) for _ in range(RING_SLOTS)]
        place[0] = FRONT_SLOTS * UNIT
        a_rw, g_rw, bonus, at_f, kt_f, rt_f = [take(1024) for _ in range(6)]
        late = place[0]
        sig_w, cs0, cs1, g_inv, kk, kk_sq = [take(1024) for _ in range(6)]
        assert place[0] == RING_SLOTS * UNIT
        cst = take(CONST_COLS)
        vec = take(VEC_COLS)
        xT = take(2048)
        ring.append(A[:, place[0]:place[0] + UNIT])
        uT = take(2048)
        o_hg, o_da = take(1024), take(1024)
        ring.append(A[:, place[0] + 3072:place[0] + 3072 + UNIT])
        rwx_a = take(14 * (T + 1))
        condb, modrow = take(256), take(512)
        gates1_at = place[0]
        gates1 = take(2048)
        o_rw = take(1024)
        work0 = place[0]
        hk, hb0, hb1, hv, hog, dk_, dv_ = [take(1024) for _ in range(7)]
        gates = [take(2048), gates1, take(2048)]
        small = take(700)
        modc = small[:, 0:48]
        sc1p, g1p, sc2p, g2p = [small[:, 48 + 8 * i:56 + 8 * i] for i in range(4)]
        condc = small[:, 80:88]
        lbv, oml = small[:, 88:92], small[:, 92:96]
        lam4 = small[:, 96:104]
        smx = small[:, 104:168]
        u2_s, u2_b, res_s, res_b = [smx[:, 8 * i:8 * i + 8] for i in range(4)]
        gend = small[:, 168:184]
        wr = small[:, 192:320]
        route = small[:, 320:700]
        lora_wa = gates[2][:, 0:512]
        lora_g = gates[2][:, 512:1024]
        lam_sb = gates[1][:, 0:256]
        lam_t = gates[1][:, 256:384]
        rwx = rwx_a.rearrange("p (n t) -> p n t", n=14)

        def M(name):
            i = MATS.index(name)
            return cst[:, i * P:(i + 1) * P]

        def V(name, i=0, n=1):
            return vec[:, VEC_AT[name][0] + i:VEC_AT[name][0] + i + n]

        def over(m, n):
            return m.unsqueeze(1).to_broadcast([P, n, m.shape[-1]])

        LN_EXP, SIGMOID = "natural_log_exp_and_others", "sigmoid_and_others"
        proj_names = (["ada0", "adaT0"] + [f"rw{i}" for i in (6, 2, 3, 0, 1)] + ["hgf0", "hgf1", "hgq0", "hgq1", "rw4", "rw5"]
                      + ["hgv0", "hgv1", "hog0", "hog1", "daq0", "daq1", "dak0", "dak1", "dav0", "dav1"]
                      + [f"gate{b}_{i}" for b in range(3) for i in range(4)]
                      + [f"br{b}_{i}" for b in range(3) for i in range(4)]
                      + [f"out{i}" for i in range(4)] + ["ln1m", "ln1v", "logit", "logitT"]
                      + [f"u2t{i}" for i in range(4)] + ["rank"])
        PJ = Groups(nc, ctx, "proj", bank[0:2], proj_names)
        lev_names = [f"a{b}_{i}" for b in (64, 32, 16, 8, 4, 0) for i in range(2)]
        lev_names.insert(2, "a128")
        HD = Groups(nc, ctx, "mix", bank[6:8], lev_names + ["hgo0", "hgo1", "hgs0", "hgs1"]
                    + [f"s{h}_{m}" for h in range(4) for m in range(2)] + [f"pT{i}" for i in range(3)]
                    + ["dao0", "dao1", "das0", "das1", "ada1", "adaT1", "ada2", "adaT2"])
        rw_names = [f"lw{i}" for i in range(2)] + [f"la{i}" for i in range(2)] + [f"lg{i}" for i in range(2)]
        rw_names += ["kk0", "kk1", "bo0", "bo1"]
        for hf in range(2):
            rw_names += [f"{hf}tok{i}" for i in range(4)]
            if hf:
                rw_names.append("0gm")
            rw_names += [f"{hf}m{m}_{hp}" for m in range(4) for hp in range(2)]
            if hf:
                rw_names.append("0gv")
            rw_names += [f"{hf}x1_{hp}" for hp in range(2)]
            for b in LEVELS[1:6]:
                rw_names += [f"{hf}y{b}_{hp}" for hp in range(2)]
                rw_names += [f"{hf}xt{b}_{hp}" for hp in range(2)]
                if b < 32:
                    rw_names += [f"{hf}xx{b}_{hp}" for hp in range(2)]
            rw_names += [f"{hf}y0_{hp}" for hp in range(2)] + [f"{hf}up_{hp}" for hp in range(2)] + [f"{hf}wat"]
            for c in range(NCH):
                if c:
                    rw_names.append(f"{hf}u{c}")
                if c < NCH - 1:
                    rw_names.append(f"{hf}s{c}")
            rw_names.append(f"{hf}o")
        rw_names += ["1gm", "1gv"]
        RW = Groups(nc, ctx, "rwkv", bank[2:6], rw_names)

        units = []
        for r in range(1):
            units += [("ada", r, q, f"ada{r}") for q in range(4)]
        in_units = [(5120, 256, "rw6"), (4096, 512, "rw3"), (3584, 512, "rw1"), (512, 512, "hgf1"), (0, 512, "hgq1"),
                    (4608, 512, "rw5"), (1024, 512, "hgv1"), (1536, 512, "hog1"), (2048, 512, "daq1"),
                    (2560, 512, "dak1"), (3072, 512, "dav1")]
        units += [("in", c0, w, last) for c0, w, last in in_units]
        for what in "g00 g01 g10 a10 a11 g11 a12 a13 g20 a20 a21 g21 a22 a23".split():
            x, y = int(what[1]), int(what[2])
            units.append(("ada", x, y, f"ada{x}") if what[0] == "a" else ("gate", x, y, f"gate{x}_{2 * y + 1}"))
        units += [("br", b, 0, f"br{b}_3") for b in range(3)]
        units += [("out", 0, i, f"out{2 * i + 1}") for i in range(2)]
        UIDX = {}
        for i, u in enumerate(units):
            UIDX[u[:3]] = i
        front_uses = [sum(1 for i in range(len(units)) if i % FRONT_SLOTS == s) for s in range(FRONT_SLOTS)]
        front_uses += [0] * (MOE_SLOTS - FRONT_SLOTS)
        slot_in = [sem(f"weights_in_slot{i}") for i in range(MOE_SLOTS)]
        ada_used = sem("ada_unit_used")

        def unit(eng, *key):
            i = UIDX[key]
            eng.wait_ge(slot_in[i % FRONT_SLOTS], 16 * (i // FRONT_SLOTS + 1))
            return ring[i % FRONT_SLOTS]

        const_in, vec_in, x_in, lora_in, row_in = sem("consts_in"), sem("vectors_in"), sem("x_in"), sem("lora_in"), sem("rows_in")
        out_done = sem("out_written")
        cond_sig, lb_exp, lb_in, ln2_sum = sem("cond_sigmoid"), sem("lower_bound_exp"), sem("lower_bound_in"), sem("ln2_sum")
        cond_ready, u_ready = sem("cond_ready"), sem("u_ready")
        modrow_ready, mod_ready = sem("modrow_ready"), sem("mod_ready")
        pad_ready, xs_ready = sem("pad_ready"), sem("shifted_ready")
        lora_act = sem("lora_act_ready")
        lora_done = sem("lora_gates_ready")
        kk_ready, kk_sqd, kk_n = sem("kk_ready"), sem("kk_squared"), sem("kk_norm_ready")
        cs_ready, dec_ready = sem("cumsum_ready"), sem("decays_ready")
        rk_ready, rwf_ready = sem("rk_ready"), sem("rwkv_factors_ready")
        sg_ready = sem("hg_sigmoids_ready")
        f_ready, logf_ready, kq_ready = sem("hg_forget_ready"), sem("hg_logf_ready"), sem("hg_k_ready")
        hcs_ready, dec_in, dec_out = sem("hg_cumsum_ready"), sem("hg_exponent_ready"), sem("hg_decay_ready")
        lev_ready = sem("hg_level_ready")
        at_ready = sem("hg_scores_ready")
        osq_ready, rms_ready = sem("out_squared"), sem("rstd_ready")
        o_ready = sem("branch_out_ready")
        s_ready, nmax_ready, e_ready, p_ready = sem("scores_ready"), sem("negmax_ready"), sem("exp_ready"), sem("probs_ready")
        lam_ready, lam_exp = sem("lambda_sums_ready"), sem("lambda_exp_ready")
        m_ready, xt_ready, nl_ready = sem("rw_matrices_ready"), sem("rw_inverse_started"), sem("rw_level_mask_ready")
        pool_ch, dq_ready, head_ready = sem("pool_chain"), sem("attention_q_ready"), sem("head_factors_ready")
        st_ready = sem("rw_state_ready")
        go_sq, go_ln, go_d = sem("gn_squared"), sem("gn_rstd"), sem("gn_centred")
        orw_copied = sem("rw_out_copied")
        merged_ready = sem("merged_ready")
        y1_ready, lnd, lnsq, lnr = sem("ln_in_ready"), sem("ln_centred"), sem("ln_squared"), sem("ln_rstd")
        u2_even, u2_odd = sem("u2_even_tiles"), sem("u2_odd_tiles")
        lg_exp_in, lg_exp = sem("router_shifted"), sem("router_exp")
        chosen_ready = sem("chosen_ready")
        flag_ready = sem("flag_ready")
        dve_ch, act_ch = sem("dve_chain"), sem("act_chain")
        x2_ready = sem("result_ready")
        v_ready, hog_sig, x_scaled, scaled_ready, fold_ready, xh_ready, res_ready = (sem("v_ready"), sem("hg_out_gate_sigmoid"), sem("x_scaled"), sem("result_scaled"), sem("norm_factors_ready"),
                                                                sem("xhat_ready"), sem("residual_ready"))

        pick_ready, pw_ready = sem("picks_ready"), sem("weighted_picks_ready")
        pw_full, pw_copied = sem("pick_transposes_done"), sem("pick_transposes_copied")
        xg_full, xg_ready = sem("gather_done"), sem("gathered_ready")
        gate_full, up_full = sem("gate_done"), sem("up_done")
        sig_ready, h_ready = sem("silu_ready"), sem("hidden_ready")
        hT_full, hT_ready = sem("hidden_transposed"), sem("hidden_t_ready")
        y_full, y_ready = sem("down_done"), sem("y_ready")
        comb_full, comb_added = sem("combine_done"), sem("combine_added")
        moe_ch = sem("moe_dve_chain")
        blk_ch = sem("moe_pass_chain")

        gate_slots = ((0, 1), (6, 7))
        comb_bank = (bank[7], bank[4])
        XG = rwx_a[:, 0:1024]
        HM = rwx_a[:, 1024:1536]
        HH = rwx_a[:, 1536:2048]
        HT_ = rwx_a[:, 2048:2560]
        SG = rwx_a[:, 2560:3072]
        place[0] = work0
        U2K = take(2048)
        PK = take(2048)
        PWT = take(2048)
        Y = take(1024)
        PW = gates[2]
        ACC = gates[0]
        LNT = gates[1]

        lvX, lvE = gates[0][:, 0:1024], gates[0][:, 1024:2048]
        lvK, lvQ = cs1, gates[2][:, 0:1024]
        scoresT = A[:, gates1_at + 1024:gates1_at + 2560]
        dq_map = [lvX, gates[2][:, 1024:2048]]
        vs = bonus
        hog_s = gates[1][:, 0:1024]
        att = A[:, late:late + 3072]
        probsT = A[:, late + 3072:late + 4608]
        daSq = A[:, late + 4608:late + 5632]
        daR = hb1
        RB = route[:, 0:E]
        rt2 = route[:, 16:20]
        scores, chosen = route[:, 20:52], route[:, 52:84]
        slot = route[:, 196:228]
        lgT = LNT[:, 256:512]

        def rw_mats(hf):
            lt = [A[:, late + i * 1024:late + (i + 1) * 1024] for i in range(6)]
            wk = [A[:, work0 + i * 1024:work0 + (i + 1) * 1024] for i in range(7)]
            NT, X, XT, YY = lt[0:4]
            NL = lt[4:6]
            AKT, RBT, RKT = wk[0:3]
            tok = [A[:, work0 + 3072 + i * 512:work0 + 3584 + i * 512] for i in range(4)]
            UP, WAT = [A[:, work0 + 5120 + i * 512:work0 + 5632 + i * 512] for i in range(2)]
            ST = rwx_a[:, 0:1024]
            Y0 = rwx_a[:, 1536:2048]
            return NT, X, XT, YY, NL, AKT, RBT, RKT, tok, Y0, UP, WAT, ST

        def kk_gn(hf):
            return rwx_a[:, 1024:1536]

        block = ctx.enter_context(nc.Block())

        @block.sync
        def _(sp):
            sp.dma_start(vec, vecs).then_inc(vec_in, 16)
            n_ada = [0]

            def load(i):
                u = units[i]
                s = i % FRONT_SLOTS
                if i >= FRONT_SLOTS:
                    prev = units[i - FRONT_SLOTS]
                    if prev[0] == "ada":
                        sp.wait_ge(ada_used, 4 * prev[1] + prev[2] + 1)
                    else:
                        t, full, free, k = PJ.at(prev[3])
                        sp.wait_ge(full, k + 1)
                if u[0] == "ada":
                    src = w_ada[:, u[2] * 2:u[2] * 2 + 2, u[1] * 2048:(u[1] + 1) * 2048]
                    dst = ring[s].rearrange("p (k c) -> p k c", k=2)
                elif u[0] == "in":
                    src = w_in[:, :, u[1]:u[1] + u[2]]
                    dst = ring[s][:, 0:KT * u[2]].rearrange("p (k c) -> p k c", k=KT)
                elif u[0] == "gate":
                    src = w_merge[:, u[1], :, u[2] * 512:(u[2] + 1) * 512]
                    dst = ring[s].rearrange("p (k c) -> p k c", k=KT)
                elif u[0] == "br":
                    src = w_branch[:, u[1] * 4:u[1] * 4 + 4, :]
                    dst = ring[s].rearrange("p (k c) -> p k c", k=4)
                else:
                    src = w_out[:, :, u[2] * 512:(u[2] + 1) * 512]
                    dst = ring[s].rearrange("p (k c) -> p k c", k=KT)
                sp.dma_start(dst, src).then_inc(slot_in[s], 16)

            sp.dma_start(cst[:, 0:P], consts[:, 0:P]).then_inc(const_in, 16)
            for i in range(3):
                load(i)
            sp.dma_start(tiles(xT, KT), xt).then_inc(x_in, 16)
            load(3)
            load(4)
            sp.dma_start(cst[:, P:CONST_COLS], consts[:, P:CONST_COLS]).then_inc(const_in, 16)
            sp.dma_start(lora_wa[0:64, :], rw_w_up).then_inc(lora_in, 16)
            sp.dma_start(lora_wa[64:128, :], rw_a_up).then_inc(lora_in, 16)
            sp.dma_start(lora_g, rw_g_up).then_inc(lora_in, 16)
            sp.dma_start(lam_sb, lam_row.to_broadcast([P, 256])).then_inc(row_in, 16)
            sp.dma_start(wr.rearrange("p (k e) -> p k e", k=KT), w_router).then_inc(row_in, 16)
            sp.dma_start(route[:, 0:E], rbias_row.to_broadcast([P, E])).then_inc(row_in, 16)
            for i in range(5, len(units)):
                load(i)

            def expert_load(s, what, e):
                w, kt = ((w_gate, KT), (w_up, KT), (w_down, FE // P))[what]
                src = w[bass.ds(e, 1), :, :, :].rearrange("e p k c -> p (e k) c")
                sp.dma_start(ring[s].rearrange("p (k c) -> p k c", k=kt), src).then_inc(slot_in[s], 16)

            def load_gates(p, odd, n):
                sp.wait_ge(gate_full, n - 1)
                for j in range(2):
                    expert_load(gate_slots[odd][j], 0, 2 * p + j)

            def load_pair(p, n):
                sp.wait_ge(up_full, n)
                for j in range(2):
                    expert_load(2 + j, 1, 2 * p + j)
                sp.wait_ge(y_full, 2 * n)
                for j in range(2):
                    expert_load(4 + j, 2, 2 * p + j)

            def two_pairs(p, n):
                load_gates(p + 1, 1, n + 1)
                load_pair(p, n)
                load_gates(p + 2, 0, n + 2)
                load_pair(p + 1, n + 1)

            def last_pairs(n):
                load_gates(PAIRS - 1, 1, n + 1)
                load_pair(PAIRS - 2, n)
                load_pair(PAIRS - 1, n + 1)

            sp.wait_ge(merged_ready, 4)
            for s in range(FRONT_SLOTS, RING_SLOTS):
                expert_load(s, s // 2, s % 2)
            nu = len(units)
            for i in range(nu - FRONT_SLOTS, nu):
                t, full, free, k = PJ.at(units[i][3])
                sp.wait_ge(full, k + 1)
                s = i % FRONT_SLOTS
                expert_load(s, s // 2, s % 2)
            t, full, free, k = PJ.at("u2t3")
            sp.wait_ge(full, k + 1)
            expert_load(6, 0, 2)
            sp.wait_ge(flag_ready, 1)
            expert_load(7, 0, 3)
            load_gates(2, 0, 2)
            load_pair(1, 1)
            with sp.Fori(1, PAIRS // 2 - 1) as h:
                two_pairs(2 * h, 2 * h)
            last_pairs(PAIRS - 2)
            over_ = sp.value_load(flag_i[0:1, 0:1], min_val=0, max_val=1)
            with sp.If(over_ > 0):
                with sp.Fori(1, PASSES) as b:
                    load_gates(0, 0, b * PAIRS)
                    with sp.Fori(0, PAIRS // 2 - 1) as h:
                        two_pairs(2 * h, b * PAIRS + 2 * h)
                    last_pairs(b * PAIRS + PAIRS - 2)
            for i in range(4):
                sp.wait_ge(x2_ready, 2 * i + 2)
                sp.dma_start(out[:, 2 * i:2 * i + 2, :], tiles(uT, KT)[:, 2 * i:2 * i + 2, :]).then_inc(out_done, 16)
            sp.wait_ge(out_done, 64)

        @block.gpsimd
        def _(pool):
            n = [0]

            def link(ins):
                n[0] += 1
                ins.then_inc(pool_ch, 1)
                pool.wait_ge(pool_ch, n[0])

            nc.gpsimd.memset(rwx[:, :, 0:1], 0.0).then_inc(pad_ready, 1)
            pool.wait_ge(const_in, 32)

            def one_head(dst, src, head, *more):
                return nc.gpsimd.tensor_scalar(dst, src, M("pair")[:, head * 64:head * 64 + 1], *more)

            pool.wait_ge(u_ready, KT)
            nc.gpsimd.tensor_scalar(xT, xT, ALPHA, None, ALU.mult).then_inc(x_scaled, 1)
            PJ.wait_read(pool, "rw4")
            PJ.wait_read(pool, "rw5")
            v3, vs3 = rwx[:, 8:12, 1:], tiles(vs, 4)
            link(nc.gpsimd.tensor_tensor(vs3, rwx[:, 8:12, 0:T], v3, ALU.subtract))
            for m in range(4):
                ins = nc.gpsimd.tensor_scalar(vs3[:, m, :], vs3[:, m, :], V("mu", 8 + m), None, ALU.mult)
                ins.then_inc(pool_ch, 1)
            n[0] += 4
            pool.wait_ge(pool_ch, n[0])
            nc.gpsimd.tensor_tensor(v3, v3, vs3, ALU.add).then_inc(v_ready, 1)
            PJ.wait_read(pool, "daq0")
            PJ.wait_read(pool, "daq1")
            HD.wait_full(pool, "a128")
            for m in range(2):
                one_head(dq_map[m], o_da, m, 0.125, ALU.mult, ALU.mult).then_inc(dq_ready, 1)
            for hf in range(2):
                NT, X, _, YY, NL = rw_mats(hf)[0:5]
                for src, dst, frees in ((a_rw, X, ((HD, "pT2"), (HD, "pT1")) if hf == 0 else ((RW, "0xt32_1"),)),
                                        (kt_f, YY, ((HD, "dao0"), (HD, "dao1")) if hf == 0 else ((RW, "0xt32_0"),))):
                    for G, g in frees:
                        G.wait_full(pool, g)
                    if hf == 0:
                        pool.wait_ge(rwf_ready, 1)
                    for hp in range(2):
                        one_head(dst[:, hp * 512:(hp + 1) * 512], src[:, hf * 512:(hf + 1) * 512], hp, None,
                                 ALU.mult).then_inc(head_ready, 1)
                pool.wait_ge(m_ready, 8 * hf + 2)
                for i, b in enumerate(LEVELS[1:6]):
                    if i >= 2:
                        RW.wait_full(pool, f"{hf}y{LEVELS[i - 1]}_1")
                    nc.gpsimd.tensor_tensor(tiles(NL[i % 2], 8), tiles(NT, 8), over(M(f"lev{b}"), 8),
                                            ALU.mult).then_inc(nl_ready, 1)
                    pool.wait_ge(nl_ready, 5 * hf + i + 1)

            x3, u3 = tiles(xT, KT), tiles(uT, KT)
            pool.wait_ge(fold_ready, 1)
            for m in range(0, KT, 2):
                pool.wait_ge(xh_ready, m // 2 + 1)
                nc.gpsimd.tensor_scalar(u3[:, m, :], x3[:, m, :], u2_s[:, m:m + 1], u2_b[:, m:m + 1], ALU.mult,
                                        ALU.add).then_inc(u2_even, 1)
            t, full, free, k = PJ.at("out3")
            pool.wait_ge(full, k + 1)
            nc.gpsimd.memset(ACC, 0.0).then_inc(comb_added, 1)
            pool.wait_ge(u2_even, KT // 2)
            pool.wait_ge(u2_odd, KT // 2)
            for m in range(KT):
                nc.gpsimd.tensor_scalar(x3[:, m, :], x3[:, m, :], res_s[:, m:m + 1], res_b[:, m:m + 1], ALU.mult,
                                        ALU.add).then_inc(res_ready, 1)

        @block.tensor
        def _(pe):
            mm = nc.tensor.matmul

            def mod_rows(r, q):
                G = HD if r else PJ
                if q == 0:
                    G.claim(pe, f"ada{r}")
                t, full, free, n = G.at(f"ada{r}")
                w = unit(pe, "ada", r, q).rearrange("p (k c) -> p k c", k=2)
                for k in range(2):
                    for g in range(4):
                        last = mm(t[32 * g:32 * g + 32, :], condb[:, (2 * q + k) * 32:(2 * q + k) * 32 + 32],
                                  w[:, k, g * 512:(g + 1) * 512], start=(q + k == 0), stop=(q == 3 and k == 1))
                if q == 3:
                    last.then_inc(full, 1)
                    G.wait_full(pe, f"ada{r}")
                    pe.nop().then_inc(ada_used, 1)
                else:
                    last.then_inc(ada_used, 1)

            def mod_cols(r):
                pe.wait_ge(modrow_ready, r + 1)
                t, full = (HD if r else PJ).claim(pe, f"adaT{r}")
                for i in range(4):
                    last = nc.tensor.transpose(t[:, i * P:(i + 1) * P], modrow[:, i * P:(i + 1) * P], M("ident"))
                last.then_inc(full, 1)

            uv = tiles(uT, KT)

            def project(name, w, m0, rhs=uv, kt=KT, first=False):
                t, full = PJ.claim(pe, name)
                for i in range(2):
                    for k in range(kt):
                        if first and i == 0:
                            pe.wait_ge(u_ready, k + 1)
                        last = mm(t[:, i * T:(i + 1) * T], w[:, k, (m0 + i) * P:(m0 + i + 1) * P], rhs[:, k, :],
                                  start=(k == 0), stop=(k == kt - 1))
                last.then_inc(full, 1)

            def project_tokens(name, w, b):
                t, full = PJ.claim(pe, name)
                for k in range(KT):
                    last = mm(t[:, :], uv[:, k, b * P:(b + 1) * P], w[:, k, :], start=(k == 0), stop=(k == KT - 1))
                last.then_inc(full, 1)

            def gate_group(b, i):
                w = unit(pe, "gate", b, i // 2).rearrange("p (k c) -> p k c", k=KT)
                project(f"gate{b}_{i}", w, 2 * (i % 2))

            pe.wait_ge(cond_ready, 1)
            for q in range(4):
                mod_rows(0, q)
            pe.wait_ge(const_in, 16)
            mod_cols(0)

            def in_group(name, c0, i, w_=512):
                w = unit(pe, "in", c0, w_)[:, 0:KT * w_].rearrange("p (k c) -> p k c", k=KT)
                project(name, w, 2 * i, first=(name == "rw6"))

            def in_tokens(name, c0, i):
                project_tokens(name, unit(pe, "in", c0, 512).rearrange("p (k c) -> p k c", k=KT), i)

            in_group("rw6", 5120, 0, 256)
            in_group("rw2", 4096, 0)
            in_group("rw3", 4096, 1)

            pe.wait_ge(lora_in, 48)
            pe.wait_ge(lora_act, 2)
            for what, lhs, rhs in (("lw", lora_wa[0:64, :], rwx[0:64, 12, 1:]), ("la", lora_wa[64:128, :], rwx[64:128, 12, 1:]),
                                   ("lg", lora_g, rwx[:, 13, 1:])):
                for i in range(2):
                    t, full = RW.claim(pe, f"{what}{i}")
                    for j in range(2):
                        m = 2 * i + j
                        last = mm(t[:, j * T:(j + 1) * T], lhs[:, m * P:(m + 1) * P], rhs, start=True, stop=True)
                    last.then_inc(full, 1)
            in_group("rw0", 3584, 0)
            in_group("rw1", 3584, 1)

            def head_sums(what):
                for i in range(2):
                    t, full = RW.claim(pe, f"{what}{i}")
                    mm(t[:, :], M("pair"), kk_sq[:, i * 512:(i + 1) * 512], start=True, stop=True).then_inc(full, 1)

            pe.wait_ge(kk_sqd, 1)
            pe.wait_ge(const_in, 32)
            head_sums("kk")
            in_group("hgf0", 512, 0)
            in_group("hgf1", 512, 1)
            in_group("hgq0", 0, 0)
            in_group("hgq1", 0, 1)
            in_group("rw4", 4608, 0)
            in_group("rw5", 4608, 1)

            q3, k3 = tiles(lvQ, 4), tiles(lvK, 4)

            def level(name, n, sk, sq, kk_=None, qq_=None):
                pe.wait_ge(lev_ready, n)
                t, full = HD.claim(pe, name)
                for h in range(H4):
                    last = mm(t[:, h * P:(h + 1) * P], (kk_ or k3)[:, h, sk:sk + P], (qq_ or q3)[:, h, sq:sq + P],
                              start=True, stop=True)
                last.then_inc(full, 1)

            in_tokens("hgv0", 1024, 0)
            in_tokens("hgv1", 1024, 1)
            level("a64_0", 1, 0, 0)
            level("a64_1", 1, P, P)
            in_group("hog0", 1536, 0)
            level("a128", 2, 0, 0, tiles(lvX, 8)[:, 0:4, :], tiles(lvX, 8)[:, 4:8, :])
            in_group("hog1", 1536, 1)
            for i, b in enumerate((32, 16, 8, 4, 0)):
                for s in range(2):
                    level(f"a{b}_{s}", 3 + i, s * P, s * P)
                if i < 4:
                    what, c0 = (("daq", 2048), ("dak", 2560))[i // 2]
                    in_group(f"{what}{i % 2}", c0, i % 2)
                if i == 0:
                    pe.wait_ge(rk_ready, 1)
                    head_sums("bo")
            in_tokens("dav0", 3072, 0)
            pe.wait_ge(at_ready, 1)
            hv3, A4 = tiles(hv, 2), scoresT.rearrange("p (a h t) -> p a h t", a=3, h=H4)
            for s in range(2):
                t, full = HD.claim(pe, f"hgo{s}")
                for h in range(H4):
                    o = t[:, h * P:(h + 1) * P]
                    if s == 0:
                        last = mm(o, hv3[:, 0, h * P:(h + 1) * P], A4[:, 0, h, :], start=True, stop=True)
                    else:
                        mm(o, hv3[:, 0, h * P:(h + 1) * P], A4[:, 2, h, :], start=True, stop=False)
                        last = mm(o, hv3[:, 1, h * P:(h + 1) * P], A4[:, 1, h, :], start=False, stop=True)
                last.then_inc(full, 1)
            in_tokens("dav1", 3072, 1)
            for s in range(2):
                pe.wait_ge(osq_ready, s + 1)
                t, full = HD.claim(pe, f"hgs{s}")
                mm(t[:, :], M("ones_dv"), lvE[:, s * 512:(s + 1) * 512], start=True, stop=True).then_inc(full, 1)

            dk3, dv3 = tiles(dk_, 4), tiles(dv_, 2)
            PJ.wait_read(pe, "dak1")
            pe.wait_ge(dq_ready, 2)
            for h in range(H4):
                for m in range(2):
                    dq = tiles(dq_map[m], 4)
                    t, full = HD.claim(pe, f"s{h}_{m}")
                    mm(t[:, 0:P], dq[:, h, 0:P], dk3[:, h, 0:P], start=True, stop=True)
                    mm(t[:, P:3 * P], dq[:, h, P:T], dk3[:, h, :], start=True, stop=True).then_inc(full, 1)
            gate_group(0, 0)
            gate_group(0, 1)
            pe.wait_ge(p_ready, 1)
            S8 = tiles(att, 8)
            for i in range(3):
                t, full = HD.claim(pe, f"pT{i}")
                for h in range(H4):
                    last = nc.tensor.transpose(t[:, h * P:(h + 1) * P], S8[:, 2 * h, i * P:(i + 1) * P], M("ident"))
                last.then_inc(full, 1)
            gate_group(0, 2)
            PJ.wait_read(pe, "dav1")
            HD.wait_read(pe, "pT2")
            HD.wait_read(pe, "pT1")
            pT3 = probsT.rearrange("p (a h t) -> p a h t", a=3, h=H4)
            for s in range(2):
                t, full = HD.claim(pe, f"dao{s}")
                for h in range(H4):
                    o = t[:, h * P:(h + 1) * P]
                    if s == 0:
                        last = mm(o, dv3[:, 0, h * P:(h + 1) * P], pT3[:, 0, h, :], start=True, stop=True)
                    else:
                        mm(o, dv3[:, 0, h * P:(h + 1) * P], pT3[:, 1, h, :], start=True, stop=False)
                        last = mm(o, dv3[:, 1, h * P:(h + 1) * P], pT3[:, 2, h, :], start=False, stop=True)
                last.then_inc(full, 1)
            af, bf, kf, rf = [tiles(x, 4) for x in (at_f, a_rw, kt_f, rt_f)]
            vf = rwx[:, 8:12, 1:]

            def rw_tokens(hf):
                for n, src in enumerate((af, bf, kf, vf)):
                    t, full = RW.claim(pe, f"{hf}tok{n}")
                    for s in range(2):
                        for jj in range(2):
                            o = (s * 2 + jj) * P
                            last = nc.tensor.transpose(t[:, o:o + P], src[:, 2 * hf + jj, s * P:(s + 1) * P], M("ident"))
                    last.then_inc(full, 1)

            pe.wait_ge(rwf_ready, 1)
            rw_tokens(0)
            gate_group(0, 3)
            for s in range(2):
                pe.wait_ge(osq_ready, 2 + s + 1)
                t, full = HD.claim(pe, f"das{s}")
                mm(t[:, :], M("ones_dv"), daSq[:, s * 512:(s + 1) * 512], start=True, stop=True).then_inc(full, 1)

            def gn_mean(hf):
                pe.wait_ge(orw_copied, hf + 1)
                t, full = RW.claim(pe, f"{hf}gm")
                mm(t[:, :], M("pair_mean"), o_rw[:, hf * 512:(hf + 1) * 512], start=True, stop=True).then_inc(full, 1)

            def gn_var(hf):
                pe.wait_ge(go_sq, hf + 1)
                t, full = RW.claim(pe, f"{hf}gv")
                mm(t[:, :], M("pair_mean"), kk_gn(hf), start=True, stop=True).then_inc(full, 1)

            gate_group(1, 0)
            for hf in range(2):
                NT, X, XT, YY, NL, AKT, RBT, RKT, tok, Y0, UP, WAT, ST = rw_mats(hf)
                j0 = 2 * hf

                def q_of(hp, jj, s):
                    return slice(((hp * 2 + jj) * 2 + s) * P, ((hp * 2 + jj) * 2 + s + 1) * P)

                if hf:
                    rw_tokens(hf)
                    gn_mean(0)
                pe.wait_ge(head_ready, 4 * hf + 4)
                for n, (lh, rh) in enumerate(((X, af), (YY, af), (X, rf), (YY, rf))):
                    for hp in range(2):
                        lh3 = tiles(lh, 4)[:, 2 * hp:2 * hp + 2, :]
                        t, full = RW.claim(pe, f"{hf}m{n}_{hp}")
                        for jj in range(2):
                            for s in range(2):
                                o = (jj * 2 + s) * P
                                last = mm(t[:, o:o + P], lh3[:, jj, s * P:(s + 1) * P], rh[:, j0 + jj, s * P:(s + 1) * P],
                                          start=True, stop=True)
                        last.then_inc(full, 1)
                if hf:
                    gn_var(0)
                    gate_group(2, 0)
                pe.wait_ge(xt_ready, hf + 1)
                for hp in range(2):
                    t, full = RW.claim(pe, f"{hf}x1_{hp}")
                    for i in range(4):
                        q = (hp * 4 + i) * P
                        last = nc.tensor.transpose(t[:, i * P:(i + 1) * P], XT[:, q:q + P], M("ident"))
                    last.then_inc(full, 1)
                for i, b in enumerate(LEVELS[1:6]):
                    pe.wait_ge(nl_ready, 5 * hf + i + 1)
                    for hp in range(2):
                        if i:
                            RW.wait_read(pe, f"{hf}xx{LEVELS[i]}_{hp}")
                        else:
                            RW.wait_read(pe, f"{hf}x1_{hp}")
                        t, full = RW.claim(pe, f"{hf}y{b}_{hp}")
                        for n in range(4):
                            q = (hp * 4 + n) * P
                            last = mm(t[:, n * P:(n + 1) * P], NL[i % 2][:, q:q + P], X[:, q:q + P], start=True, stop=True)
                        last.then_inc(full, 1)
                    if i % 2:
                        gate_group(1 + hf, 1 + i // 2)
                    else:
                        mod_rows(1 + hf, i // 2)
                    for hp in range(2):
                        RW.wait_read(pe, f"{hf}y{b}_{hp}")
                        if i:
                            RW.wait_read(pe, f"{hf}xt{LEVELS[i]}_{hp}")
                        t, full = RW.claim(pe, f"{hf}xt{b}_{hp}")
                        for n in range(4):
                            q = (hp * 4 + n) * P
                            last = mm(t[:, n * P:(n + 1) * P], YY[:, q:q + P], XT[:, q:q + P], start=True, stop=True)
                        last.then_inc(full, 1)
                    if b < 32:
                        for hp in range(2):
                            RW.wait_read(pe, f"{hf}xt{b}_{hp}")
                            t, full = RW.claim(pe, f"{hf}xx{b}_{hp}")
                            for n in range(4):
                                q = (hp * 4 + n) * P
                                last = nc.tensor.transpose(t[:, n * P:(n + 1) * P], XT[:, q:q + P], M("ident"))
                            last.then_inc(full, 1)
                mod_rows(1 + hf, 3)
                RW.wait_read(pe, f"{hf}tok3")
                pe.wait_ge(m_ready, 8 * hf + 8)
                for hp in range(2):
                    t, full = RW.claim(pe, f"{hf}y0_{hp}")
                    for jj in range(2):
                        for s in range(2):
                            o = (jj * 2 + s) * P
                            last = mm(t[:, o:o + P], AKT[:, q_of(hp, jj, s)], tok[3][:, (s * 2 + jj) * P:(s * 2 + jj + 1) * P],
                                      start=True, stop=True)
                    last.then_inc(full, 1)
                RW.wait_read(pe, f"{hf}y0_1")
                RW.wait_read(pe, f"{hf}y0_0")
                RW.wait_read(pe, f"{hf}xt32_0")
                RW.wait_read(pe, f"{hf}xt32_1")
                for hp in range(2):
                    t, full = RW.claim(pe, f"{hf}up_{hp}")
                    for jj in range(2):
                        for s in range(2):
                            o = (jj * 2 + s) * P
                            last = mm(t[:, o:o + P], XT[:, q_of(hp, jj, s)], Y0[:, o:o + P], start=True, stop=True)
                    last.then_inc(full, 1)
                t, full = RW.claim(pe, f"{hf}wat")
                for jj in range(2):
                    for s in range(2):
                        for hp in range(2):
                            o = (jj * 2 + s) * P
                            a0 = (s * 2 + jj) * P + hp * 64
                            last = mm(t[hp * 64:hp * 64 + 64, o:o + P], tok[0][:, a0:a0 + 64], XT[:, q_of(hp, jj, s)],
                                      start=True, stop=True)
                last.then_inc(full, 1)
                RW.wait_read(pe, f"{hf}wat")
                RW.wait_read(pe, f"{hf}up_0")
                RW.wait_read(pe, f"{hf}up_1")
                for c in range(NCH):
                    s, r = c // 2, slice((c % 2) * 64, (c % 2) * 64 + 64)
                    if c:
                        pe.wait_ge(st_ready, 3 * hf + c)
                        t, full = RW.claim(pe, f"{hf}u{c}")
                        for jj in range(2):
                            o = (jj * 2 + s) * P + (c % 2) * 64
                            last = mm(t[r, jj * P:(jj + 1) * P], WAT[:, o:o + 64], ST[:, (c * 2 + jj) * P:(c * 2 + jj + 1) * P],
                                      start=True, stop=True)
                        last.then_inc(full, 1)
                        RW.wait_read(pe, f"{hf}u{c}")
                    if c < NCH - 1:
                        t, full = RW.claim(pe, f"{hf}s{c}")
                        for jj in range(2):
                            a0, u0 = (s * 2 + jj) * P, (jj * 2 + s) * P
                            mm(t[:, jj * P:(jj + 1) * P], tok[1][r, a0:a0 + P], UP[r, u0:u0 + P], start=True, stop=False)
                            last = mm(t[:, jj * P:(jj + 1) * P], tok[2][r, a0:a0 + P], tok[3][r, a0:a0 + P],
                                      start=False, stop=True)
                        last.then_inc(full, 1)
                    if c == 1:
                        gate_group(1 + hf, 3)
                    elif c == 2:
                        mod_cols(1 + hf)
                t, full = RW.claim(pe, f"{hf}o")
                for jj in range(2):
                    for s in range(2):
                        o, a0 = (jj * 2 + s) * P, (s * 2 + jj) * P
                        heads = [(hp, slice(hp * 64, hp * 64 + 64), hp * 64) for hp in range(2)]
                        for hp, rr, hh in heads:
                            mm(t[rr, o:o + P], UP[:, o + hh:o + hh + 64], RBT[:, q_of(hp, jj, s)], start=True, stop=False)
                        for hp, rr, hh in heads:
                            mm(t[rr, o:o + P], tok[3][:, a0 + hh:a0 + hh + 64], RKT[:, q_of(hp, jj, s)], start=False, stop=False)
                        for c in (2 * s, 2 * s + 1):
                            for hp, rr, hh in heads:
                                s0 = (c * 2 + jj) * P + hh
                                last = mm(t[rr, o + (c % 2) * 64:o + (c % 2) * 64 + 64], ST[:, s0:s0 + 64],
                                          rf[:, j0 + jj, c * 64:(c + 1) * 64], start=False, stop=(c % 2 == 1))
                last.then_inc(full, 1)

            def branch_group(b, i):
                pe.wait_ge(o_ready, (1, 2, 4)[b])
                w = unit(pe, "br", b, 0).rearrange("p (k c) -> p k c", k=4)
                project(f"br{b}_{i}", w, 2 * i, rhs=tiles((o_hg, o_da, o_rw)[b], 4), kt=4)

            branch_group(0, 0)
            gn_mean(1)
            branch_group(0, 1)
            gn_var(1)
            for b in range(3):
                for i in range(0 if b else 2, 4):
                    branch_group(b, i)
            mg = tiles(gates[0], KT)
            pe.wait_ge(merged_ready, 4)
            for i in range(4):
                w = unit(pe, "out", 0, i // 2).rearrange("p (k c) -> p k c", k=KT)
                project(f"out{i}", w, 2 * (i % 2), rhs=mg)

            def norm_sum(t, full, src, quarter_ready, n0):
                for k in range(KT):
                    if k % 2 == 0:
                        pe.wait_ge(quarter_ready, n0 + k // 2 + 1)
                    last = mm(t[:, 0:T], M("ones_d"), tiles(src, KT)[:, k, :], start=(k == 0), stop=(k == KT - 1))
                last.then_inc(full, 1)

            norm_sum(*PJ.claim(pe, "ln1m"), xT, y1_ready, 0)
            norm_sum(*PJ.claim(pe, "ln1v"), LNT, lnsq, 0)
            pe.wait_ge(row_in, 48)
            t, full = PJ.claim(pe, "logit")
            for k in range(KT):
                pe.wait_ge((u2_even, u2_odd)[k % 2], k // 2 + 1)
                last = mm(t[0:E, 0:T], wr[:, k * E:(k + 1) * E], uv[:, k, :], start=(k == 0), stop=(k == KT - 1))
            last.then_inc(full, 1)
            PJ.wait_read(pe, "logit")
            t, full = PJ.claim(pe, "logitT")
            for s in range(2):
                last = nc.tensor.transpose(t[:, s * E:(s + 1) * E], lgT[0:E, s * P:(s + 1) * P], M("ident")[0:E, 0:E])
            last.then_inc(full, 1)
            for i in range(4):
                t, full = PJ.claim(pe, f"u2t{i}")
                for j in range(4):
                    m = (i % 2) * 4 + j
                    last = nc.tensor.transpose(t[:, j * P:(j + 1) * P], uv[:, m, (i // 2) * P:(i // 2 + 1) * P], M("ident"))
                last.then_inc(full, 1)
            pe.wait_ge(chosen_ready, 1)
            t, full = PJ.claim(pe, "rank")
            ch = chosen.rearrange("p (b e) -> p b e", b=2)
            mm(t[:, 0:E], M("before"), ch[:, 0, :], start=True, stop=True)
            mm(t[:, E:2 * E], M("before"), ch[:, 1, :], start=True, stop=False)
            mm(t[:, E:2 * E], M("ones"), ch[:, 0, :], start=False, stop=True)
            mm(t[:, 2 * E:3 * E], M("ones"), ch[:, 0, :], start=True, stop=False)
            mm(t[:, 2 * E:3 * E], M("ones"), ch[:, 1, :], start=False, stop=True).then_inc(full, 1)

            PWv = PW.rearrange("p (b n s) -> p b n s", b=2, n=PAIRS)

            def transpose_picks(b):
                pe.wait_ge(pw_ready, b + 1)
                for f in range(4):
                    for j in range(2):
                        for s in range(2):
                            o = (2 * j + s) * P
                            last = nc.tensor.transpose(bank[4 + f][:, o:o + P], PWv[:, s, 2 * f + j, :], M("ident"))
                    last.then_inc(pw_full, 1)

            def gather(p, n, half):
                if not isinstance(n, int) or n > 0:
                    pe.wait_ge(xg_ready, 2 * n)
                for j in range(4):
                    m = half * 4 + j
                    for s in range(2):
                        last = mm(bank[half][:, j * P:(j + 1) * P], U2K[:, s * D + m * P:s * D + (m + 1) * P],
                                  PK[:, bass.ds(s * 1024 + p * P, P)], start=(s == 0), stop=(s == 1))
                last.then_inc(xg_full, 1)

            xg3, hT3 = tiles(XG, KT), tiles(HT_, 4)

            def pair(p, n, h, odd, more, b):
                pe.wait_ge(xg_ready, 2 * n + 2)
                for what, bk, done_ in ((0, 2, gate_full), (1, 3, up_full)):
                    slots = (2, 3) if what else gate_slots[odd]
                    for s in slots:
                        pe.wait_ge(slot_in[s], 16 * (n if what else h) + 16 * (front_uses[s] + 1))
                    for k in range(KT):
                        for j in range(2):
                            w = ring[slots[j]].rearrange("p (k c) -> p k c", k=KT)
                            last = mm(bank[bk][j * 64:j * 64 + 64, :], xg3[:, k, j * 64:j * 64 + 64], w[:, k, :],
                                      start=(k == 0), stop=(k == KT - 1))
                    last.then_inc(done_, 1)
                if more:
                    gather(p + 1, n + 1, 0)
                pe.wait_ge(h_ready, n + 1)
                pe.wait_ge(comb_added, 4 * n + 1)
                for k in range(4):
                    last = nc.tensor.transpose(bank[4][:, k * P:(k + 1) * P], HH[:, k * P:(k + 1) * P], M("ident"))
                last.then_inc(hT_full, 1)
                if more:
                    gather(p + 1, n + 1, 1)
                pe.wait_ge(hT_ready, n + 1)
                for j in range(2):
                    pe.wait_ge(slot_in[4 + j], 16 * n + 16 * (front_uses[4 + j] + 1))
                for half in range(2):
                    for k in range(4):
                        for j in range(2):
                            w = ring[4 + j].rearrange("p (k c) -> p k c", k=4)
                            last = mm(bank[5 + half][j * 64:j * 64 + 64, :], hT3[:, k, j * 64:j * 64 + 64],
                                      w[:, k, half * 512:(half + 1) * 512], start=(k == 0), stop=(k == 3))
                    last.then_inc(y_full, 1)
                pe.wait_ge(pw_copied, 4 * b + 4)
                for i in range(4):
                    if i % 2 == 0:
                        pe.wait_ge(y_ready, 2 * n + i // 2 + 1)
                    if i >= 2:
                        pe.wait_ge(comb_added, 4 * n + i)
                    bk = comb_bank[i % 2]
                    for j in range(2):
                        m = 2 * i + j
                        last = mm(bk[:, j * T:(j + 1) * T], Y[:, m * P:(m + 1) * P], PWT[:, bass.ds(p * T, T)],
                                  start=True, stop=True)
                    last.then_inc(comb_full, 1)

            def one_pass(b, n0, h0):
                pe.wait_ge(pick_ready, 2 * b + 1)
                gather(0, n0, 0)
                gather(0, n0, 1)
                transpose_picks(b)
                with pe.Fori(0, PAIRS // 2 - 1) as h:
                    pair(2 * h, n0 + 2 * h, h0 + h, 0, True, b)
                    pair(2 * h + 1, n0 + 2 * h + 1, h0 + h, 1, True, b)
                pair(PAIRS - 2, n0 + PAIRS - 2, h0 + PAIRS // 2 - 1, 0, True, b)
                pair(PAIRS - 1, n0 + PAIRS - 1, h0 + PAIRS // 2 - 1, 1, False, b)

            PJ.wait_read(pe, "rank")
            PJ.wait_read(pe, "u2t3")
            one_pass(0, 0, 0)
            pe.wait_ge(flag_ready, 1)
            over_ = pe.value_load(flag_i[0:1, 0:1], min_val=0, max_val=1)
            with pe.If(over_ > 0):
                with pe.Fori(1, PASSES) as b:
                    one_pass(b, b * PAIRS, b * (PAIRS // 2))

            norm_sum(bank[0], ln2_sum, xT, y1_ready, 4)
            norm_sum(bank[1], ln2_sum, LNT, lnsq, 4)

        @block.scalar
        def _(act):
            n = [0]

            def link(ins):
                n[0] += 1
                ins.then_inc(act_ch, 1)
                act.wait_ge(act_ch, n[0])

            def done(ins, s, v):
                ins.then_inc(s, 1)
                act.wait_ge(s, v)

            def fn(out_, in_, f, **kw):
                return nc.scalar.activation(out_, in_, f, **kw)

            act.wait_ge(vec_in, 16)
            done(fn(condc, V("c", 0, 8), ACT.Sigmoid), cond_sig, 1)

            act.wait_ge(lb_in, 1)
            done(fn(lbv, lbv, ACT.Exp), lb_exp, 1)

            act.wait_ge(pad_ready, 1)
            def shift_in(*groups):
                for g in groups:
                    t, free, k = PJ.wait_full(act, f"rw{g}")
                    done(fn(rwx[:, 2 * g:2 * g + 2, 1:], tiles(t[:, :], 2), ACT.Copy), free, k)

            def copy_in(name, g, dst):
                t, free, k = PJ.wait_full(act, f"{name}{g}")
                done(fn(dst[:, g * 512:(g + 1) * 512], t[:, :], ACT.Copy), free, k)

            shift_in(6, 2)
            act.wait_ge(xs_ready, 1)
            done(fn(rwx[0:64, 12, 1:], rwx[0:64, 12, 1:], ACT.Tanh), lora_act, 1)
            done(fn(rwx[:, 13, 1:], rwx[:, 13, 1:], ACT.Sigmoid), lora_act, 2)
            shift_in(3)
            for what, dst, v in (("lw", sig_w, "w0"), ("la", a_rw, "a0")):
                for i in range(2):
                    t, free, k = RW.wait_full(act, f"{what}{i}")
                    for j in range(2):
                        m = 2 * i + j
                        ins = fn(dst[:, m * T:(m + 1) * T], t[:, j * T:(j + 1) * T], ACT.Sigmoid, bias=V(v, m))
                        if j:
                            done(ins, free, k)
                        else:
                            link(ins)
            act.nop().then_inc(lora_done, 1)
            for i in range(2):
                t, free, k = RW.wait_full(act, f"lg{i}")
                done(fn(g_rw[:, i * 512:(i + 1) * 512], t[:, :], ACT.Copy), free, k)
            act.wait_ge(kk_ready, 1)
            done(fn(kk_sq, kk, ACT.Square), kk_sqd, 1)
            shift_in(0, 1)
            for g in range(2):
                t, free, k = PJ.wait_full(act, f"hgf{g}")
                link(fn(hb0[:, g * 512:(g + 1) * 512], t[:, :], ACT.Sigmoid))
                done(fn(hk[:, g * 512:(g + 1) * 512], t[:, :], ACT.Sigmoid, scale=-1.0), free, k)
            for g in range(2):
                copy_in("hgq", g, o_hg)
            nc.scalar.preload_act_table_set(LN_EXP)
            act.wait_ge(cs_ready, 1)
            link(fn(g_inv, cs0, ACT.Exp, scale=DECAY))
            link(fn(cs0, cs0, ACT.Exp, scale=-DECAY))
            done(fn(sig_w, sig_w, ACT.Exp, scale=-DECAY), dec_ready, 1)
            act.wait_ge(f_ready, 1)
            done(fn(hb0, hb0, ACT.Ln), logf_ready, 1)
            shift_in(4, 5)
            act.wait_ge(kk_n, 1)
            link(fn(kk_sq, kk_sq, ACT.Ln))
            done(fn(kk_sq, kk_sq, ACT.Exp, scale=-0.5), kk_n, 2)
            act.wait_ge(lam_ready, 1)
            done(fn(lam4[:, 2:4], lam4[:, 0:2], ACT.Exp), lam_exp, 1)
            copy_in("hgv", 0, hv)
            act.wait_ge(dec_in, 1)
            link(fn(lvE, lvE, ACT.Exp, scale=-1.0))
            done(fn(lvQ, hb0, ACT.Exp), dec_out, 1)
            act.wait_ge(dec_in, 2)
            done(fn(small[:, 184:192], small[:, 184:192], ACT.Exp), dec_out, 2)
            copy_in("hgv", 1, hv)
            copy_in("hog", 0, hog)

            def level_decay(i):
                act.wait_ge(dec_in, 3 + i)
                done(fn(lvE, lvE, ACT.Exp, scale=-1.0), dec_out, 3 + i)

            level_decay(0)
            copy_in("hog", 1, hog)
            level_decay(1)
            copy_in("daq", 0, o_da)
            level_decay(2)
            copy_in("daq", 1, o_da)
            level_decay(3)
            copy_in("dak", 0, dk_)
            act.wait_ge(dec_in, 7)
            link(fn(lvQ, lvE, ACT.Exp))
            done(fn(lvE, lvE, ACT.Exp, scale=-1.0), dec_out, 7)
            copy_in("dak", 1, dk_)
            copy_in("dav", 0, dv_)
            for s in range(2):
                t, free, k = HD.wait_full(act, f"hgo{s}")
                link(fn(tiles(o_hg, 4)[:, :, s * P:(s + 1) * P], tiles(t[:, :], 4), ACT.Copy))
                done(fn(lvE[:, s * 512:(s + 1) * 512], t[:, :], ACT.Square), free, k)
                act.nop().then_inc(osq_ready, 1)
            copy_in("dav", 1, dv_)
            for s in range(2):
                t, free, k = HD.wait_full(act, f"hgs{s}")
                link(fn(lvK[:, s * 512:(s + 1) * 512], t[:, :], ACT.Ln, bias=RMS_EPS))
                done(fn(lvK[:, s * 512:(s + 1) * 512], lvK[:, s * 512:(s + 1) * 512], ACT.Exp, scale=-0.5), free, k)
            def gate_sig(b, i):
                t, free, k = PJ.wait_full(act, f"gate{b}_{i}")
                for j in range(2):
                    m = 2 * i + j
                    ins = fn(gates[b][:, m * T:(m + 1) * T], t[:, j * T:(j + 1) * T], ACT.Sigmoid, bias=V("b_merge", b * 8 + m))
                    if j:
                        done(ins, free, k)
                    else:
                        link(ins)

            S8 = tiles(att, 8)
            for i in range(8):
                if i % 2 == 0:
                    act.wait_ge(nmax_ready, i // 2 + 1)
                link(fn(S8[:, i, 0:P], S8[:, i, 0:P], ACT.Exp, bias=smx[:, i:i + 1], accum_out=smx[:, 16 + i:17 + i]))
                ins = fn(S8[:, i, P:3 * P], S8[:, i, P:3 * P], ACT.Exp, bias=smx[:, 8 + i:9 + i],
                         accum_out=smx[:, 24 + i:25 + i])
                done(ins, e_ready, i + 1)
            nc.scalar.preload_act_table_set(SIGMOID)
            done(fn(hog_s, hog, ACT.Sigmoid), hog_sig, 1)
            gate_sig(0, 0)
            gate_sig(0, 1)
            for i in range(3):
                t, free, k = HD.wait_full(act, f"pT{i}")
                done(fn(probsT[:, i * 512:(i + 1) * 512], t[:, :], ACT.Copy), free, k)
            gate_sig(0, 2)
            for s in range(2):
                t, free, k = HD.wait_full(act, f"dao{s}")
                link(fn(tiles(o_da, 4)[:, :, s * P:(s + 1) * P], tiles(t[:, :], 4), ACT.Copy))
                done(fn(daSq[:, s * 512:(s + 1) * 512], t[:, :], ACT.Square), free, k)
                act.nop().then_inc(osq_ready, 1)
            def token_copies(hf):
                for i in range(4):
                    t, free, k = RW.wait_full(act, f"{hf}tok{i}")
                    done(fn(rw_mats(hf)[8][i], t[:, :], ACT.Copy), free, k)

            def gn_square(hf):
                act.wait_ge(go_d, hf + 1)
                done(fn(kk_gn(hf), o_rw[:, hf * 512:(hf + 1) * 512], ACT.Square), go_sq, hf + 1)

            def gn_rstd(hf):
                t, free, k = RW.wait_full(act, f"{hf}gv")
                link(fn(kk_gn(hf), t[:, :], ACT.Ln, bias=GN_EPS))
                done(fn(kk_gn(hf), kk_gn(hf), ACT.Exp, scale=-0.5), free, k)

            act.wait_ge(o_ready, 1)
            token_copies(0)
            gate_sig(0, 3)
            nc.scalar.preload_act_table_set(LN_EXP)
            for s in range(2):
                t, free, k = HD.wait_full(act, f"das{s}")
                link(fn(daR[:, s * 512:(s + 1) * 512], t[:, :], ACT.Ln, bias=RMS_EPS))
                done(fn(daR[:, s * 512:(s + 1) * 512], daR[:, s * 512:(s + 1) * 512], ACT.Exp, scale=-0.5), free, k)
            nc.scalar.preload_act_table_set(SIGMOID)
            gate_sig(1, 0)
            act.wait_ge(o_ready, 2)
            for hf in range(2):
                NT, X, XT, YY, NL, AKT, RBT, RKT, tok, Y0, UP, WAT, ST = rw_mats(hf)
                if hf:
                    token_copies(hf)
                    gn_square(0)
                    nc.scalar.preload_act_table_set(LN_EXP)
                    gn_rstd(0)
                    nc.scalar.preload_act_table_set(SIGMOID)
                    gate_sig(2, 0)
                for hp in range(2):
                    t, free, k = RW.wait_full(act, f"{hf}x1_{hp}")
                    done(fn(X[:, hp * 512:(hp + 1) * 512], t[:, :], ACT.Copy), free, k)
                for i, b in enumerate(LEVELS[1:6]):
                    for hp in range(2):
                        t, free, k = RW.wait_full(act, f"{hf}y{b}_{hp}")
                        done(fn(YY[:, hp * 512:(hp + 1) * 512], t[:, :], ACT.Copy), free, k)
                    if i % 2:
                        gate_sig(1 + hf, 1 + i // 2)
                    if b < 32:
                        for hp in range(2):
                            t, free, k = RW.wait_full(act, f"{hf}xx{b}_{hp}")
                            done(fn(X[:, hp * 512:(hp + 1) * 512], t[:, :], ACT.Copy), free, k)
                for hp in range(2):
                    t, free, k = RW.wait_full(act, f"{hf}y0_{hp}")
                    done(fn(tiles(Y0, 4)[:, :, hp * 64:hp * 64 + 64], tiles(t[:, :], 4)[:, :, hp * 64:hp * 64 + 64],
                            ACT.Copy), free, k)
                for hp in range(2):
                    t, free, k = RW.wait_full(act, f"{hf}up_{hp}")
                    done(fn(tiles(UP, 4)[:, :, hp * 64:hp * 64 + 64], tiles(t[:, :], 4)[:, :, hp * 64:hp * 64 + 64],
                            ACT.Copy), free, k)
                t, free, k = RW.wait_full(act, f"{hf}wat")
                done(fn(WAT, t[:, :], ACT.Copy), free, k)
                gate_sig(1 + hf, 3)
                t, free, k = RW.wait_full(act, f"{hf}o")
                done(fn(o_rw[:, hf * 512:(hf + 1) * 512], t[:, :], ACT.Copy), free, k)
                act.nop().then_inc(orw_copied, 1)
            gn_square(1)
            nc.scalar.preload_act_table_set(LN_EXP)
            gn_rstd(1)
            def squares(n0):
                for i in range(n0, n0 + 4):
                    sl = slice((i - n0) * 512, (i - n0 + 1) * 512)
                    act.wait_ge(lnd, i + 1)
                    fn(LNT[:, sl], xT[:, sl], ACT.Square).then_inc(lnsq, 1)

            squares(0)
            t, free, k = PJ.wait_full(act, "ln1v")
            link(fn(LNT[:, 0:T], t[:, 0:T], ACT.Ln, bias=LN_EPS))
            done(fn(LNT[:, 0:T], LNT[:, 0:T], ACT.Exp, scale=-0.5), free, k)
            for m in range(1, KT, 2):
                act.wait_ge(xh_ready, m // 2 + 1)
                fn(tiles(uT, KT)[:, m, :], tiles(xT, KT)[:, m, :], ACT.Identity, bias=u2_b[:, m:m + 1],
                   scale=u2_s[:, m:m + 1]).then_inc(u2_odd, 1)
            t, free, k = PJ.wait_full(act, "logit")
            done(fn(lgT[0:E, :], t[0:E, 0:T], ACT.Copy), free, k)
            for i in range(4):
                if i == 1:
                    act.wait_ge(lg_exp_in, 1)
                    done(fn(scores, scores, ACT.Exp), lg_exp, 1)
                t, free, k = PJ.wait_full(act, f"u2t{i}")
                done(fn(U2K[:, i * 512:(i + 1) * 512], t[:, :], ACT.Copy), free, k)

            def gathered(n, half):
                act.wait_ge(xg_full, 2 * n + half + 1)
                done(fn(XG[:, half * 512:(half + 1) * 512], bank[half][:, :], ACT.Copy), xg_ready, 2 * n + half + 1)

            def pair(n, more):
                act.wait_ge(gate_full, n + 1)
                done(fn(SG, bank[2][:, :], ACT.Sigmoid), sig_ready, n + 1)
                if more:
                    act.wait_ge(up_full, n + 1)
                    gathered(n + 1, 0)
                act.wait_ge(hT_full, n + 1)
                done(fn(HT_, bank[4][:, :], ACT.Copy), hT_ready, n + 1)
                if more:
                    gathered(n + 1, 1)
                for half in range(2):
                    act.wait_ge(y_full, 2 * n + half + 1)
                    done(fn(Y[:, half * 512:(half + 1) * 512], bank[5 + half][:, :], ACT.Copy), y_ready, 2 * n + half + 1)

            def one_pass(b, n0):
                gathered(n0, 0)
                gathered(n0, 1)
                for f in range(4):
                    act.wait_ge(pw_full, 4 * b + f + 1)
                    done(fn(PWT[:, f * 512:(f + 1) * 512], bank[4 + f][:, :], ACT.Copy), pw_copied, 4 * b + f + 1)
                with act.Fori(0, PAIRS - 1) as p:
                    pair(n0 + p, True)
                pair(n0 + PAIRS - 1, False)

            nc.scalar.preload_act_table_set(SIGMOID)
            one_pass(0, 0)
            act.wait_ge(flag_ready, 1)
            over_ = act.value_load(flag_i[0:1, 0:1], min_val=0, max_val=1)
            with act.If(over_ > 0):
                with act.Fori(1, PASSES) as b:
                    one_pass(b, b * PAIRS)
            nc.scalar.preload_act_table_set(LN_EXP)
            squares(4)
            act.wait_ge(ln2_sum, 2)
            link(fn(LNT[:, 0:T], bank[1][:, 0:T], ACT.Ln, bias=LN_EPS))
            done(fn(LNT[:, 0:T], LNT[:, 0:T], ACT.Exp, scale=-0.5), lnr, 1)
            for m in range(KT):
                act.wait_ge(scaled_ready, m + 1)
                fn(tiles(uT, KT)[:, m, :], tiles(uT, KT)[:, m, :], ACT.Identity, bias=V("ln_b", 8 + m)).then_inc(x2_ready, 1)

        @block.vector
        def _(dve):
            n = [0]
            v = nc.vector

            def link(ins):
                n[0] += 1
                ins.then_inc(dve_ch, 1)
                dve.wait_ge(dve_ch, n[0])

            def done(ins, s, val):
                ins.then_inc(s, 1)
                dve.wait_ge(s, val)

            def tick(s):
                dve.nop().then_inc(s, 1)

            dve.wait_ge(vec_in, 16)
            dve.wait_ge(cond_sig, 1)
            link(v.tensor_tensor(condc, condc, V("c", 0, 8), ALU.mult))
            done(v.tensor_copy(condb.rearrange("p (k r) -> p k r", k=KT), condc.unsqueeze(2).to_broadcast([P, KT, 32])),
                 cond_ready, 1)
            done(v.tensor_tensor(lbv, V("hg_lb", 0, 4), V("hg_lb", 0, 4), ALU.subtract), lb_in, 1)
            dve.wait_ge(lb_exp, 1)
            link(v.reciprocal(oml, lbv))
            link(v.tensor_tensor(oml, oml, lbv, ALU.mult))
            link(v.tensor_tensor(lbv, oml, oml, ALU.subtract))
            link(v.tensor_scalar(oml, lbv, -1.0, 1.0, ALU.mult, ALU.add))

            def mod_row(r):
                t, free, k = (HD if r else PJ).wait_full(dve, f"ada{r}")
                done(v.tensor_copy(modrow, t[:, :]), free, k)
                tick(modrow_ready)

            def mod_cols(r):
                t, free, k = (HD if r else PJ).wait_full(dve, f"adaT{r}")
                src = t[:, :].rearrange("p (i g x) -> p g i x", i=4, g=4)[:, :, :, 0]
                dst = modc[:, 16 * r:16 * r + 16].rearrange("p (g i) -> p g i", g=4)
                done(v.tensor_tensor(dst, src, V("b_ada", 16 * r, 16).rearrange("p (g i) -> p g i", g=4), ALU.add), free, k)

            mod_row(0)
            mod_cols(0)
            link(v.tensor_scalar(sc1p, modc[:, 8:16], 1.0, None, ALU.add))
            dve.wait_ge(x_in, 16)
            x3, u3 = tiles(xT, KT), tiles(uT, KT)
            for m in range(KT):
                done(v.tensor_scalar(u3[:, m, :], x3[:, m, :], sc1p[:, m:m + 1], modc[:, m:m + 1], ALU.mult, ALU.add),
                     u_ready, m + 1)

            dve.wait_ge(row_in, 48)
            l4 = tiles(lam_sb, 4)
            link(v.tensor_tensor(tiles(lam_t, 2), l4[:, 0:4:2, :], l4[:, 1:4:2, :], ALU.mult))
            done(v.tensor_reduce(lam4[:, 0:2], tiles(lam_t, 2), axis=AX.X, op=ALU.add), lam_ready, 1)

            def shift(*ms):
                for m in ms:
                    PJ.wait_read(dve, f"rw{m // 2}")
                    link(v.tensor_tensor(hb1[:, 0:T], rwx[:, m, 0:T], rwx[:, m, 1:], ALU.subtract))
                    link(v.scalar_tensor_tensor(rwx[:, m, 1:], hb1[:, 0:T], V("mu", m), rwx[:, m, 1:], ALU.mult, ALU.add))

            shift(12, 13)
            tick(xs_ready)
            r3, k3, v3 = [rwx[:, 4 * i:4 * i + 4, 1:] for i in range(3)]
            shift(4, 5, 6, 7)
            kk3, sq3 = tiles(kk, 4), tiles(kk_sq, 4)
            for j in range(4):
                link(v.tensor_scalar(kk3[:, j, :], k3[:, j, :], V("k_k", j), None, ALU.mult))
            tick(kk_ready)

            def cumsum(a, b, save=None):
                for i in range(6):
                    d = 1 << i
                    s_, t_ = (a, b) if i % 2 == 0 else (b, a)
                    sv, tv = [x.rearrange("p (n c) -> p n c", c=C) for x in (s_, t_)]
                    link(v.tensor_tensor(tv[:, :, d:C], sv[:, :, d:C], sv[:, :, 0:C - d], ALU.add))
                    link(v.tensor_copy(tv[:, :, 0:d], sv[:, :, 0:d]))

            dve.wait_ge(lora_done, 1)
            link(v.tensor_copy(cs0, sig_w))
            cumsum(cs0, cs1)
            done(v.tensor_tensor(sig_w, cs0, sig_w, ALU.subtract), cs_ready, 1)
            for j in range(4):
                link(v.tensor_scalar(cs1[:, j * T:(j + 1) * T], a_rw[:, j * T:(j + 1) * T], -1.0, V("k_a", j), ALU.add, ALU.mult))
            link(v.scalar_tensor_tensor(k3, tiles(cs1, 4), 1.0, k3, ALU.add, ALU.mult))
            shift(0, 1, 2, 3)

            def rw_key_norm():
                for i in range(2):
                    t, free, k = RW.wait_full(dve, f"kk{i}")
                    done(v.tensor_scalar(kk_sq[:, i * 512:(i + 1) * 512], t[:, :], 1e-12, None, ALU.max), free, k)
                tick(kk_n)

            def rw_bonus_product():
                dve.wait_ge(kk_n, 2)
                link(v.tensor_tensor(kk, kk, kk_sq, ALU.mult))
                link(v.tensor_tensor(sq3, r3, k3, ALU.mult))
                for j in range(4):
                    link(v.tensor_scalar(sq3[:, j, :], sq3[:, j, :], V("r_k", j), None, ALU.mult))
                tick(rk_ready)

            def rw_a_factor():
                dve.wait_ge(dec_ready, 1)
                link(v.scalar_tensor_tensor(at_f, kk, -1.0, sig_w, ALU.mult, ALU.mult))
                link(v.tensor_tensor(a_rw, a_rw, kk, ALU.mult))

            def rw_bk_factors():
                link(v.tensor_tensor(a_rw, a_rw, g_inv, ALU.mult))
                link(v.tensor_tensor(tiles(kt_f, 4), k3, tiles(g_inv, 4), ALU.mult))

            def rw_r_factor():
                link(v.tensor_tensor(tiles(rt_f, 4), r3, tiles(cs0, 4), ALU.mult))
                link(v.tensor_copy(gend.rearrange("p (n c) -> p n c", c=1), cs0.rearrange("p (n c) -> p n c", c=C)[:, :, C - 1:C]))

            def rw_bonus():
                dve.wait_ge(v_ready, 1)
                for i in range(2):
                    t, free, k = RW.wait_full(dve, f"bo{i}")
                    done(v.tensor_tensor(tiles(bonus, 4)[:, 2 * i:2 * i + 2, :], tiles(t[:, :], 2), v3[:, 2 * i:2 * i + 2, :],
                                         ALU.mult), free, k)
                tick(rwf_ready)

            PJ.wait_read(dve, "hgf1")
            hb03, hk3 = tiles(hb0, 4), tiles(hk, 4)
            for h in range(H4):
                link(v.tensor_scalar(hb03[:, h, :], hb03[:, h, :], oml[:, h:h + 1], lbv[:, h:h + 1], ALU.mult, ALU.add))
                link(v.tensor_scalar(hk3[:, h, :], hk3[:, h, :], oml[:, h:h + 1], None, ALU.mult))
            done(v.tensor_scalar(hb0, hb0, 1e-6, None, ALU.max), f_ready, 1)
            rw_key_norm()
            dve.wait_ge(logf_ready, 1)
            cumsum(hb0, hb1)
            PJ.wait_read(dve, "hgq1")
            hcs = hb0.rearrange("p (n c) -> p n c", c=C)
            ev = lvE.rearrange("p (n c) -> p n c", c=C)
            done(v.tensor_tensor(ev, hcs, hcs[:, :, C - 1:C].to_broadcast([P, 16, C]), ALU.subtract), dec_in, 1)
            far = small[:, 184:192]
            ends = hcs[:, :, C - 1:C].rearrange("p (h c) x -> p h (c x)", h=4)[:, :, 1:3]
            link(v.tensor_copy(far.rearrange("p (h c) -> p h c", h=4), ends))
            rw_bonus_product()
            dve.wait_ge(dec_out, 1)
            tick(dec_in)
            link(v.tensor_tensor(lvK, hk, lvE, ALU.mult))
            link(v.tensor_tensor(lvQ, o_hg, lvQ, ALU.mult))
            tick(lev_ready)
            dve.wait_ge(dec_out, 2)
            K128, Q128 = tiles(lvX, 8)[:, 0:4, :], tiles(lvX, 8)[:, 4:8, :]
            f3 = far.rearrange("p (h c) -> p h c", h=4)
            Kl, Ql = tiles(lvK, 4), tiles(lvQ, 4)
            link(v.tensor_tensor(K128[:, :, 0:C], Kl[:, :, 0:C], f3[:, :, 0:1].to_broadcast([P, 4, C]), ALU.mult))
            link(v.tensor_copy(K128[:, :, C:P], Kl[:, :, C:P]))
            link(v.tensor_copy(Q128[:, :, 0:C], Ql[:, :, P:P + C]))
            link(v.tensor_tensor(Q128[:, :, C:P], Ql[:, :, P + C:T], f3[:, :, 1:2].to_broadcast([P, 4, C]), ALU.mult))
            tick(lev_ready)
            A4 = scoresT.rearrange("p (a h t) -> p a h t", a=3, h=H4)

            def take_scores(b, first):
                for s in range(2):
                    t, free, k = HD.wait_full(dve, f"a{b}_{s}")
                    m = over(M(f"lev{b}" if b else "quad"), 4)
                    if first:
                        done(v.tensor_tensor(A4[:, s], tiles(t[:, :], 4), m, ALU.mult), free, k)
                    else:
                        done(v.tensor_tensor(tiles(hb1[:, 0:512], 4), tiles(t[:, :], 4), m, ALU.mult), free, k)
                        link(v.tensor_tensor(A4[:, s], A4[:, s], tiles(hb1[:, 0:512], 4), ALU.add))

            take_scores(64, True)
            t, free, k = HD.wait_full(dve, "a128")
            done(v.tensor_copy(A4[:, 2], tiles(t[:, :], 4)), free, k)
            prev = None
            for i, b in enumerate((32, 16, 8, 4, 0)):
                w = 2 * b if b else 4
                nn = 1024 // w
                bv, e_ = [x.rearrange("p (n c) -> p n c", c=w) for x in (hb0, lvE)]
                if not b:
                    take_scores(prev, False)
                if b:
                    ref = bv[:, :, b - 1:b].to_broadcast([P, nn, b])
                    link(v.tensor_tensor(e_[:, :, 0:b], bv[:, :, 0:b], ref, ALU.subtract))
                    done(v.tensor_tensor(e_[:, :, b:w], ref, bv[:, :, b:w], ALU.subtract), dec_in, 3 + i)
                else:
                    ref = bv[:, :, 1:2].to_broadcast([P, nn, w])
                    done(v.tensor_tensor(e_, bv, ref, ALU.subtract), dec_in, 3 + i)
                if i and b:
                    take_scores(prev, False)
                prev = b
                if i == 0:
                    rw_a_factor()
                elif i == 1:
                    rw_bk_factors()
                elif i == 2:
                    rw_r_factor()
                elif i == 3:
                    rw_bonus()
                dve.wait_ge(dec_out, 3 + i)
                link(v.tensor_tensor(lvK, hk, lvE, ALU.mult))
                link(v.tensor_tensor(lvQ, o_hg, lvE if b else lvQ, ALU.mult))
                tick(lev_ready)
            take_scores(0, False)
            PJ.wait_read(dve, "hgv1")
            tick(at_ready)
            HD.wait_read(dve, "hgo1")
            HD.wait_read(dve, "hgo0")
            for s in range(2):
                HD.wait_read(dve, f"hgs{s}")
                o = tiles(o_hg, 4)[:, :, s * P:(s + 1) * P]
                link(v.scalar_tensor_tensor(o, o, V("hg_norm"), tiles(lvK[:, s * 512:(s + 1) * 512], 4), ALU.mult, ALU.mult))

            S8 = tiles(att, 8)
            dist = cst[:, DIST0:DIST0 + 3 * P]
            for h in range(H4):
                slope = 2.0 ** (-8.0 * (h + 1) / H4)
                for m in range(2):
                    t, free, k = HD.wait_full(dve, f"s{h}_{m}")
                    done(v.scalar_tensor_tensor(S8[:, 2 * h + m, :], dist, -slope, t[:, 0:3 * P], ALU.mult, ALU.add), free, k)
                for (c0, c1, o) in ((0, P, 0), (P, 3 * P, 8)):
                    link(v.tensor_reduce(smx[:, 32 + o + 2 * h:34 + o + 2 * h], S8[:, 2 * h:2 * h + 2, c0:c1], axis=AX.X, op=ALU.max))
                    link(v.tensor_scalar(smx[:, o + 2 * h:o + 2 * h + 2], smx[:, 32 + o + 2 * h:34 + o + 2 * h], -1.0, None, ALU.mult))
                tick(nmax_ready)
            dve.wait_ge(lam_exp, 1)
            link(v.tensor_tensor(lam4[:, 4:5], lam4[:, 2:3], lam4[:, 3:4], ALU.subtract))
            link(v.tensor_scalar(lam4[:, 5:6], lam4[:, 4:5], LAM_INIT, -1.0, ALU.add, ALU.mult))
            sums, recips = [smx[:, c:c + 16].rearrange("p (o i) -> p o i", o=2) for c in (16, 48)]
            for h in range(H4):
                dve.wait_ge(e_ready, 2 * h + 2)
                link(v.reciprocal(recips[:, :, 2 * h:2 * h + 2], sums[:, :, 2 * h:2 * h + 2]))
                link(v.tensor_scalar(recips[:, :, 2 * h + 1], recips[:, :, 2 * h + 1], lam4[:, 5:6], None, ALU.mult))
                for (c0, c1, o) in ((0, P, 48), (P, 3 * P, 56)):
                    link(v.tensor_scalar(S8[:, 2 * h, c0:c1], S8[:, 2 * h, c0:c1], smx[:, o + 2 * h:o + 2 * h + 1], None, ALU.mult))
                    link(v.scalar_tensor_tensor(S8[:, 2 * h, c0:c1], S8[:, 2 * h + 1, c0:c1], smx[:, o + 2 * h + 1:o + 2 * h + 2],
                                                S8[:, 2 * h, c0:c1], ALU.mult, ALU.add))
            tick(p_ready)
            dve.wait_ge(hog_sig, 1)
            link(v.tensor_tensor(hog, hog, hog_s, ALU.mult))
            link(v.tensor_tensor(o_hg, o_hg, hog, ALU.mult))
            tick(o_ready)
            link(v.tensor_scalar(lam4[:, 6:7], V("da_subln"), 1.0 - LAM_INIT, None, ALU.mult))
            HD.wait_read(dve, "dao1")
            HD.wait_read(dve, "dao0")
            for s in range(2):
                HD.wait_read(dve, f"das{s}")
                o = tiles(o_da, 4)[:, :, s * P:(s + 1) * P]
                link(v.scalar_tensor_tensor(o, o, lam4[:, 6:7], tiles(daR[:, s * 512:(s + 1) * 512], 4), ALU.mult, ALU.mult))
            tick(o_ready)

            def gn_centre(hf):
                dve.wait_ge(orw_copied, hf + 1)
                o = o_rw[:, hf * 512:(hf + 1) * 512]
                t, free, k = RW.wait_full(dve, f"{hf}gm")
                done(v.tensor_tensor(o, o, t[:, :], ALU.subtract), free, k)
                tick(go_d)

            def gn_finish(hf):
                o = o_rw[:, hf * 512:(hf + 1) * 512]
                RW.wait_read(dve, f"{hf}gv")
                link(v.tensor_tensor(o, o, kk_gn(hf), ALU.mult))
                for jj in range(2):
                    j = 2 * hf + jj
                    link(v.tensor_scalar(o_rw[:, j * T:(j + 1) * T], o_rw[:, j * T:(j + 1) * T], V("gn_g", j), V("gn_b", j),
                                         ALU.mult, ALU.add))
                link(v.tensor_tensor(o, o, bonus[:, hf * 512:(hf + 1) * 512], ALU.add))
                link(v.tensor_tensor(o, o, g_rw[:, hf * 512:(hf + 1) * 512], ALU.mult))
                tick(o_ready)

            for hf in range(2):
                NT, X, XT, YY, NL, AKT, RBT, RKT, tok, Y0, UP, WAT, ST = rw_mats(hf)
                if hf:
                    gn_centre(0)
                for i, (dst, mask) in enumerate(((NT, "strict"), (AKT, "strict"), (RBT, "incl"), (RKT, "incl"))):
                    if i == 1:
                        link(v.tensor_tensor(tiles(XT, 8), tiles(NT, 8), over(M("lev1"), 8), ALU.mult))
                        done(v.tensor_tensor(tiles(XT, 8), tiles(XT, 8), over(M("ident"), 8), ALU.add), xt_ready, hf + 1)
                    for hp in range(2):
                        t, free, k = RW.wait_full(dve, f"{hf}m{i}_{hp}")
                        done(v.tensor_tensor(tiles(dst[:, hp * 512:(hp + 1) * 512], 4), tiles(t[:, :], 4), over(M(mask), 4),
                                             ALU.mult), free, k)
                        tick(m_ready)
                link(v.memset(ST[:, 0:2 * P], 0.0))
                for i, b in enumerate(LEVELS[1:6]):
                    for hp in range(2):
                        t, free, k = RW.wait_full(dve, f"{hf}xt{b}_{hp}")
                        d_ = XT[:, hp * 512:(hp + 1) * 512]
                        done(v.tensor_tensor(d_, d_, t[:, :], ALU.add), free, k)
                if hf:
                    gn_finish(0)
                mod_row(1 + hf)
                RW.wait_read(dve, f"{hf}up_0")
                RW.wait_read(dve, f"{hf}up_1")
                U4 = UP.rearrange("p (j s d) -> p j s d", j=2, s=2)
                for c in range(NCH):
                    s, r = c // 2, slice((c % 2) * 64, (c % 2) * 64 + 64)
                    if c:
                        t, free, k = RW.wait_full(dve, f"{hf}u{c}")
                        done(v.tensor_tensor(U4[r, :, s, :], U4[r, :, s, :], tiles(t[:, 0:256], 2)[r], ALU.add), free, k)
                    if c < NCH - 1:
                        t, free, k = RW.wait_full(dve, f"{hf}s{c}")
                        nxt = tiles(ST[:, (c + 1) * 256:(c + 2) * 256], 2)
                        done(v.tensor_tensor(nxt, tiles(t[:, 0:256], 2), over(M("pair"), 2), ALU.mult), free, k)
                        link(v.tensor_tensor(nxt, nxt, tiles(ST[:, c * 256:(c + 1) * 256], 2), ALU.add))
                        for jj in range(2):
                            g = (2 * hf + jj) * 4 + c
                            ins = v.tensor_scalar(nxt[:, jj, :], nxt[:, jj, :], gend[:, g:g + 1], None, ALU.mult)
                            if jj:
                                done(ins, st_ready, 3 * hf + c + 1)
                            else:
                                link(ins)
                mod_cols(1 + hf)

            link(v.tensor_scalar(g1p, modc[:, 16:24], 1.0, None, ALU.add))
            link(v.tensor_scalar(sc2p, modc[:, 32:40], 1.0, None, ALU.add))
            link(v.tensor_scalar(g2p, modc[:, 40:48], 1.0, None, ALU.add))
            link(v.tensor_tensor(u2_s, V("ln_g", 0, 8), sc2p, ALU.mult))
            link(v.tensor_tensor(u2_b, V("ln_b", 0, 8), sc2p, ALU.mult))
            link(v.tensor_tensor(u2_b, u2_b, modc[:, 24:32], ALU.add))
            link(v.tensor_scalar(res_s, V("ln_g", 0, 8), ALPHA, None, ALU.mult))
            done(v.tensor_scalar(res_b, V("ln_b", 0, 8), ALPHA, None, ALU.mult), fold_ready, 1)

            for b in range(3):
                for i in range(4):
                    PJ.wait_read(dve, f"gate{b}_{i}")
                    t, free, k = PJ.wait_full(dve, f"br{b}_{i}")
                    g = gates[b][:, i * 512:(i + 1) * 512]
                    done(v.tensor_tensor(g, g, t[:, :], ALU.mult), free, k)
                    if b:
                        m_ = gates[0][:, i * 512:(i + 1) * 512]
                        link(v.tensor_tensor(m_, m_, g, ALU.add))
                    if b == 2:
                        tick(merged_ready)
                    if b == 0 and i == 0:
                        gn_centre(1)
                    elif b == 0 and i == 1:
                        gn_finish(1)
            dve.wait_ge(x_scaled, 1)
            for i in range(4):
                t, free, k = PJ.wait_full(dve, f"out{i}")
                for j in range(2):
                    m = 2 * i + j
                    ins = v.scalar_tensor_tensor(x3[:, m, :], t[:, j * T:(j + 1) * T], g1p[:, m:m + 1], x3[:, m, :],
                                                 ALU.mult, ALU.add)
                    if j:
                        done(ins, free, k)
                    else:
                        link(ins)
                tick(y1_ready)

            def centre(mean, n0):
                for i in range(4):
                    q = x3[:, 2 * i:2 * i + 2, :]
                    done(v.tensor_tensor(q, q, over(mean, 2), ALU.subtract), lnd, n0 + i + 1)

            t, free, k = PJ.wait_full(dve, "ln1m")
            centre(t[:, 0:T], 0)
            dve.nop().then_inc(free, 1)
            PJ.wait_read(dve, "ln1v")
            for i in range(4):
                q = x3[:, 2 * i:2 * i + 2, :]
                done(v.tensor_tensor(q, q, over(LNT[:, 0:T], 2), ALU.mult), xh_ready, i + 1)

            s3 = scores.rearrange("p (b e) -> p b e", b=2)
            t, free, k = PJ.wait_full(dve, "logitT")
            done(v.tensor_copy(scores, t[:, 0:2 * E]), free, k)
            link(v.tensor_reduce(rt2[:, 0:2], s3, axis=AX.X, op=ALU.max))
            done(v.tensor_tensor(s3, s3, rt2[:, 0:2].unsqueeze(2).to_broadcast([P, 2, E]), ALU.subtract), lg_exp_in, 1)
            dve.wait_ge(lg_exp, 1)
            link(v.tensor_reduce(rt2[:, 0:2], s3, axis=AX.X, op=ALU.add))
            link(v.reciprocal(rt2[:, 2:4], rt2[:, 0:2]))
            link(v.tensor_tensor(s3, s3, rt2[:, 2:4].unsqueeze(2).to_broadcast([P, 2, E]), ALU.mult))
            sel = route[:, 84:116]
            link(v.tensor_tensor(sel.rearrange("p (b e) -> p b e", b=2), s3, RB.unsqueeze(1).to_broadcast([P, 2, E]), ALU.add))
            s4 = sel.rearrange("p (n j) -> p n j", j=4)
            big, big2 = LNT[:, 0:128], LNT[:, 128:256]
            tie = cst[:, TIE0:TIE0 + 16].rearrange("p (j i) -> p j i", j=4)

            def ranks(vals, nn, out_):
                w = nn * 16
                b3 = big[:, 0:w].rearrange("p (n j i) -> p n j i", j=4, i=4)
                c3 = big2[:, 0:w].rearrange("p (n j i) -> p n j i", j=4, i=4)
                vi = vals.unsqueeze(2).to_broadcast([P, nn, 4, 4])
                vj = vals.unsqueeze(3).to_broadcast([P, nn, 4, 4])
                link(v.tensor_tensor(b3, vi, vj, ALU.is_gt))
                link(v.tensor_tensor(c3, vi, vj, ALU.is_equal))
                link(v.tensor_tensor(c3, c3, tie.unsqueeze(1).to_broadcast([P, nn, 4, 4]), ALU.mult))
                link(v.tensor_tensor(b3, b3, c3, ALU.add))
                link(v.tensor_reduce(out_, b3, axis=AX.X, op=ALU.add))

            rk = route[:, 116:148]
            ranks(s4, 8, rk.rearrange("p (n j) -> p n j", j=4))
            top2 = route[:, 148:180]
            link(v.tensor_scalar(top2, rk, 2.0, None, ALU.is_lt))
            gs = route[:, 180:188]
            link(v.tensor_tensor(rk, top2, sel, ALU.mult))
            link(v.tensor_reduce(gs, rk.rearrange("p (n j) -> p n j", j=4), axis=AX.X, op=ALU.add))
            grk = route[:, 188:196]
            ranks(gs.rearrange("p (n j) -> p n j", j=4), 2, grk.rearrange("p (n j) -> p n j", j=4))
            link(v.tensor_scalar(grk, grk, 1.0, None, ALU.is_lt))
            done(v.tensor_tensor(chosen.rearrange("p (n j) -> p n j", j=4), top2.rearrange("p (n j) -> p n j", j=4),
                                 grk.unsqueeze(2).to_broadcast([P, 8, 4]), ALU.mult), chosen_ready, 1)
            link(v.tensor_tensor(scores, scores, chosen, ALU.mult))
            link(v.tensor_reduce(rt2[:, 0:2], s3, axis=AX.X, op=ALU.add))
            link(v.reciprocal(rt2[:, 2:4], rt2[:, 0:2]))
            link(v.tensor_tensor(s3, s3, rt2[:, 2:4].unsqueeze(2).to_broadcast([P, 2, E]), ALU.mult))
            t, free, k = PJ.wait_full(dve, "rank")
            link(v.tensor_reduce(rt2[:, 0:1], t[:, 2 * E:3 * E], axis=AX.X, op=ALU.max))
            done(v.scalar_tensor_tensor(slot, t[:, 0:2 * E], 1.0, chosen, ALU.add, ALU.mult), free, k)
            link(v.tensor_scalar(slot, slot, -1.0, None, ALU.add))
            done(v.tensor_scalar(flag_i[0:1, 0:1], rt2[0:1, 0:1], float(CAP), None, ALU.is_gt), flag_ready, 1)

            iota = cst[:, IOTA0:IOTA0 + CAP]

            def picks(b):
                step = [0]

                def chain(ins):
                    step[0] += 1
                    done(ins, blk_ch, 7 * b + step[0])

                wt, sl = [[x[:, s * E:(s + 1) * E] for s in range(2)] for x in (scores, slot)]
                pk, pw = [[x[:, s * 1024:(s + 1) * 1024].rearrange("p (e j) -> p e j", e=E) for s in range(2)] for x in (PK, PW)]
                for e0, e1 in ((0, 2), (2, E)):
                    for s in range(2):
                        chain(v.tensor_tensor(pk[s][:, e0:e1], over(iota, e1 - e0),
                                              sl[s][:, e0:e1].unsqueeze(2).to_broadcast([P, e1 - e0, CAP]), ALU.is_equal))
                    tick(pick_ready)
                for s in range(2):
                    chain(v.tensor_tensor(pw[s], pk[s], wt[s].unsqueeze(2).to_broadcast([P, E, CAP]), ALU.mult))
                chain(v.tensor_scalar(slot, slot, -float(CAP), None, ALU.add))
                tick(pw_ready)

            def pair(n_):
                dve.wait_ge(sig_ready, n_ + 1)
                done(v.tensor_tensor(HM, bank[2][:, :], SG, ALU.mult), moe_ch, n_ + 1)
                dve.wait_ge(up_full, n_ + 1)
                done(v.tensor_tensor(HH, bank[3][:, :], HM, ALU.mult), h_ready, n_ + 1)
                for i in range(4):
                    dve.wait_ge(comb_full, 4 * n_ + i + 1)
                    a_ = ACC[:, i * 512:(i + 1) * 512]
                    bk = comb_bank[i % 2]
                    done(v.tensor_tensor(a_, a_, bk[:, :], ALU.add), comb_added, 4 * n_ + i + 2)

            def one_pass(b, n0):
                picks(b)
                with dve.Fori(0, PAIRS) as p:
                    pair(n0 + p)

            one_pass(0, 0)
            over_ = dve.value_load(flag_i[0:1, 0:1], min_val=0, max_val=1)
            with dve.If(over_ > 0):
                with dve.Fori(1, PASSES) as b:
                    one_pass(b, b * PAIRS)

            a3 = tiles(ACC, KT)
            dve.wait_ge(res_ready, KT)
            for m in range(KT):
                ins = v.scalar_tensor_tensor(x3[:, m, :], a3[:, m, :], g2p[:, m:m + 1], x3[:, m, :], ALU.mult, ALU.add)
                if m % 2:
                    done(ins, y1_ready, 4 + m // 2 + 1)
                else:
                    link(ins)
            dve.wait_ge(ln2_sum, 1)
            centre(bank[0][:, 0:T], 4)
            dve.wait_ge(lnr, 1)
            for m in range(KT):
                done(v.scalar_tensor_tensor(u3[:, m, :], x3[:, m, :], V("ln_g", 8 + m), LNT[:, 0:T], ALU.mult, ALU.mult),
                     scaled_ready, m + 1)


_INS = ["xt", "w_ada", "w_in", "w_merge", "w_branch", "w_out", "w_router", "w_gate", "w_up", "w_down",
        "vecs", "consts", "lam_row", "rbias_row", "rw_w_up", "rw_a_up", "rw_g_up"]


def _constants():
    import numpy as np
    i = np.arange(P)
    s, t = i[:, None], i[None, :]
    same = lambda w: (s // w) == (t // w)
    m = {"ident": s == t, "ones_d": np.full((P, P), 1.0 / D), "ones_dv": np.full((P, P), 1.0 / P),
         "pair": same(64), "pair_mean": same(64) / 64.0, "ones": np.ones((P, P)),
         "quad": same(4) & (s <= t), "strict": same(C) & (s < t), "incl": same(C) & (s <= t), "before": s < t}
    for b in LEVELS:
        m[f"lev{b}"] = same(2 * b) & (s % (2 * b) < b) & (t % (2 * b) >= b)
    own = np.where(s >= t, s - t, 1e33)
    dist = np.concatenate([own, s - t + P, own], 1)
    iota = np.broadcast_to(np.arange(CAP), (P, CAP))
    j4 = np.arange(4)
    tie = np.broadcast_to((j4[None, :] < j4[:, None]).reshape(1, 16), (P, 16))
    return np.concatenate([np.asarray(m[n], np.float32) for n in MATS] + [dist, iota, tie], 1).astype(np.float32)


def kernel(**inputs):
    import numpy as np
    import concourse.bacc as bacc
    from concourse.bass_utils import run_bass_kernel_spmd

    a = {k: np.asarray(x) for k, x in inputs.items()}

    def by_channel(w):
        return w.reshape(-1, P, w.shape[-1])

    cols = lambda x: x.reshape(-1, P).T
    parts = {"c": a["c"], "b_ada": a["b_ada"], "hg_lb": a["hg_lb_logits"], "hg_norm": a["hg_norm_g"],
             "da_subln": a["da_subln_g"], "mu": a["rw_mu"], "w0": a["rw_w0"], "a0": a["rw_a0"], "k_k": a["rw_k_k"],
             "k_a": a["rw_k_a"], "r_k": a["rw_r_k"], "gn_g": a["rw_gn_g"], "gn_b": a["rw_gn_b"],
             "b_merge": a["b_merge"], "ln_g": a["ln_g"], "ln_b": a["ln_b"]}
    arrays = {
        "xt": by_channel(a["x"][0].T), "w_ada": by_channel(a["w_ada"][0]), "w_in": by_channel(a["w_in"][0]),
        "w_merge": a["w_merge"][0].reshape(3, KT, P, D), "w_branch": by_channel(a["w_branch"][0]),
        "w_out": by_channel(a["w_out"][0]), "w_router": by_channel(a["w_router"]),
        "w_gate": a["w_exp_gate"][0].reshape(E, KT, P, FE), "w_up": a["w_exp_up"][0].reshape(E, KT, P, FE),
        "w_down": a["w_exp_down"][0].reshape(E, FE // P, P, D),
        "vecs": np.concatenate([cols(parts[n]) for n, _ in VECS], 1), "consts": _constants(),
        "lam_row": a["da_lambda"].reshape(1, 256), "rbias_row": a["router_bias"].reshape(1, E),
        "rw_w_up": a["rw_w_up"][0], "rw_a_up": a["rw_a_up"][0], "rw_g_up": a["rw_g_up"][0],
    }
    arrays = {k: np.ascontiguousarray(x) for k, x in arrays.items()}
    nc = bacc.Bacc("TRN2", target_bir_lowering=False, num_devices=1)
    d = {n: nc.dram_tensor(f"in_{n}", arrays[n].shape, mybir.dt.from_np(arrays[n].dtype), kind="ExternalInput").ap()
         for n in _INS}
    for n in ("xt", "w_ada", "w_in", "w_branch", "w_out", "w_router"):
        d[n] = d[n].rearrange("k p c -> p k c")
    d["w_merge"] = d["w_merge"].rearrange("b k p c -> p b k c")
    for n in ("w_gate", "w_up", "w_down"):
        d[n] = d[n].rearrange("e k p c -> e p k c")
    out = nc.dram_tensor("out_t", (KT, P, T), F32, kind="ExternalOutput").ap().rearrange("k p c -> p k c")
    build(nc, out=out, **d)
    r = run_bass_kernel_spmd(nc, [{f"in_{n}": arrays[n] for n in _INS}], core_ids=[0])
    return np.ascontiguousarray(r.results[0]["out_t"].reshape(D, T).T).reshape(1, T, D)
```

```python
import concourse.bass as bass
from concourse import mybir
from contextlib import ExitStack
import math

F32 = mybir.dt.float32
I32, BF16 = mybir.dt.int32, mybir.dt.bfloat16
ALU = mybir.AluOpType
ACT = mybir.ActivationFunctionType
AX = mybir.AxisListType

P = 128
T = 256
D = 1024
KT = D // P
C = 64
NCH = T // C
H4 = 4
E = 16
FE = 512
CAP = 64
PASSES = T // CAP
PAIRS = E // 2
ALPHA = 2.0 ** 0.25
LN_EPS, RMS_EPS, GN_EPS = 1e-5, 1e-6, 64e-5
LAM_INIT = 0.8 - 0.6 * math.exp(-0.3 * 0)
DECAY = math.exp(-0.5)
UNIT = 4096
FRONT_SLOTS, RING_SLOTS, MOE_SLOTS = 3, 6, 10

LEVELS = (1, 2, 4, 8, 16, 32, 64)
KEPT_MATS = ["ident", "ones_d", "ones", "before"]
MIX_MATS = ["ones_dv", "pair", "pair_mean"] + [f"lev{b}" for b in LEVELS] + ["quad", "strict", "incl"]
IOTA0 = P * len(KEPT_MATS)
TIE0 = IOTA0 + CAP
KEPT_COLS = TIE0 + 16
DIST0 = P * len(MIX_MATS)
MIX_COLS = DIST0 + 3 * P
CONST_COLS = KEPT_COLS + MIX_COLS

VECS = [("c", 8), ("b_ada", 48), ("hg_lb", 4), ("hg_norm", 1), ("da_subln", 1), ("mu", 14), ("w0", 4),
        ("a0", 4), ("k_k", 4), ("k_a", 4), ("r_k", 4), ("gn_g", 4), ("gn_b", 4), ("b_merge", 24),
        ("ln_g", 16), ("ln_b", 16)]
VEC_AT, _n = {}, 0
for _name, _w in VECS:
    VEC_AT[_name] = (_n, _w)
    _n += _w
VEC_COLS = _n


class Groups:

    def __init__(self, nc, ctx, what, banks, names):
        self.banks, self.names = banks, {n: i for i, n in enumerate(names)}
        assert len(self.names) == len(names)
        self.full = [ctx.enter_context(nc.semaphore(f"{what}_full{i}")) for i in range(len(banks))]
        self.free = [ctx.enter_context(nc.semaphore(f"{what}_read{i}")) for i in range(len(banks))]

    def at(self, name):
        i = self.names[name]
        b, k = i % len(self.banks), i // len(self.banks)
        return self.banks[b], self.full[b], self.free[b], k

    def claim(self, pe, name):
        t, full, free, k = self.at(name)
        if k:
            pe.wait_ge(free, k)
        return t, full

    def wait_full(self, eng, name):
        t, full, free, k = self.at(name)
        eng.wait_ge(full, k + 1)
        return t, free, k + 1

    def wait_read(self, eng, name):
        t, full, free, k = self.at(name)
        eng.wait_ge(free, k + 1)


def build(nc, xt, w_ada, w_in, w_merge, w_branch, w_out, w_router, w_gate, w_up, w_down,
          vecs, consts, lam_row, rbias_row, rw_w_up, rw_a_up, rw_g_up, out):
    ctx = ExitStack()
    with ctx:
        def sem(name):
            return ctx.enter_context(nc.semaphore(name))

        total = 53200
        A = ctx.enter_context(nc.sbuf_tensor("arena", [P, total], F32))
        flag_i = ctx.enter_context(nc.sbuf_tensor("overflow_flag", [1, 1], I32))
        bank = [ctx.enter_context(nc.psum_tensor(f"bank{i}", [P, 512], F32)) for i in range(8)]
        place = [0]

        def take(width):
            at = place[0]
            place[0] += width
            assert place[0] <= total, place[0]
            return A[:, at:at + width]

        def tiles(ap, n):
            return ap.rearrange("p (n t) -> p n t", n=n)

        ring = [take(UNIT) for _ in range(RING_SLOTS)]
        place[0] = FRONT_SLOTS * UNIT
        a_rw, g_rw, bonus, at_f, kt_f, rt_f = [take(1024) for _ in range(6)]
        late = place[0]
        sig_w, cs0, cs1, g_inv, kk, kk_sq = [take(1024) for _ in range(6)]
        assert place[0] == RING_SLOTS * UNIT
        cst = take(KEPT_COLS)
        vec = take(VEC_COLS)
        xT = take(2048)
        ring.append(A[:, place[0]:place[0] + UNIT])
        uT = take(2048)
        o_hg, o_da = take(1024), take(1024)
        ring.append(A[:, place[0] + 3072:place[0] + 3072 + UNIT])
        rwx_a = take(14 * (T + 1))
        condb, modrow = take(256), take(512)
        gates1_at = place[0]
        gates1 = take(2048)
        o_rw = take(1024)
        work0 = place[0]
        hk, hb0, hb1, hv, hog, dk_, dv_ = [take(1024) for _ in range(7)]
        gates0 = take(2048)
        ring.append(A[:, place[0]:place[0] + UNIT])
        gates = [gates0, gates1, take(2048)]
        mix_cst = take(MIX_COLS)
        ring.append(A[:, work0 + 2048:work0 + 2048 + UNIT])
        small = take(700)
        modc = small[:, 0:48]
        sc1p, g1p, sc2p, g2p = [small[:, 48 + 8 * i:56 + 8 * i] for i in range(4)]
        condc = small[:, 80:88]
        lbv, oml = small[:, 88:92], small[:, 92:96]
        lam4 = small[:, 96:104]
        smx = small[:, 104:168]
        u2_s, u2_b, res_s, res_b = [smx[:, 8 * i:8 * i + 8] for i in range(4)]
        gend = small[:, 168:184]
        wr = small[:, 192:320]
        route = small[:, 320:700]
        lora_wa = gates[2][:, 0:512]
        lora_g = gates[2][:, 512:1024]
        lam_sb = gates[1][:, 0:256]
        lam_t = gates[1][:, 256:384]
        rwx = rwx_a.rearrange("p (n t) -> p n t", n=14)

        def M(name):
            mats, at = (KEPT_MATS, cst) if name in KEPT_MATS else (MIX_MATS, mix_cst)
            i = mats.index(name)
            return at[:, i * P:(i + 1) * P]

        def V(name, i=0, n=1):
            return vec[:, VEC_AT[name][0] + i:VEC_AT[name][0] + i + n]

        def over(m, n):
            return m.unsqueeze(1).to_broadcast([P, n, m.shape[-1]])

        LN_EXP, SIGMOID = "natural_log_exp_and_others", "sigmoid_and_others"
        proj_names = (["ada0", "adaT0"] + [f"rw{i}" for i in (6, 2, 3, 0, 1)] + ["hgf0", "hgf1", "hgq0", "hgq1", "rw4", "rw5"]
                      + ["hgv0", "hgv1", "hog0", "hog1", "daq0", "daq1", "dak0", "dak1", "dav0", "dav1"]
                      + [f"gate{b}_{i}" for b in range(3) for i in range(4)]
                      + [f"br{b}_{i}" for b in range(3) for i in range(4)]
                      + [f"out{i}" for i in range(4)] + ["ln1m", "ln1v", "logit", "logitT"]
                      + [f"u2t{i}" for i in range(4)] + ["rank"])
        PJ = Groups(nc, ctx, "proj", bank[0:2], proj_names)
        lev_names = [f"a{b}_{i}" for b in (64, 32, 16, 8, 4, 0) for i in range(2)]
        lev_names.insert(2, "a128")
        HD = Groups(nc, ctx, "mix", bank[6:8], lev_names + ["hgo0", "hgo1", "hgs0", "hgs1"]
                    + [f"s{h}_{m}" for h in range(4) for m in range(2)] + [f"pT{i}" for i in range(3)]
                    + ["dao0", "dao1", "das0", "das1", "ada1", "adaT1", "ada2", "adaT2"])
        rw_names = [f"lw{i}" for i in range(2)] + [f"la{i}" for i in range(2)] + [f"lg{i}" for i in range(2)]
        rw_names += ["kk0", "kk1", "bo0", "bo1"]
        for hf in range(2):
            rw_names += [f"{hf}tok{i}" for i in range(4)]
            if hf:
                rw_names.append("0gm")
            rw_names += [f"{hf}m{m}_{hp}" for m in range(4) for hp in range(2)]
            if hf:
                rw_names.append("0gv")
            rw_names += [f"{hf}x1_{hp}" for hp in range(2)]
            for b in LEVELS[1:6]:
                rw_names += [f"{hf}y{b}_{hp}" for hp in range(2)]
                rw_names += [f"{hf}xt{b}_{hp}" for hp in range(2)]
                if b < 32:
                    rw_names += [f"{hf}xx{b}_{hp}" for hp in range(2)]
            rw_names += [f"{hf}y0_{hp}" for hp in range(2)] + [f"{hf}up_{hp}" for hp in range(2)] + [f"{hf}wat"]
            for c in range(NCH):
                if c:
                    rw_names.append(f"{hf}u{c}")
                if c < NCH - 1:
                    rw_names.append(f"{hf}s{c}")
            rw_names.append(f"{hf}o")
        rw_names += ["1gm", "1gv"]
        RW = Groups(nc, ctx, "rwkv", bank[2:6], rw_names)

        units = []
        units += [("ada", 0, q, "ada0") for q in range(4)]
        in_units = [(5120, 256, "rw6"), (4096, 512, "rw3"), (3584, 512, "rw1"), (512, 512, "hgf1"), (0, 512, "hgq1"),
                    (4608, 512, "rw5"), (1024, 512, "hgv1"), (1536, 512, "hog1"), (2048, 512, "daq1"),
                    (2560, 512, "dak1"), (3072, 512, "dav1")]
        units += [("in", c0, w, last) for c0, w, last in in_units]
        for what in "g00 g01 g10 a10 a11 g11 a12 a13 g20 a20 a21 g21 a22 a23".split():
            x, y = int(what[1]), int(what[2])
            units.append(("ada", x, y, f"ada{x}") if what[0] == "a" else ("gate", x, y, f"gate{x}_{2 * y + 1}"))
        units += [("br", b, 0, f"br{b}_3") for b in range(3)]
        units += [("out", 0, i, f"out{2 * i + 1}") for i in range(2)]
        UIDX = {}
        for i, u in enumerate(units):
            UIDX[u[:3]] = i
        front_uses = [sum(1 for i in range(len(units)) if i % FRONT_SLOTS == s) for s in range(FRONT_SLOTS)]
        front_uses += [0] * (MOE_SLOTS - FRONT_SLOTS)
        slot_in = [sem(f"weights_in_slot{i}") for i in range(MOE_SLOTS)]
        ada_used = sem("ada_unit_used")

        def unit(eng, *key):
            i = UIDX[key]
            eng.wait_ge(slot_in[i % FRONT_SLOTS], 16 * (i // FRONT_SLOTS + 1))
            return ring[i % FRONT_SLOTS]

        const_in, vec_in, x_in, lora_in, row_in = sem("consts_in"), sem("vectors_in"), sem("x_in"), sem("lora_in"), sem("rows_in")
        out_done = sem("out_written")
        cond_sig, lb_exp, lb_in, ln2_sum = sem("cond_sigmoid"), sem("lower_bound_exp"), sem("lower_bound_in"), sem("ln2_sum")
        cond_ready, u_ready = sem("cond_ready"), sem("u_ready")
        modrow_ready = sem("modrow_ready")
        pad_ready, xs_ready = sem("pad_ready"), sem("shifted_ready")
        lora_act = sem("lora_act_ready")
        lora_done = sem("lora_gates_ready")
        kk_ready, kk_sqd, kk_n = sem("kk_ready"), sem("kk_squared"), sem("kk_norm_ready")
        cs_ready, dec_ready = sem("cumsum_ready"), sem("decays_ready")
        rk_ready, rwf_ready = sem("rk_ready"), sem("rwkv_factors_ready")
        f_ready, logf_ready = sem("hg_forget_ready"), sem("hg_logf_ready")
        dec_in, dec_out = sem("hg_exponent_ready"), sem("hg_decay_ready")
        lev_ready = sem("hg_level_ready")
        at_ready = sem("hg_scores_ready")
        osq_ready = sem("out_squared")
        o_ready = sem("branch_out_ready")
        nmax_ready, e_ready, p_ready = sem("negmax_ready"), sem("exp_ready"), sem("probs_ready")
        lam_ready, lam_exp = sem("lambda_sums_ready"), sem("lambda_exp_ready")
        m_ready, xt_ready, nl_ready = sem("rw_matrices_ready"), sem("rw_inverse_started"), sem("rw_level_mask_ready")
        pool_ch, dq_ready, head_ready = sem("pool_chain"), sem("attention_q_ready"), sem("head_factors_ready")
        st_ready = sem("rw_state_ready")
        go_sq, go_d = sem("gn_squared"), sem("gn_centred")
        orw_copied = sem("rw_out_copied")
        merged_ready = sem("merged_ready")
        y1_ready, lnd, lnsq, lnr = sem("ln_in_ready"), sem("ln_centred"), sem("ln_squared"), sem("ln_rstd")
        u2_even, u2_odd = sem("u2_even_tiles"), sem("u2_odd_tiles")
        lg_exp_in, lg_exp = sem("router_shifted"), sem("router_exp")
        chosen_ready = sem("chosen_ready")
        flag_ready = sem("flag_ready")
        dve_ch, act_ch = sem("dve_chain"), sem("act_chain")
        x2_ready = sem("result_ready")
        v_ready, hog_sig, x_scaled = sem("v_ready"), sem("hg_out_gate_sigmoid"), sem("x_scaled")
        fold_ready, xh_ready = sem("norm_factors_ready"), sem("xhat_ready")
        res_ready, scaled_ready = sem("residual_ready"), sem("result_scaled")

        pick_ready, pw_ready = sem("picks_ready"), sem("weighted_picks_ready")
        pw_full, pw_copied = sem("pick_transposes_done"), sem("pick_transposes_copied")
        xg_full, xg_ready = sem("gather_done"), sem("gathered_ready")
        gate_full, up_full = sem("gate_done"), sem("up_done")
        sig_ready, h_ready = sem("silu_ready"), sem("hidden_ready")
        hT_full, hT_ready = sem("hidden_transposed"), sem("hidden_t_ready")
        y_full, y_ready = sem("down_done"), sem("y_ready")
        comb_full, comb_added = sem("combine_done"), sem("combine_added")
        mean_done, count_mats = sem("result_mean_done"), sem("count_matrices_ready")
        moe_ch, pick_ch, comb_half = sem("moe_dve_chain"), sem("pick_chain"), sem("combine_half_added")
        blk_ch = sem("moe_pass_chain")

        gate_slots, up_slots = ((0, 1), (6, 7)), ((2, 3), (8, 9))
        comb_bank = (bank[7], bank[4])
        XG = rwx_a[:, 0:1024]
        GH = rwx_a[:, 1024:1536]
        HT_ = rwx_a[:, 1536:2048]
        PK, PW, PWT = [rwx_a[:, 2048 + 256 * i:2304 + 256 * i] for i in range(3)]
        U2K = A[:, work0:work0 + 2048]
        Y = A[:, work0 + 6144:work0 + 7168]
        U2 = rwx_a[:, 0:2048]
        before16, ones16 = [gates[0][:, 64 * i:64 * i + 64].bitcast(BF16) for i in range(2)]
        chosen16 = gates[0][:, 128:144].bitcast(BF16)
        LNT = U2K

        lvX, lvE = gates[0][:, 0:1024], gates[0][:, 1024:2048]
        lvK, lvQ = cs1, gates[2][:, 0:1024]
        scoresT = A[:, gates1_at + 1024:gates1_at + 2560]
        dq_map = [lvX, gates[2][:, 1024:2048]]
        vs = bonus
        hog_s = gates[1][:, 0:1024]
        att = A[:, late:late + 3072]
        probsT = A[:, late + 3072:late + 4608]
        daSq = A[:, late + 4608:late + 5632]
        daR = hb1
        RB = route[:, 0:E]
        rt2 = route[:, 16:20]
        scores, chosen = route[:, 20:52], route[:, 52:84]
        slot = route[:, 196:228]
        lgT = Y[:, 256:512]

        def rw_mats(hf):
            lt = [A[:, late + i * 1024:late + (i + 1) * 1024] for i in range(6)]
            wk = [A[:, work0 + i * 1024:work0 + (i + 1) * 1024] for i in range(7)]
            NT, X, XT, YY = lt[0:4]
            NL = lt[4:6]
            AKT, RBT, RKT = wk[0:3]
            tok = [A[:, work0 + 3072 + i * 512:work0 + 3584 + i * 512] for i in range(4)]
            UP, WAT = [A[:, work0 + 5120 + i * 512:work0 + 5632 + i * 512] for i in range(2)]
            ST = rwx_a[:, 0:1024]
            Y0 = rwx_a[:, 1536:2048]
            return NT, X, XT, YY, NL, AKT, RBT, RKT, tok, Y0, UP, WAT, ST

        def kk_gn(hf):
            return rwx_a[:, 1024:1536]

        block = ctx.enter_context(nc.Block())

        @block.sync
        def _(sp):
            sp.dma_start(vec, vecs).then_inc(vec_in, 16)

            def load(i):
                u = units[i]
                s = i % FRONT_SLOTS
                if i >= FRONT_SLOTS:
                    prev = units[i - FRONT_SLOTS]
                    if prev[0] == "ada":
                        sp.wait_ge(ada_used, 4 * prev[1] + prev[2] + 1)
                    else:
                        t, full, free, k = PJ.at(prev[3])
                        sp.wait_ge(full, k + 1)
                if u[0] == "ada":
                    src = w_ada[:, u[2] * 2:u[2] * 2 + 2, u[1] * 2048:(u[1] + 1) * 2048]
                    dst = ring[s].rearrange("p (k c) -> p k c", k=2)
                elif u[0] == "in":
                    src = w_in[:, :, u[1]:u[1] + u[2]]
                    dst = ring[s][:, 0:KT * u[2]].rearrange("p (k c) -> p k c", k=KT)
                elif u[0] == "gate":
                    src = w_merge[:, u[1], :, u[2] * 512:(u[2] + 1) * 512]
                    dst = ring[s].rearrange("p (k c) -> p k c", k=KT)
                elif u[0] == "br":
                    src = w_branch[:, u[1] * 4:u[1] * 4 + 4, :]
                    dst = ring[s].rearrange("p (k c) -> p k c", k=4)
                else:
                    src = w_out[:, :, u[2] * 512:(u[2] + 1) * 512]
                    dst = ring[s].rearrange("p (k c) -> p k c", k=KT)
                sp.dma_start(dst, src).then_inc(slot_in[s], 16)

            sp.dma_start(cst[:, 0:P], consts[:, 0:P]).then_inc(const_in, 16)
            for i in range(4):
                load(i)
            sp.dma_start(tiles(xT, KT), xt).then_inc(x_in, 16)
            load(4)
            load(5)
            sp.dma_start(cst[:, P:KEPT_COLS], consts[:, P:KEPT_COLS]).then_inc(const_in, 16)
            sp.dma_start(mix_cst, consts[:, KEPT_COLS:CONST_COLS]).then_inc(const_in, 16)
            sp.dma_start(lora_wa[0:64, :], rw_w_up).then_inc(lora_in, 16)
            sp.dma_start(lora_wa[64:128, :], rw_a_up).then_inc(lora_in, 16)
            sp.dma_start(lora_g, rw_g_up).then_inc(lora_in, 16)
            sp.dma_start(lam_sb, lam_row.to_broadcast([P, 256])).then_inc(row_in, 16)
            sp.dma_start(wr.rearrange("p (k e) -> p k e", k=KT), w_router).then_inc(row_in, 16)
            sp.dma_start(route[:, 0:E], rbias_row.to_broadcast([P, E])).then_inc(row_in, 16)
            for i in range(6, len(units)):
                load(i)

            def expert_load(s, what, e):
                w, kt = ((w_gate, KT), (w_up, KT), (w_down, FE // P))[what]
                src = w[bass.ds(e, 1), :, :, :].rearrange("e p k c -> p (e k) c")
                sp.dma_start(ring[s].rearrange("p (k c) -> p k c", k=kt), src).then_inc(slot_in[s], 16)

            def load_gate(p, j, odd, n):
                sp.wait_ge(gate_full, n - 1)
                expert_load(gate_slots[odd][j], 0, 2 * p + j)

            def load_gates(p, odd, n):
                for j in range(2):
                    load_gate(p, j, odd, n)

            def load_up(p, j, odd, n):
                sp.wait_ge(up_full, n - 1)
                expert_load(up_slots[odd][j], 1, 2 * p + j)

            def load_downs(p, n):
                sp.wait_ge(y_full, 2 * n)
                for j in range(2):
                    expert_load(4 + j, 2, 2 * p + j)

            def step(p, odd, n):
                load_gates(p + 1, 1 - odd, n + 1)
                load_downs(p, n)
                for j in range(2):
                    load_up(p + 1, j, 1 - odd, n + 1)

            def last_steps(n):
                load_downs(PAIRS - 2, n)
                load_gates(PAIRS - 1, 1, n + 1)
                for j in range(2):
                    load_up(PAIRS - 1, j, 1, n + 1)
                load_downs(PAIRS - 1, n + 1)

            t, full, free, k = RW.at("1o")
            sp.wait_ge(full, k + 1)
            expert_load(9, 1, 3)
            t, full, free, k = PJ.at("br1_3")
            sp.wait_ge(full, k + 1)
            expert_load(6, 0, 2)
            sp.wait_ge(merged_ready, 4)
            for s in range(FRONT_SLOTS, RING_SLOTS):
                expert_load(s, s // 2, s % 2)
            expert_load(7, 0, 3)
            expert_load(8, 1, 2)
            nu = len(units)
            for i in range(nu - FRONT_SLOTS, nu):
                t, full, free, k = PJ.at(units[i][3])
                sp.wait_ge(full, k + 1)
                s = i % FRONT_SLOTS
                expert_load(s, s // 2, s % 2)
            load_gates(2, 0, 2)
            load_up(2, 0, 0, 2)
            load_downs(1, 1)
            load_up(2, 1, 0, 2)
            with sp.Fori(1, PAIRS // 2 - 1) as h:
                step(2 * h, 0, 2 * h)
                step(2 * h + 1, 1, 2 * h + 1)
            last_steps(PAIRS - 2)
            sp.wait_ge(flag_ready, 1)
            over_ = sp.value_load(flag_i[0:1, 0:1], min_val=0, max_val=1)
            with sp.If(over_ > 0):
                with sp.Fori(1, PASSES) as b:
                    load_gates(0, 0, b * PAIRS)
                    for j in range(2):
                        load_up(0, j, 0, b * PAIRS)
                    with sp.Fori(0, PAIRS // 2 - 1) as h:
                        step(2 * h, 0, b * PAIRS + 2 * h)
                        step(2 * h + 1, 1, b * PAIRS + 2 * h + 1)
                    last_steps(b * PAIRS + PAIRS - 2)
            for i in range(4):
                sp.wait_ge(x2_ready, 2 * i + 2)
                sp.dma_start(out[:, 2 * i:2 * i + 2, :], tiles(uT, KT)[:, 2 * i:2 * i + 2, :]).then_inc(out_done, 16)
            sp.wait_ge(out_done, 64)

        @block.gpsimd
        def _(pool):
            n = [0]

            def link(ins):
                n[0] += 1
                ins.then_inc(pool_ch, 1)
                pool.wait_ge(pool_ch, n[0])

            nc.gpsimd.memset(rwx[:, :, 0:1], 0.0).then_inc(pad_ready, 1)
            pool.wait_ge(const_in, 48)

            def one_head(dst, src, head, *more):
                return nc.gpsimd.tensor_scalar(dst, src, M("pair")[:, head * 64:head * 64 + 1], *more)

            pool.wait_ge(u_ready, KT)
            nc.gpsimd.tensor_scalar(xT, xT, ALPHA, None, ALU.mult).then_inc(x_scaled, 1)
            PJ.wait_read(pool, "rw4")
            PJ.wait_read(pool, "rw5")
            v3, vs3 = rwx[:, 8:12, 1:], tiles(vs, 4)
            link(nc.gpsimd.tensor_tensor(vs3, rwx[:, 8:12, 0:T], v3, ALU.subtract))
            for m in range(4):
                ins = nc.gpsimd.tensor_scalar(vs3[:, m, :], vs3[:, m, :], V("mu", 8 + m), None, ALU.mult)
                ins.then_inc(pool_ch, 1)
            n[0] += 4
            pool.wait_ge(pool_ch, n[0])
            nc.gpsimd.tensor_tensor(v3, v3, vs3, ALU.add).then_inc(v_ready, 1)
            PJ.wait_read(pool, "daq0")
            PJ.wait_read(pool, "daq1")
            HD.wait_full(pool, "a128")
            for m in range(2):
                one_head(dq_map[m], o_da, m, 0.125, ALU.mult, ALU.mult).then_inc(dq_ready, 1)
            for hf in range(2):
                NT, X, _, YY, NL = rw_mats(hf)[0:5]
                for src, dst, frees in ((a_rw, X, ((HD, "pT2"), (HD, "pT1")) if hf == 0 else ((RW, "0xt32_1"),)),
                                        (kt_f, YY, ((HD, "dao0"), (HD, "dao1")) if hf == 0 else ((RW, "0xt32_0"),))):
                    for G, g in frees:
                        G.wait_full(pool, g)
                    if hf == 0:
                        pool.wait_ge(rwf_ready, 1)
                    for hp in range(2):
                        one_head(dst[:, hp * 512:(hp + 1) * 512], src[:, hf * 512:(hf + 1) * 512], hp, None,
                                 ALU.mult).then_inc(head_ready, 1)
                pool.wait_ge(m_ready, 8 * hf + 2)
                for i, b in enumerate(LEVELS[1:6]):
                    if i >= 2:
                        RW.wait_full(pool, f"{hf}y{LEVELS[i - 1]}_1")
                    nc.gpsimd.tensor_tensor(tiles(NL[i % 2], 8), tiles(NT, 8), over(M(f"lev{b}"), 8),
                                            ALU.mult).then_inc(nl_ready, 1)
                    pool.wait_ge(nl_ready, 5 * hf + i + 1)

            t, full, free, k = PJ.at("out3")
            pool.wait_ge(full, k + 1)
            for dst, name in ((before16, "before"), (ones16, "ones")):
                nc.gpsimd.tensor_copy(dst, M(name)).then_inc(count_mats, 1)
            x3, u3 = tiles(xT, KT), tiles(U2, KT)
            pool.wait_ge(fold_ready, 1)
            for m in range(0, KT, 2):
                pool.wait_ge(xh_ready, m // 2 + 1)
                nc.gpsimd.tensor_scalar(u3[:, m, :], x3[:, m, :], u2_s[:, m:m + 1], u2_b[:, m:m + 1], ALU.mult,
                                        ALU.add).then_inc(u2_even, 1)
            pool.wait_ge(u2_even, KT // 2)
            pool.wait_ge(u2_odd, KT // 2)
            for m in range(KT):
                nc.gpsimd.tensor_scalar(x3[:, m, :], x3[:, m, :], res_s[:, m:m + 1], res_b[:, m:m + 1], ALU.mult,
                                        ALU.add).then_inc(res_ready, 1)

        @block.tensor
        def _(pe):
            mm = nc.tensor.matmul

            def mod_rows(r, q):
                G = HD if r else PJ
                if q == 0:
                    G.claim(pe, f"ada{r}")
                t, full, free, n = G.at(f"ada{r}")
                w = unit(pe, "ada", r, q).rearrange("p (k c) -> p k c", k=2)
                for k in range(2):
                    for g in range(4):
                        last = mm(t[32 * g:32 * g + 32, :], condb[:, (2 * q + k) * 32:(2 * q + k) * 32 + 32],
                                  w[:, k, g * 512:(g + 1) * 512], start=(q + k == 0), stop=(q == 3 and k == 1))
                if q == 3:
                    last.then_inc(full, 1)
                    G.wait_full(pe, f"ada{r}")
                    pe.nop().then_inc(ada_used, 1)
                else:
                    last.then_inc(ada_used, 1)

            def mod_cols(r):
                pe.wait_ge(modrow_ready, r + 1)
                t, full = (HD if r else PJ).claim(pe, f"adaT{r}")
                for i in range(4):
                    last = nc.tensor.transpose(t[:, i * P:(i + 1) * P], modrow[:, i * P:(i + 1) * P], M("ident"))
                last.then_inc(full, 1)

            uv = tiles(uT, KT)

            def project(name, w, m0, rhs=uv, kt=KT, ready=None, per_count=1, part=None):
                t, full = PJ.claim(pe, name) if part != 1 else PJ.at(name)[0:2]
                for i in range(2) if part is None else (part,):
                    for k in range(kt):
                        if ready and i == 0 and k % per_count == 0:
                            pe.wait_ge(ready, k // per_count + 1)
                        last = mm(t[:, i * T:(i + 1) * T], w[:, k, (m0 + i) * P:(m0 + i + 1) * P], rhs[:, k, :],
                                  start=(k == 0), stop=(k == kt - 1))
                if part != 0:
                    last.then_inc(full, 1)

            def project_tokens(name, w, b):
                t, full = PJ.claim(pe, name)
                for k in range(KT):
                    last = mm(t[:, :], uv[:, k, b * P:(b + 1) * P], w[:, k, :], start=(k == 0), stop=(k == KT - 1))
                last.then_inc(full, 1)

            def gate_group(b, i, part=None):
                w = unit(pe, "gate", b, i // 2).rearrange("p (k c) -> p k c", k=KT)
                project(f"gate{b}_{i}", w, 2 * (i % 2), part=part)

            pe.wait_ge(cond_ready, 1)
            for q in range(4):
                mod_rows(0, q)
            pe.wait_ge(const_in, 16)
            mod_cols(0)

            def in_group(name, c0, i, w_=512):
                w = unit(pe, "in", c0, w_)[:, 0:KT * w_].rearrange("p (k c) -> p k c", k=KT)
                project(name, w, 2 * i, ready=u_ready if name == "rw6" else None)

            def in_tokens(name, c0, i):
                project_tokens(name, unit(pe, "in", c0, 512).rearrange("p (k c) -> p k c", k=KT), i)

            in_group("rw6", 5120, 0, 256)
            in_group("rw2", 4096, 0)
            in_group("rw3", 4096, 1)

            pe.wait_ge(lora_in, 48)
            pe.wait_ge(lora_act, 2)
            for what, lhs, rhs in (("lw", lora_wa[0:64, :], rwx[0:64, 12, 1:]), ("la", lora_wa[64:128, :], rwx[64:128, 12, 1:]),
                                   ("lg", lora_g, rwx[:, 13, 1:])):
                for i in range(2):
                    t, full = RW.claim(pe, f"{what}{i}")
                    for j in range(2):
                        m = 2 * i + j
                        last = mm(t[:, j * T:(j + 1) * T], lhs[:, m * P:(m + 1) * P], rhs, start=True, stop=True)
                    last.then_inc(full, 1)
            in_group("rw0", 3584, 0)
            in_group("rw1", 3584, 1)

            def head_sums(what):
                for i in range(2):
                    t, full = RW.claim(pe, f"{what}{i}")
                    mm(t[:, :], M("pair"), kk_sq[:, i * 512:(i + 1) * 512], start=True, stop=True).then_inc(full, 1)

            pe.wait_ge(kk_sqd, 1)
            pe.wait_ge(const_in, 48)
            head_sums("kk")
            in_group("hgf0", 512, 0)
            in_group("hgf1", 512, 1)
            in_group("hgq0", 0, 0)
            in_group("hgq1", 0, 1)
            in_group("rw4", 4608, 0)
            in_group("rw5", 4608, 1)

            q3, k3 = tiles(lvQ, 4), tiles(lvK, 4)

            def level(name, n, sk, sq, kk_=None, qq_=None):
                pe.wait_ge(lev_ready, n)
                t, full = HD.claim(pe, name)
                for h in range(H4):
                    last = mm(t[:, h * P:(h + 1) * P], (kk_ or k3)[:, h, sk:sk + P], (qq_ or q3)[:, h, sq:sq + P],
                              start=True, stop=True)
                last.then_inc(full, 1)

            in_tokens("hgv0", 1024, 0)
            in_tokens("hgv1", 1024, 1)
            level("a64_0", 1, 0, 0)
            level("a64_1", 1, P, P)
            in_group("hog0", 1536, 0)
            level("a128", 2, 0, 0, tiles(lvX, 8)[:, 0:4, :], tiles(lvX, 8)[:, 4:8, :])
            in_group("hog1", 1536, 1)
            for i, b in enumerate((32, 16, 8, 4, 0)):
                for s in range(2):
                    level(f"a{b}_{s}", 3 + i, s * P, s * P)
                if i < 4:
                    what, c0 = (("daq", 2048), ("dak", 2560))[i // 2]
                    in_group(f"{what}{i % 2}", c0, i % 2)
                if i == 0:
                    pe.wait_ge(rk_ready, 1)
                    head_sums("bo")
            in_tokens("dav0", 3072, 0)
            pe.wait_ge(at_ready, 1)
            hv3, A4 = tiles(hv, 2), scoresT.rearrange("p (a h t) -> p a h t", a=3, h=H4)
            for s in range(2):
                t, full = HD.claim(pe, f"hgo{s}")
                for h in range(H4):
                    o = t[:, h * P:(h + 1) * P]
                    if s == 0:
                        last = mm(o, hv3[:, 0, h * P:(h + 1) * P], A4[:, 0, h, :], start=True, stop=True)
                    else:
                        mm(o, hv3[:, 0, h * P:(h + 1) * P], A4[:, 2, h, :], start=True, stop=False)
                        last = mm(o, hv3[:, 1, h * P:(h + 1) * P], A4[:, 1, h, :], start=False, stop=True)
                last.then_inc(full, 1)
            in_tokens("dav1", 3072, 1)
            for s in range(2):
                pe.wait_ge(osq_ready, s + 1)
                t, full = HD.claim(pe, f"hgs{s}")
                mm(t[:, :], M("ones_dv"), lvE[:, s * 512:(s + 1) * 512], start=True, stop=True).then_inc(full, 1)

            dk3, dv3 = tiles(dk_, 4), tiles(dv_, 2)
            PJ.wait_read(pe, "dak1")
            pe.wait_ge(dq_ready, 2)
            for h in range(H4):
                for m in range(2):
                    dq = tiles(dq_map[m], 4)
                    t, full = HD.claim(pe, f"s{h}_{m}")
                    mm(t[:, 0:P], dq[:, h, 0:P], dk3[:, h, 0:P], start=True, stop=True)
                    mm(t[:, P:3 * P], dq[:, h, P:T], dk3[:, h, :], start=True, stop=True).then_inc(full, 1)
            gate_group(0, 0)
            gate_group(0, 1)
            pe.wait_ge(p_ready, 1)
            S8 = tiles(att, 8)
            for i in range(3):
                t, full = HD.claim(pe, f"pT{i}")
                for h in range(H4):
                    last = nc.tensor.transpose(t[:, h * P:(h + 1) * P], S8[:, 2 * h, i * P:(i + 1) * P], M("ident"))
                last.then_inc(full, 1)
            gate_group(0, 2)
            PJ.wait_read(pe, "dav1")
            HD.wait_read(pe, "pT2")
            HD.wait_read(pe, "pT1")
            pT3 = probsT.rearrange("p (a h t) -> p a h t", a=3, h=H4)
            for s in range(2):
                t, full = HD.claim(pe, f"dao{s}")
                for h in range(H4):
                    o = t[:, h * P:(h + 1) * P]
                    if s == 0:
                        last = mm(o, dv3[:, 0, h * P:(h + 1) * P], pT3[:, 0, h, :], start=True, stop=True)
                    else:
                        mm(o, dv3[:, 0, h * P:(h + 1) * P], pT3[:, 1, h, :], start=True, stop=False)
                        last = mm(o, dv3[:, 1, h * P:(h + 1) * P], pT3[:, 2, h, :], start=False, stop=True)
                last.then_inc(full, 1)
            af, bf, kf, rf = [tiles(x, 4) for x in (at_f, a_rw, kt_f, rt_f)]
            vf = rwx[:, 8:12, 1:]

            def rw_tokens(hf):
                for n, src in enumerate((af, bf, kf, vf)):
                    t, full = RW.claim(pe, f"{hf}tok{n}")
                    for s in range(2):
                        for jj in range(2):
                            o = (s * 2 + jj) * P
                            last = nc.tensor.transpose(t[:, o:o + P], src[:, 2 * hf + jj, s * P:(s + 1) * P], M("ident"))
                    last.then_inc(full, 1)

            pe.wait_ge(rwf_ready, 1)
            rw_tokens(0)
            gate_group(0, 3)
            for s in range(2):
                pe.wait_ge(osq_ready, 2 + s + 1)
                t, full = HD.claim(pe, f"das{s}")
                mm(t[:, :], M("ones_dv"), daSq[:, s * 512:(s + 1) * 512], start=True, stop=True).then_inc(full, 1)

            def gn_mean(hf):
                pe.wait_ge(orw_copied, hf + 1)
                t, full = RW.claim(pe, f"{hf}gm")
                mm(t[:, :], M("pair_mean"), o_rw[:, hf * 512:(hf + 1) * 512], start=True, stop=True).then_inc(full, 1)

            def gn_var(hf):
                pe.wait_ge(go_sq, hf + 1)
                t, full = RW.claim(pe, f"{hf}gv")
                mm(t[:, :], M("pair_mean"), kk_gn(hf), start=True, stop=True).then_inc(full, 1)

            gate_group(1, 0)
            for hf in range(2):
                NT, X, XT, YY, NL, AKT, RBT, RKT, tok, Y0, UP, WAT, ST = rw_mats(hf)
                j0 = 2 * hf

                def q_of(hp, jj, s):
                    return slice(((hp * 2 + jj) * 2 + s) * P, ((hp * 2 + jj) * 2 + s + 1) * P)

                if hf:
                    rw_tokens(hf)
                    gn_mean(0)
                pe.wait_ge(head_ready, 4 * hf + 4)
                for n, (lh, rh) in enumerate(((X, af), (YY, af), (X, rf), (YY, rf))):
                    for hp in range(2):
                        lh3 = tiles(lh, 4)[:, 2 * hp:2 * hp + 2, :]
                        t, full = RW.claim(pe, f"{hf}m{n}_{hp}")
                        for jj in range(2):
                            for s in range(2):
                                o = (jj * 2 + s) * P
                                last = mm(t[:, o:o + P], lh3[:, jj, s * P:(s + 1) * P], rh[:, j0 + jj, s * P:(s + 1) * P],
                                          start=True, stop=True)
                        last.then_inc(full, 1)
                if hf:
                    gn_var(0)
                    gate_group(2, 0)
                pe.wait_ge(xt_ready, hf + 1)
                for hp in range(2):
                    t, full = RW.claim(pe, f"{hf}x1_{hp}")
                    for i in range(4):
                        q = (hp * 4 + i) * P
                        last = nc.tensor.transpose(t[:, i * P:(i + 1) * P], XT[:, q:q + P], M("ident"))
                    last.then_inc(full, 1)
                for i, b in enumerate(LEVELS[1:6]):
                    pe.wait_ge(nl_ready, 5 * hf + i + 1)
                    for hp in range(2):
                        if i:
                            RW.wait_read(pe, f"{hf}xx{LEVELS[i]}_{hp}")
                        else:
                            RW.wait_read(pe, f"{hf}x1_{hp}")
                        t, full = RW.claim(pe, f"{hf}y{b}_{hp}")
                        for n in range(4):
                            q = (hp * 4 + n) * P
                            last = mm(t[:, n * P:(n + 1) * P], NL[i % 2][:, q:q + P], X[:, q:q + P], start=True, stop=True)
                        last.then_inc(full, 1)
                    if i % 2:
                        gate_group(1 + hf, 1 + i // 2)
                    else:
                        mod_rows(1 + hf, i // 2)
                    for hp in range(2):
                        RW.wait_read(pe, f"{hf}y{b}_{hp}")
                        if i:
                            RW.wait_read(pe, f"{hf}xt{LEVELS[i]}_{hp}")
                        t, full = RW.claim(pe, f"{hf}xt{b}_{hp}")
                        for n in range(4):
                            q = (hp * 4 + n) * P
                            last = mm(t[:, n * P:(n + 1) * P], YY[:, q:q + P], XT[:, q:q + P], start=True, stop=True)
                        last.then_inc(full, 1)
                    if b < 32:
                        for hp in range(2):
                            RW.wait_read(pe, f"{hf}xt{b}_{hp}")
                            t, full = RW.claim(pe, f"{hf}xx{b}_{hp}")
                            for n in range(4):
                                q = (hp * 4 + n) * P
                                last = nc.tensor.transpose(t[:, n * P:(n + 1) * P], XT[:, q:q + P], M("ident"))
                            last.then_inc(full, 1)
                RW.wait_read(pe, f"{hf}tok3")
                pe.wait_ge(m_ready, 8 * hf + 8)
                for hp in range(2):
                    t, full = RW.claim(pe, f"{hf}y0_{hp}")
                    for jj in range(2):
                        for s in range(2):
                            o = (jj * 2 + s) * P
                            last = mm(t[:, o:o + P], AKT[:, q_of(hp, jj, s)], tok[3][:, (s * 2 + jj) * P:(s * 2 + jj + 1) * P],
                                      start=True, stop=True)
                    last.then_inc(full, 1)
                mod_rows(1 + hf, 3)
                RW.wait_read(pe, f"{hf}y0_1")
                RW.wait_read(pe, f"{hf}y0_0")
                RW.wait_read(pe, f"{hf}xt32_0")
                RW.wait_read(pe, f"{hf}xt32_1")
                for hp in range(2):
                    t, full = RW.claim(pe, f"{hf}up_{hp}")
                    for jj in range(2):
                        for s in range(2):
                            o = (jj * 2 + s) * P
                            last = mm(t[:, o:o + P], XT[:, q_of(hp, jj, s)], Y0[:, o:o + P], start=True, stop=True)
                    last.then_inc(full, 1)
                t, full = RW.claim(pe, f"{hf}wat")
                for jj in range(2):
                    for s in range(2):
                        for hp in range(2):
                            o = (jj * 2 + s) * P
                            a0 = (s * 2 + jj) * P + hp * 64
                            last = mm(t[hp * 64:hp * 64 + 64, o:o + P], tok[0][:, a0:a0 + 64], XT[:, q_of(hp, jj, s)],
                                      start=True, stop=True)
                last.then_inc(full, 1)
                RW.wait_read(pe, f"{hf}wat")
                RW.wait_read(pe, f"{hf}up_0")
                RW.wait_read(pe, f"{hf}up_1")
                for c in range(NCH):
                    s, r = c // 2, slice((c % 2) * 64, (c % 2) * 64 + 64)
                    if c:
                        pe.wait_ge(st_ready, 3 * hf + c)
                        t, full = RW.claim(pe, f"{hf}u{c}")
                        for jj in range(2):
                            o = (jj * 2 + s) * P + (c % 2) * 64
                            last = mm(t[r, jj * P:(jj + 1) * P], WAT[:, o:o + 64], ST[:, (c * 2 + jj) * P:(c * 2 + jj + 1) * P],
                                      start=True, stop=True)
                        last.then_inc(full, 1)
                        RW.wait_read(pe, f"{hf}u{c}")
                    if c < NCH - 1:
                        t, full = RW.claim(pe, f"{hf}s{c}")
                        for jj in range(2):
                            a0, u0 = (s * 2 + jj) * P, (jj * 2 + s) * P
                            mm(t[:, jj * P:(jj + 1) * P], tok[1][r, a0:a0 + P], UP[r, u0:u0 + P], start=True, stop=False)
                            last = mm(t[:, jj * P:(jj + 1) * P], tok[2][r, a0:a0 + P], tok[3][r, a0:a0 + P],
                                      start=False, stop=True)
                        last.then_inc(full, 1)
                    if c < 2:
                        gate_group(1 + hf, 3, part=c)
                    elif c == 2:
                        mod_cols(1 + hf)
                t, full = RW.claim(pe, f"{hf}o")
                for jj in range(2):
                    for s in range(2):
                        o, a0 = (jj * 2 + s) * P, (s * 2 + jj) * P
                        heads = [(hp, slice(hp * 64, hp * 64 + 64), hp * 64) for hp in range(2)]
                        for hp, rr, hh in heads:
                            mm(t[rr, o:o + P], UP[:, o + hh:o + hh + 64], RBT[:, q_of(hp, jj, s)], start=True, stop=False)
                        for hp, rr, hh in heads:
                            mm(t[rr, o:o + P], tok[3][:, a0 + hh:a0 + hh + 64], RKT[:, q_of(hp, jj, s)], start=False, stop=False)
                        for c in (2 * s, 2 * s + 1):
                            for hp, rr, hh in heads:
                                s0 = (c * 2 + jj) * P + hh
                                last = mm(t[rr, o + (c % 2) * 64:o + (c % 2) * 64 + 64], ST[:, s0:s0 + 64],
                                          rf[:, j0 + jj, c * 64:(c + 1) * 64], start=False, stop=(c % 2 == 1))
                last.then_inc(full, 1)

            def branch_group(b, i):
                pe.wait_ge(o_ready, (1, 2, 4)[b])
                w = unit(pe, "br", b, 0).rearrange("p (k c) -> p k c", k=4)
                project(f"br{b}_{i}", w, 2 * i, rhs=tiles((o_hg, o_da, o_rw)[b], 4), kt=4)

            branch_group(0, 0)
            gn_mean(1)
            branch_group(0, 1)
            gn_var(1)
            for b in range(3):
                for i in range(0 if b else 2, 4):
                    branch_group(b, i)
            mg = tiles(gates[0], KT)
            for i in range(4):
                w = unit(pe, "out", 0, i // 2).rearrange("p (k c) -> p k c", k=KT)
                project(f"out{i}", w, 2 * (i % 2), rhs=mg, ready=merged_ready, per_count=2)

            def norm_sum(t, full, src, quarter_ready=None, n0=0):
                for k in range(KT):
                    if quarter_ready and k % 2 == 0:
                        pe.wait_ge(quarter_ready, n0 + k // 2 + 1)
                    last = mm(t[:, 0:T], M("ones_d"), tiles(src, KT)[:, k, :], start=(k == 0), stop=(k == KT - 1))
                last.then_inc(full, 1)

            norm_sum(*PJ.claim(pe, "ln1m"), xT, y1_ready, 0)
            norm_sum(*PJ.claim(pe, "ln1v"), LNT, lnsq, 0)
            pe.wait_ge(row_in, 48)
            t, full = PJ.claim(pe, "logit")
            for k in range(KT):
                pe.wait_ge((u2_even, u2_odd)[k % 2], k // 2 + 1)
                last = mm(t[0:E, 0:T], wr[:, k * E:(k + 1) * E], tiles(U2, KT)[:, k, :], start=(k == 0), stop=(k == KT - 1))
            last.then_inc(full, 1)
            PJ.wait_read(pe, "logit")
            t, full = PJ.claim(pe, "logitT")
            for s in range(2):
                last = nc.tensor.transpose(t[:, s * E:(s + 1) * E], lgT[0:E, s * P:(s + 1) * P], M("ident")[0:E, 0:E])
            last.then_inc(full, 1)
            for i in range(4):
                t, full = PJ.claim(pe, f"u2t{i}")
                for j in range(4):
                    m = (i % 2) * 4 + j
                    last = nc.tensor.transpose(t[:, j * P:(j + 1) * P], tiles(U2, KT)[:, m, (i // 2) * P:(i // 2 + 1) * P], M("ident"))
                last.then_inc(full, 1)
            pe.wait_ge(chosen_ready, 1)
            t, full = PJ.claim(pe, "rank")
            pe.wait_ge(count_mats, 2)
            ch = chosen16.rearrange("p (b e) -> p b e", b=2)
            mm(t[:, 0:E], before16, ch[:, 0, :], start=True, stop=True)
            mm(t[:, E:2 * E], before16, ch[:, 1, :], start=True, stop=False)
            mm(t[:, E:2 * E], ones16, ch[:, 0, :], start=False, stop=True)
            mm(t[:, 2 * E:3 * E], ones16, ch[:, 0, :], start=True, stop=False)
            mm(t[:, 2 * E:3 * E], ones16, ch[:, 1, :], start=False, stop=True).then_inc(full, 1)

            def gather(n, half):
                if half == 0:
                    pe.wait_ge(pick_ready, n + 1)
                if not isinstance(n, int) or n > 0:
                    pe.wait_ge(xg_ready, 2 * n)
                for j in range(4):
                    m = half * 4 + j
                    for s in range(2):
                        last = mm(bank[half][:, j * P:(j + 1) * P], U2K[:, s * D + m * P:s * D + (m + 1) * P],
                                  PK[:, s * P:(s + 1) * P], start=(s == 0), stop=(s == 1))
                last.then_inc(xg_full, 1)

            xg3, hT3 = tiles(XG, KT), tiles(HT_, 4)

            def pair(n, h, odd, more):
                for what, bk, done_ in ((0, 2, gate_full), (1, 3, up_full)):
                    slots = (up_slots if what else gate_slots)[odd]
                    for s in slots:
                        pe.wait_ge(slot_in[s], 16 * h + 16 * (front_uses[s] + 1))
                    for k in range(KT):
                        if what == 0 and k % 4 == 0:
                            pe.wait_ge(xg_ready, 2 * n + k // 4 + 1)
                        for j in range(2):
                            w = ring[slots[j]].rearrange("p (k c) -> p k c", k=KT)
                            last = mm(bank[bk][j * 64:j * 64 + 64, :], xg3[:, k, j * 64:j * 64 + 64], w[:, k, :],
                                      start=(k == 0), stop=(k == KT - 1))
                    last.then_inc(done_, 1)
                    if what == 0:
                        pe.wait_ge(pw_ready, n + 1)
                        pe.wait_ge(comb_added, 4 * n + 1)
                        for s in range(2):
                            last = nc.tensor.transpose(bank[7][:, s * P:(s + 1) * P], PW[:, s * P:(s + 1) * P], M("ident"))
                        last.then_inc(pw_full, 1)
                if more:
                    gather(n + 1, 0)
                pe.wait_ge(h_ready, n + 1)
                for k in range(4):
                    last = nc.tensor.transpose(bank[4][:, k * P:(k + 1) * P], GH[:, k * P:(k + 1) * P], M("ident"))
                last.then_inc(hT_full, 1)
                if more:
                    gather(n + 1, 1)
                pe.wait_ge(hT_ready, n + 1)
                for j in range(2):
                    pe.wait_ge(slot_in[4 + j], 16 * n + 16 * (front_uses[4 + j] + 1))
                for half in range(2):
                    for k in range(4):
                        for j in range(2):
                            w = ring[4 + j].rearrange("p (k c) -> p k c", k=4)
                            last = mm(bank[5 + half][j * 64:j * 64 + 64, :], hT3[:, k, j * 64:j * 64 + 64],
                                      w[:, k, half * 512:(half + 1) * 512], start=(k == 0), stop=(k == 3))
                    last.then_inc(y_full, 1)
                pe.wait_ge(pw_copied, n + 1)
                for i in range(4):
                    if i % 2 == 0:
                        pe.wait_ge(y_ready, 2 * n + i // 2 + 1)
                    if i >= 2:
                        pe.wait_ge(comb_added, 4 * n + i)
                    bk = comb_bank[i % 2]
                    for j in range(2):
                        m = 2 * i + j
                        last = mm(bk[:, j * T:(j + 1) * T], Y[:, m * P:(m + 1) * P], PWT,
                                  start=True, stop=True)
                    last.then_inc(comb_full, 1)

            def one_pass(n0, h0):
                gather(n0, 0)
                gather(n0, 1)
                with pe.Fori(0, PAIRS // 2 - 1) as h:
                    pair(n0 + 2 * h, h0 + h, 0, True)
                    pair(n0 + 2 * h + 1, h0 + h, 1, True)
                pair(n0 + PAIRS - 2, h0 + PAIRS // 2 - 1, 0, True)
                pair(n0 + PAIRS - 1, h0 + PAIRS // 2 - 1, 1, False)

            PJ.wait_read(pe, "rank")
            PJ.wait_read(pe, "u2t3")
            def result_mean(pairs_done, sums_done):
                norm_sum(bank[0], mean_done, xT, comb_added, 4 * pairs_done - 3)
                pe.wait_ge(mean_done, sums_done)

            one_pass(0, 0)
            result_mean(PAIRS, 1)
            pe.wait_ge(flag_ready, 1)
            over_ = pe.value_load(flag_i[0:1, 0:1], min_val=0, max_val=1)
            with pe.If(over_ > 0):
                with pe.Fori(1, PASSES) as b:
                    one_pass(b * PAIRS, b * (PAIRS // 2))
                result_mean(PASSES * PAIRS, 2)

            pe.nop().then_inc(ln2_sum, 1)
            norm_sum(bank[1], ln2_sum, LNT, lnsq, 4)

        @block.scalar
        def _(act):
            n = [0]

            def link(ins):
                n[0] += 1
                ins.then_inc(act_ch, 1)
                act.wait_ge(act_ch, n[0])

            def done(ins, s, v):
                ins.then_inc(s, 1)
                act.wait_ge(s, v)

            def fn(out_, in_, f, **kw):
                return nc.scalar.activation(out_, in_, f, **kw)

            act.wait_ge(vec_in, 16)
            done(fn(condc, V("c", 0, 8), ACT.Sigmoid), cond_sig, 1)

            act.wait_ge(lb_in, 1)
            done(fn(lbv, lbv, ACT.Exp), lb_exp, 1)

            act.wait_ge(pad_ready, 1)
            def shift_in(*groups):
                for g in groups:
                    t, free, k = PJ.wait_full(act, f"rw{g}")
                    done(fn(rwx[:, 2 * g:2 * g + 2, 1:], tiles(t[:, :], 2), ACT.Copy), free, k)

            def copy_in(name, g, dst):
                t, free, k = PJ.wait_full(act, f"{name}{g}")
                done(fn(dst[:, g * 512:(g + 1) * 512], t[:, :], ACT.Copy), free, k)

            shift_in(6, 2)
            act.wait_ge(xs_ready, 1)
            done(fn(rwx[0:64, 12, 1:], rwx[0:64, 12, 1:], ACT.Tanh), lora_act, 1)
            done(fn(rwx[:, 13, 1:], rwx[:, 13, 1:], ACT.Sigmoid), lora_act, 2)
            shift_in(3)
            for what, dst, v in (("lw", sig_w, "w0"), ("la", a_rw, "a0")):
                for i in range(2):
                    t, free, k = RW.wait_full(act, f"{what}{i}")
                    for j in range(2):
                        m = 2 * i + j
                        ins = fn(dst[:, m * T:(m + 1) * T], t[:, j * T:(j + 1) * T], ACT.Sigmoid, bias=V(v, m))
                        if j:
                            done(ins, free, k)
                        else:
                            link(ins)
            act.nop().then_inc(lora_done, 1)
            for i in range(2):
                t, free, k = RW.wait_full(act, f"lg{i}")
                done(fn(g_rw[:, i * 512:(i + 1) * 512], t[:, :], ACT.Copy), free, k)
            act.wait_ge(kk_ready, 1)
            done(fn(kk_sq, kk, ACT.Square), kk_sqd, 1)
            shift_in(0, 1)
            for g in range(2):
                t, free, k = PJ.wait_full(act, f"hgf{g}")
                link(fn(hb0[:, g * 512:(g + 1) * 512], t[:, :], ACT.Sigmoid))
                done(fn(hk[:, g * 512:(g + 1) * 512], t[:, :], ACT.Sigmoid, scale=-1.0), free, k)
            for g in range(2):
                copy_in("hgq", g, o_hg)
            nc.scalar.preload_act_table_set(LN_EXP)
            act.wait_ge(cs_ready, 1)
            link(fn(g_inv, cs0, ACT.Exp, scale=DECAY))
            link(fn(cs0, cs0, ACT.Exp, scale=-DECAY))
            done(fn(sig_w, sig_w, ACT.Exp, scale=-DECAY), dec_ready, 1)
            act.wait_ge(f_ready, 1)
            done(fn(hb0, hb0, ACT.Ln), logf_ready, 1)
            shift_in(4, 5)
            act.wait_ge(kk_n, 1)
            link(fn(kk_sq, kk_sq, ACT.Ln))
            done(fn(kk_sq, kk_sq, ACT.Exp, scale=-0.5), kk_n, 2)
            act.wait_ge(lam_ready, 1)
            done(fn(lam4[:, 2:4], lam4[:, 0:2], ACT.Exp), lam_exp, 1)
            copy_in("hgv", 0, hv)
            act.wait_ge(dec_in, 1)
            link(fn(lvE, lvE, ACT.Exp, scale=-1.0))
            done(fn(lvQ, hb0, ACT.Exp), dec_out, 1)
            act.wait_ge(dec_in, 2)
            done(fn(small[:, 184:192], small[:, 184:192], ACT.Exp), dec_out, 2)
            copy_in("hgv", 1, hv)
            copy_in("hog", 0, hog)

            def level_decay(i):
                act.wait_ge(dec_in, 3 + i)
                done(fn(lvE, lvE, ACT.Exp, scale=-1.0), dec_out, 3 + i)

            level_decay(0)
            copy_in("hog", 1, hog)
            level_decay(1)
            copy_in("daq", 0, o_da)
            level_decay(2)
            copy_in("daq", 1, o_da)
            level_decay(3)
            copy_in("dak", 0, dk_)
            act.wait_ge(dec_in, 7)
            link(fn(lvQ, lvE, ACT.Exp))
            done(fn(lvE, lvE, ACT.Exp, scale=-1.0), dec_out, 7)
            copy_in("dak", 1, dk_)
            copy_in("dav", 0, dv_)
            for s in range(2):
                t, free, k = HD.wait_full(act, f"hgo{s}")
                link(fn(tiles(o_hg, 4)[:, :, s * P:(s + 1) * P], tiles(t[:, :], 4), ACT.Copy))
                done(fn(lvE[:, s * 512:(s + 1) * 512], t[:, :], ACT.Square), free, k)
                act.nop().then_inc(osq_ready, 1)
            copy_in("dav", 1, dv_)
            for s in range(2):
                t, free, k = HD.wait_full(act, f"hgs{s}")
                link(fn(lvK[:, s * 512:(s + 1) * 512], t[:, :], ACT.Ln, bias=RMS_EPS))
                done(fn(lvK[:, s * 512:(s + 1) * 512], lvK[:, s * 512:(s + 1) * 512], ACT.Exp, scale=-0.5), free, k)
            def gate_sig(b, i):
                t, free, k = PJ.wait_full(act, f"gate{b}_{i}")
                for j in range(2):
                    m = 2 * i + j
                    ins = fn(gates[b][:, m * T:(m + 1) * T], t[:, j * T:(j + 1) * T], ACT.Sigmoid, bias=V("b_merge", b * 8 + m))
                    if j:
                        done(ins, free, k)
                    else:
                        link(ins)

            S8 = tiles(att, 8)
            for i in range(8):
                if i % 2 == 0:
                    act.wait_ge(nmax_ready, i // 2 + 1)
                link(fn(S8[:, i, 0:P], S8[:, i, 0:P], ACT.Exp, bias=smx[:, i:i + 1], accum_out=smx[:, 16 + i:17 + i]))
                ins = fn(S8[:, i, P:3 * P], S8[:, i, P:3 * P], ACT.Exp, bias=smx[:, 8 + i:9 + i],
                         accum_out=smx[:, 24 + i:25 + i])
                done(ins, e_ready, i + 1)
            nc.scalar.preload_act_table_set(SIGMOID)
            done(fn(hog_s, hog, ACT.Sigmoid), hog_sig, 1)
            gate_sig(0, 0)
            gate_sig(0, 1)
            for i in range(3):
                t, free, k = HD.wait_full(act, f"pT{i}")
                done(fn(probsT[:, i * 512:(i + 1) * 512], t[:, :], ACT.Copy), free, k)
            gate_sig(0, 2)
            for s in range(2):
                t, free, k = HD.wait_full(act, f"dao{s}")
                link(fn(tiles(o_da, 4)[:, :, s * P:(s + 1) * P], tiles(t[:, :], 4), ACT.Copy))
                done(fn(daSq[:, s * 512:(s + 1) * 512], t[:, :], ACT.Square), free, k)
                act.nop().then_inc(osq_ready, 1)
            def token_copies(hf):
                for i in range(4):
                    t, free, k = RW.wait_full(act, f"{hf}tok{i}")
                    done(fn(rw_mats(hf)[8][i], t[:, :], ACT.Copy), free, k)

            def gn_square(hf):
                act.wait_ge(go_d, hf + 1)
                done(fn(kk_gn(hf), o_rw[:, hf * 512:(hf + 1) * 512], ACT.Square), go_sq, hf + 1)

            def gn_rstd(hf):
                t, free, k = RW.wait_full(act, f"{hf}gv")
                link(fn(kk_gn(hf), t[:, :], ACT.Ln, bias=GN_EPS))
                done(fn(kk_gn(hf), kk_gn(hf), ACT.Exp, scale=-0.5), free, k)

            act.wait_ge(o_ready, 1)
            token_copies(0)
            gate_sig(0, 3)
            nc.scalar.preload_act_table_set(LN_EXP)
            for s in range(2):
                t, free, k = HD.wait_full(act, f"das{s}")
                link(fn(daR[:, s * 512:(s + 1) * 512], t[:, :], ACT.Ln, bias=RMS_EPS))
                done(fn(daR[:, s * 512:(s + 1) * 512], daR[:, s * 512:(s + 1) * 512], ACT.Exp, scale=-0.5), free, k)
            nc.scalar.preload_act_table_set(SIGMOID)
            gate_sig(1, 0)
            act.wait_ge(o_ready, 2)
            for hf in range(2):
                NT, X, XT, YY, NL, AKT, RBT, RKT, tok, Y0, UP, WAT, ST = rw_mats(hf)
                if hf:
                    token_copies(hf)
                    gn_square(0)
                    nc.scalar.preload_act_table_set(LN_EXP)
                    gn_rstd(0)
                    nc.scalar.preload_act_table_set(SIGMOID)
                    gate_sig(2, 0)
                for hp in range(2):
                    t, free, k = RW.wait_full(act, f"{hf}x1_{hp}")
                    done(fn(X[:, hp * 512:(hp + 1) * 512], t[:, :], ACT.Copy), free, k)
                for i, b in enumerate(LEVELS[1:6]):
                    for hp in range(2):
                        t, free, k = RW.wait_full(act, f"{hf}y{b}_{hp}")
                        done(fn(YY[:, hp * 512:(hp + 1) * 512], t[:, :], ACT.Copy), free, k)
                    if i % 2:
                        gate_sig(1 + hf, 1 + i // 2)
                    if b < 32:
                        for hp in range(2):
                            t, free, k = RW.wait_full(act, f"{hf}xx{b}_{hp}")
                            done(fn(X[:, hp * 512:(hp + 1) * 512], t[:, :], ACT.Copy), free, k)
                for hp in range(2):
                    t, free, k = RW.wait_full(act, f"{hf}y0_{hp}")
                    done(fn(tiles(Y0, 4)[:, :, hp * 64:hp * 64 + 64], tiles(t[:, :], 4)[:, :, hp * 64:hp * 64 + 64],
                            ACT.Copy), free, k)
                for hp in range(2):
                    t, free, k = RW.wait_full(act, f"{hf}up_{hp}")
                    done(fn(tiles(UP, 4)[:, :, hp * 64:hp * 64 + 64], tiles(t[:, :], 4)[:, :, hp * 64:hp * 64 + 64],
                            ACT.Copy), free, k)
                t, free, k = RW.wait_full(act, f"{hf}wat")
                done(fn(WAT, t[:, :], ACT.Copy), free, k)
                gate_sig(1 + hf, 3)
                t, free, k = RW.wait_full(act, f"{hf}o")
                done(fn(o_rw[:, hf * 512:(hf + 1) * 512], t[:, :], ACT.Copy), free, k)
                act.nop().then_inc(orw_copied, 1)
            gn_square(1)
            nc.scalar.preload_act_table_set(LN_EXP)
            gn_rstd(1)
            def squares(n0):
                for i in range(n0, n0 + 4):
                    sl = slice((i - n0) * 512, (i - n0 + 1) * 512)
                    act.wait_ge(lnd, i + 1)
                    fn(LNT[:, sl], xT[:, sl], ACT.Square).then_inc(lnsq, 1)

            squares(0)
            t, free, k = PJ.wait_full(act, "ln1v")
            link(fn(LNT[:, 0:T], t[:, 0:T], ACT.Ln, bias=LN_EPS))
            done(fn(LNT[:, 0:T], LNT[:, 0:T], ACT.Exp, scale=-0.5), free, k)
            for m in range(1, KT, 2):
                act.wait_ge(xh_ready, m // 2 + 1)
                fn(tiles(U2, KT)[:, m, :], tiles(xT, KT)[:, m, :], ACT.Identity, bias=u2_b[:, m:m + 1],
                   scale=u2_s[:, m:m + 1]).then_inc(u2_odd, 1)
            t, free, k = PJ.wait_full(act, "logit")
            done(fn(lgT[0:E, :], t[0:E, 0:T], ACT.Copy), free, k)
            for i in range(4):
                if i == 1:
                    act.wait_ge(lg_exp_in, 1)
                    done(fn(scores, scores, ACT.Exp), lg_exp, 1)
                t, free, k = PJ.wait_full(act, f"u2t{i}")
                done(fn(U2K[:, i * 512:(i + 1) * 512], t[:, :], ACT.Copy), free, k)

            def gathered(n, half):
                act.wait_ge(xg_full, 2 * n + half + 1)
                done(fn(XG[:, half * 512:(half + 1) * 512], bank[half][:, :], ACT.Copy), xg_ready, 2 * n + half + 1)

            def pair(n, more):
                act.wait_ge(gate_full, n + 1)
                done(fn(GH, bank[2][:, :], ACT.Sigmoid), sig_ready, n + 1)
                act.wait_ge(pw_full, n + 1)
                done(fn(PWT, bank[7][:, 0:T], ACT.Copy), pw_copied, n + 1)
                if more:
                    act.wait_ge(up_full, n + 1)
                    gathered(n + 1, 0)
                act.wait_ge(hT_full, n + 1)
                done(fn(HT_, bank[4][:, :], ACT.Copy), hT_ready, n + 1)
                if more:
                    gathered(n + 1, 1)
                for half in range(2):
                    act.wait_ge(y_full, 2 * n + half + 1)
                    done(fn(Y[:, half * 512:(half + 1) * 512], bank[5 + half][:, :], ACT.Copy), y_ready, 2 * n + half + 1)

            def one_pass(n0):
                gathered(n0, 0)
                gathered(n0, 1)
                with act.Fori(0, PAIRS - 1) as p:
                    pair(n0 + p, True)
                pair(n0 + PAIRS - 1, False)

            nc.scalar.preload_act_table_set(SIGMOID)
            one_pass(0)
            act.wait_ge(flag_ready, 1)
            over_ = act.value_load(flag_i[0:1, 0:1], min_val=0, max_val=1)
            with act.If(over_ > 0):
                with act.Fori(1, PASSES) as b:
                    one_pass(b * PAIRS)
            nc.scalar.preload_act_table_set(LN_EXP)
            squares(4)
            act.wait_ge(ln2_sum, 2)
            link(fn(LNT[:, 0:T], bank[1][:, 0:T], ACT.Ln, bias=LN_EPS))
            done(fn(LNT[:, 0:T], LNT[:, 0:T], ACT.Exp, scale=-0.5), lnr, 1)
            for m in range(KT):
                act.wait_ge(scaled_ready, m // 2 + 1)
                fn(tiles(uT, KT)[:, m, :], tiles(xT, KT)[:, m, :], ACT.Identity, bias=V("ln_b", 8 + m),
                   scale=V("ln_g", 8 + m)).then_inc(x2_ready, 1)

        @block.vector
        def _(dve):
            n = [0]
            v = nc.vector

            def link(ins):
                n[0] += 1
                ins.then_inc(dve_ch, 1)
                dve.wait_ge(dve_ch, n[0])

            def done(ins, s, val):
                ins.then_inc(s, 1)
                dve.wait_ge(s, val)

            def tick(s):
                dve.nop().then_inc(s, 1)

            dve.wait_ge(vec_in, 16)
            dve.wait_ge(cond_sig, 1)
            link(v.tensor_tensor(condc, condc, V("c", 0, 8), ALU.mult))
            done(v.tensor_copy(condb.rearrange("p (k r) -> p k r", k=KT), condc.unsqueeze(2).to_broadcast([P, KT, 32])),
                 cond_ready, 1)
            done(v.tensor_tensor(lbv, V("hg_lb", 0, 4), V("hg_lb", 0, 4), ALU.subtract), lb_in, 1)
            dve.wait_ge(lb_exp, 1)
            link(v.reciprocal(oml, lbv))
            link(v.tensor_tensor(oml, oml, lbv, ALU.mult))
            link(v.tensor_tensor(lbv, oml, oml, ALU.subtract))
            link(v.tensor_scalar(oml, lbv, -1.0, 1.0, ALU.mult, ALU.add))

            def mod_row(r):
                t, free, k = (HD if r else PJ).wait_full(dve, f"ada{r}")
                done(v.tensor_copy(modrow, t[:, :]), free, k)
                tick(modrow_ready)

            def mod_cols(r):
                t, free, k = (HD if r else PJ).wait_full(dve, f"adaT{r}")
                src = t[:, :].rearrange("p (i g x) -> p g i x", i=4, g=4)[:, :, :, 0]
                dst = modc[:, 16 * r:16 * r + 16].rearrange("p (g i) -> p g i", g=4)
                done(v.tensor_tensor(dst, src, V("b_ada", 16 * r, 16).rearrange("p (g i) -> p g i", g=4), ALU.add), free, k)

            mod_row(0)
            mod_cols(0)
            link(v.tensor_scalar(sc1p, modc[:, 8:16], 1.0, None, ALU.add))
            dve.wait_ge(x_in, 16)
            x3, u3 = tiles(xT, KT), tiles(uT, KT)
            for m in range(KT):
                done(v.tensor_scalar(u3[:, m, :], x3[:, m, :], sc1p[:, m:m + 1], modc[:, m:m + 1], ALU.mult, ALU.add),
                     u_ready, m + 1)

            dve.wait_ge(row_in, 48)
            l4 = tiles(lam_sb, 4)
            link(v.tensor_tensor(tiles(lam_t, 2), l4[:, 0:4:2, :], l4[:, 1:4:2, :], ALU.mult))
            done(v.tensor_reduce(lam4[:, 0:2], tiles(lam_t, 2), axis=AX.X, op=ALU.add), lam_ready, 1)

            def shift(*ms):
                for m in ms:
                    PJ.wait_read(dve, f"rw{m // 2}")
                    link(v.tensor_tensor(hb1[:, 0:T], rwx[:, m, 0:T], rwx[:, m, 1:], ALU.subtract))
                    link(v.scalar_tensor_tensor(rwx[:, m, 1:], hb1[:, 0:T], V("mu", m), rwx[:, m, 1:], ALU.mult, ALU.add))

            shift(12, 13)
            tick(xs_ready)
            r3, k3, v3 = [rwx[:, 4 * i:4 * i + 4, 1:] for i in range(3)]
            shift(4, 5, 6, 7)
            kk3, sq3 = tiles(kk, 4), tiles(kk_sq, 4)
            for j in range(4):
                link(v.tensor_scalar(kk3[:, j, :], k3[:, j, :], V("k_k", j), None, ALU.mult))
            tick(kk_ready)

            def cumsum(a, b, save=None):
                for i in range(6):
                    d = 1 << i
                    s_, t_ = (a, b) if i % 2 == 0 else (b, a)
                    sv, tv = [x.rearrange("p (n c) -> p n c", c=C) for x in (s_, t_)]
                    link(v.tensor_tensor(tv[:, :, d:C], sv[:, :, d:C], sv[:, :, 0:C - d], ALU.add))
                    link(v.tensor_copy(tv[:, :, 0:d], sv[:, :, 0:d]))

            dve.wait_ge(lora_done, 1)
            link(v.tensor_copy(cs0, sig_w))
            cumsum(cs0, cs1)
            done(v.tensor_tensor(sig_w, cs0, sig_w, ALU.subtract), cs_ready, 1)
            for j in range(4):
                link(v.tensor_scalar(cs1[:, j * T:(j + 1) * T], a_rw[:, j * T:(j + 1) * T], -1.0, V("k_a", j), ALU.add, ALU.mult))
            link(v.scalar_tensor_tensor(k3, tiles(cs1, 4), 1.0, k3, ALU.add, ALU.mult))
            shift(0, 1, 2, 3)

            def rw_key_norm():
                for i in range(2):
                    t, free, k = RW.wait_full(dve, f"kk{i}")
                    done(v.tensor_scalar(kk_sq[:, i * 512:(i + 1) * 512], t[:, :], 1e-12, None, ALU.max), free, k)
                tick(kk_n)

            def rw_bonus_product():
                dve.wait_ge(kk_n, 2)
                link(v.tensor_tensor(kk, kk, kk_sq, ALU.mult))
                link(v.tensor_tensor(sq3, r3, k3, ALU.mult))
                for j in range(4):
                    link(v.tensor_scalar(sq3[:, j, :], sq3[:, j, :], V("r_k", j), None, ALU.mult))
                tick(rk_ready)

            def rw_a_factor():
                dve.wait_ge(dec_ready, 1)
                link(v.scalar_tensor_tensor(at_f, kk, -1.0, sig_w, ALU.mult, ALU.mult))
                link(v.tensor_tensor(a_rw, a_rw, kk, ALU.mult))

            def rw_bk_factors():
                link(v.tensor_tensor(a_rw, a_rw, g_inv, ALU.mult))
                link(v.tensor_tensor(tiles(kt_f, 4), k3, tiles(g_inv, 4), ALU.mult))

            def rw_r_factor():
                link(v.tensor_tensor(tiles(rt_f, 4), r3, tiles(cs0, 4), ALU.mult))
                link(v.tensor_copy(gend.rearrange("p (n c) -> p n c", c=1), cs0.rearrange("p (n c) -> p n c", c=C)[:, :, C - 1:C]))

            def rw_bonus():
                dve.wait_ge(v_ready, 1)
                for i in range(2):
                    t, free, k = RW.wait_full(dve, f"bo{i}")
                    done(v.tensor_tensor(tiles(bonus, 4)[:, 2 * i:2 * i + 2, :], tiles(t[:, :], 2), v3[:, 2 * i:2 * i + 2, :],
                                         ALU.mult), free, k)
                tick(rwf_ready)

            PJ.wait_read(dve, "hgf1")
            hb03, hk3 = tiles(hb0, 4), tiles(hk, 4)
            for h in range(H4):
                link(v.tensor_scalar(hb03[:, h, :], hb03[:, h, :], oml[:, h:h + 1], lbv[:, h:h + 1], ALU.mult, ALU.add))
                link(v.tensor_scalar(hk3[:, h, :], hk3[:, h, :], oml[:, h:h + 1], None, ALU.mult))
            done(v.tensor_scalar(hb0, hb0, 1e-6, None, ALU.max), f_ready, 1)
            rw_key_norm()
            dve.wait_ge(logf_ready, 1)
            cumsum(hb0, hb1)
            PJ.wait_read(dve, "hgq1")
            hcs = hb0.rearrange("p (n c) -> p n c", c=C)
            ev = lvE.rearrange("p (n c) -> p n c", c=C)
            done(v.tensor_tensor(ev, hcs, hcs[:, :, C - 1:C].to_broadcast([P, 16, C]), ALU.subtract), dec_in, 1)
            far = small[:, 184:192]
            ends = hcs[:, :, C - 1:C].rearrange("p (h c) x -> p h (c x)", h=4)[:, :, 1:3]
            link(v.tensor_copy(far.rearrange("p (h c) -> p h c", h=4), ends))
            rw_bonus_product()
            dve.wait_ge(dec_out, 1)
            tick(dec_in)
            link(v.tensor_tensor(lvK, hk, lvE, ALU.mult))
            link(v.tensor_tensor(lvQ, o_hg, lvQ, ALU.mult))
            tick(lev_ready)
            dve.wait_ge(dec_out, 2)
            K128, Q128 = tiles(lvX, 8)[:, 0:4, :], tiles(lvX, 8)[:, 4:8, :]
            f3 = far.rearrange("p (h c) -> p h c", h=4)
            Kl, Ql = tiles(lvK, 4), tiles(lvQ, 4)
            link(v.tensor_tensor(K128[:, :, 0:C], Kl[:, :, 0:C], f3[:, :, 0:1].to_broadcast([P, 4, C]), ALU.mult))
            link(v.tensor_copy(K128[:, :, C:P], Kl[:, :, C:P]))
            link(v.tensor_copy(Q128[:, :, 0:C], Ql[:, :, P:P + C]))
            link(v.tensor_tensor(Q128[:, :, C:P], Ql[:, :, P + C:T], f3[:, :, 1:2].to_broadcast([P, 4, C]), ALU.mult))
            tick(lev_ready)
            A4 = scoresT.rearrange("p (a h t) -> p a h t", a=3, h=H4)

            def take_scores(b, first):
                for s in range(2):
                    t, free, k = HD.wait_full(dve, f"a{b}_{s}")
                    m = over(M(f"lev{b}" if b else "quad"), 4)
                    if first:
                        done(v.tensor_tensor(A4[:, s], tiles(t[:, :], 4), m, ALU.mult), free, k)
                    else:
                        done(v.tensor_tensor(tiles(hb1[:, 0:512], 4), tiles(t[:, :], 4), m, ALU.mult), free, k)
                        link(v.tensor_tensor(A4[:, s], A4[:, s], tiles(hb1[:, 0:512], 4), ALU.add))

            take_scores(64, True)
            t, free, k = HD.wait_full(dve, "a128")
            done(v.tensor_copy(A4[:, 2], tiles(t[:, :], 4)), free, k)
            prev = None
            for i, b in enumerate((32, 16, 8, 4, 0)):
                w = 2 * b if b else 4
                nn = 1024 // w
                bv, e_ = [x.rearrange("p (n c) -> p n c", c=w) for x in (hb0, lvE)]
                if not b:
                    take_scores(prev, False)
                if b:
                    ref = bv[:, :, b - 1:b].to_broadcast([P, nn, b])
                    link(v.tensor_tensor(e_[:, :, 0:b], bv[:, :, 0:b], ref, ALU.subtract))
                    done(v.tensor_tensor(e_[:, :, b:w], ref, bv[:, :, b:w], ALU.subtract), dec_in, 3 + i)
                else:
                    ref = bv[:, :, 1:2].to_broadcast([P, nn, w])
                    done(v.tensor_tensor(e_, bv, ref, ALU.subtract), dec_in, 3 + i)
                if i and b:
                    take_scores(prev, False)
                prev = b
                if i == 0:
                    rw_a_factor()
                elif i == 1:
                    rw_bk_factors()
                elif i == 2:
                    rw_r_factor()
                elif i == 3:
                    rw_bonus()
                dve.wait_ge(dec_out, 3 + i)
                link(v.tensor_tensor(lvK, hk, lvE, ALU.mult))
                link(v.tensor_tensor(lvQ, o_hg, lvE if b else lvQ, ALU.mult))
                tick(lev_ready)
            take_scores(0, False)
            PJ.wait_read(dve, "hgv1")
            tick(at_ready)
            HD.wait_read(dve, "hgo1")
            HD.wait_read(dve, "hgo0")
            for s in range(2):
                HD.wait_read(dve, f"hgs{s}")
                o = tiles(o_hg, 4)[:, :, s * P:(s + 1) * P]
                link(v.scalar_tensor_tensor(o, o, V("hg_norm"), tiles(lvK[:, s * 512:(s + 1) * 512], 4), ALU.mult, ALU.mult))

            S8 = tiles(att, 8)
            dist = mix_cst[:, DIST0:DIST0 + 3 * P]
            for h in range(H4):
                slope = 2.0 ** (-8.0 * (h + 1) / H4)
                for m in range(2):
                    t, free, k = HD.wait_full(dve, f"s{h}_{m}")
                    done(v.scalar_tensor_tensor(S8[:, 2 * h + m, :], dist, -slope, t[:, 0:3 * P], ALU.mult, ALU.add), free, k)
                for (c0, c1, o) in ((0, P, 0), (P, 3 * P, 8)):
                    link(v.tensor_reduce(smx[:, 32 + o + 2 * h:34 + o + 2 * h], S8[:, 2 * h:2 * h + 2, c0:c1], axis=AX.X, op=ALU.max))
                    link(v.tensor_scalar(smx[:, o + 2 * h:o + 2 * h + 2], smx[:, 32 + o + 2 * h:34 + o + 2 * h], -1.0, None, ALU.mult))
                tick(nmax_ready)
            dve.wait_ge(lam_exp, 1)
            link(v.tensor_tensor(lam4[:, 4:5], lam4[:, 2:3], lam4[:, 3:4], ALU.subtract))
            link(v.tensor_scalar(lam4[:, 5:6], lam4[:, 4:5], LAM_INIT, -1.0, ALU.add, ALU.mult))
            sums, recips = [smx[:, c:c + 16].rearrange("p (o i) -> p o i", o=2) for c in (16, 48)]
            for h in range(H4):
                dve.wait_ge(e_ready, 2 * h + 2)
                link(v.reciprocal(recips[:, :, 2 * h:2 * h + 2], sums[:, :, 2 * h:2 * h + 2]))
                link(v.tensor_scalar(recips[:, :, 2 * h + 1], recips[:, :, 2 * h + 1], lam4[:, 5:6], None, ALU.mult))
                for (c0, c1, o) in ((0, P, 48), (P, 3 * P, 56)):
                    link(v.tensor_scalar(S8[:, 2 * h, c0:c1], S8[:, 2 * h, c0:c1], smx[:, o + 2 * h:o + 2 * h + 1], None, ALU.mult))
                    link(v.scalar_tensor_tensor(S8[:, 2 * h, c0:c1], S8[:, 2 * h + 1, c0:c1], smx[:, o + 2 * h + 1:o + 2 * h + 2],
                                                S8[:, 2 * h, c0:c1], ALU.mult, ALU.add))
            tick(p_ready)
            dve.wait_ge(hog_sig, 1)
            link(v.tensor_tensor(hog, hog, hog_s, ALU.mult))
            link(v.tensor_tensor(o_hg, o_hg, hog, ALU.mult))
            tick(o_ready)
            link(v.tensor_scalar(lam4[:, 6:7], V("da_subln"), 1.0 - LAM_INIT, None, ALU.mult))
            HD.wait_read(dve, "dao1")
            HD.wait_read(dve, "dao0")
            for s in range(2):
                HD.wait_read(dve, f"das{s}")
                o = tiles(o_da, 4)[:, :, s * P:(s + 1) * P]
                link(v.scalar_tensor_tensor(o, o, lam4[:, 6:7], tiles(daR[:, s * 512:(s + 1) * 512], 4), ALU.mult, ALU.mult))
            tick(o_ready)

            def gn_centre(hf):
                dve.wait_ge(orw_copied, hf + 1)
                o = o_rw[:, hf * 512:(hf + 1) * 512]
                t, free, k = RW.wait_full(dve, f"{hf}gm")
                done(v.tensor_tensor(o, o, t[:, :], ALU.subtract), free, k)
                tick(go_d)

            def gn_finish(hf):
                o = o_rw[:, hf * 512:(hf + 1) * 512]
                RW.wait_read(dve, f"{hf}gv")
                link(v.tensor_tensor(o, o, kk_gn(hf), ALU.mult))
                for jj in range(2):
                    j = 2 * hf + jj
                    link(v.tensor_scalar(o_rw[:, j * T:(j + 1) * T], o_rw[:, j * T:(j + 1) * T], V("gn_g", j), V("gn_b", j),
                                         ALU.mult, ALU.add))
                link(v.tensor_tensor(o, o, bonus[:, hf * 512:(hf + 1) * 512], ALU.add))
                link(v.tensor_tensor(o, o, g_rw[:, hf * 512:(hf + 1) * 512], ALU.mult))
                tick(o_ready)

            for hf in range(2):
                NT, X, XT, YY, NL, AKT, RBT, RKT, tok, Y0, UP, WAT, ST = rw_mats(hf)
                if hf:
                    gn_centre(0)
                for i, (dst, mask) in enumerate(((NT, "strict"), (AKT, "strict"), (RBT, "incl"), (RKT, "incl"))):
                    if i == 1:
                        link(v.tensor_tensor(tiles(XT, 8), tiles(NT, 8), over(M("lev1"), 8), ALU.mult))
                        done(v.tensor_tensor(tiles(XT, 8), tiles(XT, 8), over(M("ident"), 8), ALU.add), xt_ready, hf + 1)
                    for hp in range(2):
                        t, free, k = RW.wait_full(dve, f"{hf}m{i}_{hp}")
                        done(v.tensor_tensor(tiles(dst[:, hp * 512:(hp + 1) * 512], 4), tiles(t[:, :], 4), over(M(mask), 4),
                                             ALU.mult), free, k)
                        tick(m_ready)
                link(v.memset(ST[:, 0:2 * P], 0.0))
                for i, b in enumerate(LEVELS[1:6]):
                    for hp in range(2):
                        t, free, k = RW.wait_full(dve, f"{hf}xt{b}_{hp}")
                        d_ = XT[:, hp * 512:(hp + 1) * 512]
                        done(v.tensor_tensor(d_, d_, t[:, :], ALU.add), free, k)
                if hf:
                    gn_finish(0)
                mod_row(1 + hf)
                RW.wait_read(dve, f"{hf}up_0")
                RW.wait_read(dve, f"{hf}up_1")
                U4 = UP.rearrange("p (j s d) -> p j s d", j=2, s=2)
                for c in range(NCH):
                    s, r = c // 2, slice((c % 2) * 64, (c % 2) * 64 + 64)
                    if c:
                        t, free, k = RW.wait_full(dve, f"{hf}u{c}")
                        done(v.tensor_tensor(U4[r, :, s, :], U4[r, :, s, :], tiles(t[:, 0:256], 2)[r], ALU.add), free, k)
                    if c < NCH - 1:
                        t, free, k = RW.wait_full(dve, f"{hf}s{c}")
                        nxt = tiles(ST[:, (c + 1) * 256:(c + 2) * 256], 2)
                        done(v.tensor_tensor(nxt, tiles(t[:, 0:256], 2), over(M("pair"), 2), ALU.mult), free, k)
                        link(v.tensor_tensor(nxt, nxt, tiles(ST[:, c * 256:(c + 1) * 256], 2), ALU.add))
                        for jj in range(2):
                            g = (2 * hf + jj) * 4 + c
                            ins = v.tensor_scalar(nxt[:, jj, :], nxt[:, jj, :], gend[:, g:g + 1], None, ALU.mult)
                            if jj:
                                done(ins, st_ready, 3 * hf + c + 1)
                            else:
                                link(ins)
                mod_cols(1 + hf)

            link(v.tensor_scalar(g1p, modc[:, 16:24], 1.0, None, ALU.add))
            link(v.tensor_scalar(sc2p, modc[:, 32:40], 1.0, None, ALU.add))
            link(v.tensor_scalar(g2p, modc[:, 40:48], 1.0, None, ALU.add))
            link(v.tensor_tensor(u2_s, V("ln_g", 0, 8), sc2p, ALU.mult))
            link(v.tensor_tensor(u2_b, V("ln_b", 0, 8), sc2p, ALU.mult))
            link(v.tensor_tensor(u2_b, u2_b, modc[:, 24:32], ALU.add))
            link(v.tensor_scalar(res_s, V("ln_g", 0, 8), ALPHA, None, ALU.mult))
            done(v.tensor_scalar(res_b, V("ln_b", 0, 8), ALPHA, None, ALU.mult), fold_ready, 1)

            for b in range(3):
                for i in range(4):
                    PJ.wait_read(dve, f"gate{b}_{i}")
                    t, free, k = PJ.wait_full(dve, f"br{b}_{i}")
                    g = gates[b][:, i * 512:(i + 1) * 512]
                    done(v.tensor_tensor(g, g, t[:, :], ALU.mult), free, k)
                    if b:
                        m_ = gates[0][:, i * 512:(i + 1) * 512]
                        link(v.tensor_tensor(m_, m_, g, ALU.add))
                    if b == 2:
                        tick(merged_ready)
                    if b == 0 and i == 0:
                        gn_centre(1)
                    elif b == 0 and i == 1:
                        gn_finish(1)
            dve.wait_ge(x_scaled, 1)
            for i in range(4):
                t, free, k = PJ.wait_full(dve, f"out{i}")
                for j in range(2):
                    m = 2 * i + j
                    ins = v.scalar_tensor_tensor(x3[:, m, :], t[:, j * T:(j + 1) * T], g1p[:, m:m + 1], x3[:, m, :],
                                                 ALU.mult, ALU.add)
                    if j:
                        done(ins, free, k)
                    else:
                        link(ins)
                tick(y1_ready)

            def centre(mean, n0):
                for i in range(4):
                    q = x3[:, 2 * i:2 * i + 2, :]
                    done(v.tensor_tensor(q, q, over(mean, 2), ALU.subtract), lnd, n0 + i + 1)

            t, free, k = PJ.wait_full(dve, "ln1m")
            centre(t[:, 0:T], 0)
            dve.nop().then_inc(free, 1)
            PJ.wait_read(dve, "ln1v")
            for i in range(4):
                q = x3[:, 2 * i:2 * i + 2, :]
                done(v.tensor_tensor(q, q, over(LNT[:, 0:T], 2), ALU.mult), xh_ready, i + 1)

            s3 = scores.rearrange("p (b e) -> p b e", b=2)
            t, free, k = PJ.wait_full(dve, "logitT")
            done(v.tensor_copy(scores, t[:, 0:2 * E]), free, k)
            link(v.tensor_reduce(rt2[:, 0:2], s3, axis=AX.X, op=ALU.max))
            done(v.tensor_tensor(s3, s3, rt2[:, 0:2].unsqueeze(2).to_broadcast([P, 2, E]), ALU.subtract), lg_exp_in, 1)
            dve.wait_ge(lg_exp, 1)
            link(v.tensor_reduce(rt2[:, 0:2], s3, axis=AX.X, op=ALU.add))
            link(v.reciprocal(rt2[:, 2:4], rt2[:, 0:2]))
            link(v.tensor_tensor(s3, s3, rt2[:, 2:4].unsqueeze(2).to_broadcast([P, 2, E]), ALU.mult))
            sel = route[:, 84:116]
            link(v.tensor_tensor(sel.rearrange("p (b e) -> p b e", b=2), s3, RB.unsqueeze(1).to_broadcast([P, 2, E]), ALU.add))
            s4 = sel.rearrange("p (n j) -> p n j", j=4)
            big, big2 = Y[:, 0:128], Y[:, 128:256]
            tie = cst[:, TIE0:TIE0 + 16].rearrange("p (j i) -> p j i", j=4)

            def ranks(vals, nn, out_):
                w = nn * 16
                b3 = big[:, 0:w].rearrange("p (n j i) -> p n j i", j=4, i=4)
                c3 = big2[:, 0:w].rearrange("p (n j i) -> p n j i", j=4, i=4)
                vi = vals.unsqueeze(2).to_broadcast([P, nn, 4, 4])
                vj = vals.unsqueeze(3).to_broadcast([P, nn, 4, 4])
                link(v.tensor_tensor(b3, vi, vj, ALU.is_gt))
                link(v.tensor_tensor(c3, vi, vj, ALU.is_equal))
                link(v.tensor_tensor(c3, c3, tie.unsqueeze(1).to_broadcast([P, nn, 4, 4]), ALU.mult))
                link(v.tensor_tensor(b3, b3, c3, ALU.add))
                link(v.tensor_reduce(out_, b3, axis=AX.X, op=ALU.add))

            rk = route[:, 116:148]
            ranks(s4, 8, rk.rearrange("p (n j) -> p n j", j=4))
            top2 = route[:, 148:180]
            link(v.tensor_scalar(top2, rk, 2.0, None, ALU.is_lt))
            gs = route[:, 180:188]
            link(v.tensor_tensor(rk, top2, sel, ALU.mult))
            link(v.tensor_reduce(gs, rk.rearrange("p (n j) -> p n j", j=4), axis=AX.X, op=ALU.add))
            grk = route[:, 188:196]
            ranks(gs.rearrange("p (n j) -> p n j", j=4), 2, grk.rearrange("p (n j) -> p n j", j=4))
            link(v.tensor_scalar(grk, grk, 1.0, None, ALU.is_lt))
            for dst in (chosen16, chosen):
                ins = v.tensor_tensor(dst.rearrange("p (n j) -> p n j", j=4), top2.rearrange("p (n j) -> p n j", j=4),
                                      grk.unsqueeze(2).to_broadcast([P, 8, 4]), ALU.mult)
                if dst is chosen16:
                    done(ins, chosen_ready, 1)
                else:
                    link(ins)
            link(v.tensor_tensor(scores, scores, chosen, ALU.mult))
            link(v.tensor_reduce(rt2[:, 0:2], s3, axis=AX.X, op=ALU.add))
            link(v.reciprocal(rt2[:, 2:4], rt2[:, 0:2]))
            link(v.tensor_tensor(s3, s3, rt2[:, 2:4].unsqueeze(2).to_broadcast([P, 2, E]), ALU.mult))
            t, free, k = PJ.wait_full(dve, "rank")
            link(v.scalar_tensor_tensor(slot, t[:, 0:2 * E], 1.0, chosen, ALU.add, ALU.mult))
            done(v.tensor_reduce(rt2[:, 0:1], t[:, 2 * E:3 * E], axis=AX.X, op=ALU.max), free, k)

            iota = cst[:, IOTA0:IOTA0 + CAP]

            def picks(p, n_):
                for i, (dst, src) in enumerate(((PK, slot), (PW, scores))):
                    for s in range(2):
                        d = dst[:, s * P:(s + 1) * P].rearrange("p (e j) -> p e j", e=2)
                        of = src[:, bass.ds(2 * p + s * E, 2)].unsqueeze(2).to_broadcast([P, 2, CAP])
                        a_ = PK[:, s * P:(s + 1) * P].rearrange("p (e j) -> p e j", e=2) if i else over(iota, 2)
                        done(v.tensor_tensor(d, a_, of, ALU.mult if i else ALU.is_equal), pick_ch, 4 * n_ + 2 * i + s + 1)
                    tick(pw_ready if i else pick_ready)

            def pair(p, n_, more):
                dve.wait_ge(sig_ready, n_ + 1)
                done(v.tensor_tensor(GH, bank[2][:, :], GH, ALU.mult), moe_ch, n_ + 1)
                if more:
                    dve.wait_ge(xg_full, 2 * n_ + 2)
                    dve.wait_ge(pw_full, n_ + 1)
                    picks(p + 1, n_ + 1)
                dve.wait_ge(up_full, n_ + 1)
                done(v.tensor_tensor(GH, bank[3][:, :], GH, ALU.mult), h_ready, n_ + 1)
                for i in range(4):
                    dve.wait_ge(comb_full, 4 * n_ + i + 1)
                    bk = comb_bank[i % 2]
                    for j in range(2):
                        m = 2 * i + j
                        ins = v.scalar_tensor_tensor(x3[:, m, :], bk[:, j * T:(j + 1) * T], g2p[:, m:m + 1], x3[:, m, :],
                                                     ALU.mult, ALU.add)
                        if j:
                            done(ins, comb_added, 4 * n_ + i + 2)
                        else:
                            done(ins, comb_half, 4 * n_ + i + 1)

            def all_pairs(n0):
                with dve.Fori(0, PAIRS - 1) as p:
                    pair(p, n0 + p, True)
                pair(PAIRS - 1, n0 + PAIRS - 1, False)

            picks(0, 0)
            done(v.tensor_scalar(flag_i[0:1, 0:1], rt2[0:1, 0:1], float(CAP), None, ALU.is_gt), flag_ready, 1)
            dve.wait_ge(res_ready, KT)
            tick(comb_added)
            all_pairs(0)
            over_ = dve.value_load(flag_i[0:1, 0:1], min_val=0, max_val=1)
            with dve.If(over_ > 0):
                with dve.Fori(1, PASSES) as b:
                    done(v.tensor_scalar(slot, slot, -float(CAP), None, ALU.add), blk_ch, b)
                    picks(0, b * PAIRS)
                    all_pairs(b * PAIRS)

            dve.wait_ge(ln2_sum, 1)
            centre(bank[0][:, 0:T], 4)
            dve.wait_ge(lnr, 1)
            for i in range(4):
                q = x3[:, 2 * i:2 * i + 2, :]
                done(v.tensor_tensor(q, q, over(LNT[:, 0:T], 2), ALU.mult), scaled_ready, i + 1)


_INS = ["xt", "w_ada", "w_in", "w_merge", "w_branch", "w_out", "w_router", "w_gate", "w_up", "w_down",
        "vecs", "consts", "lam_row", "rbias_row", "rw_w_up", "rw_a_up", "rw_g_up"]


def _constants():
    import numpy as np
    i = np.arange(P)
    s, t = i[:, None], i[None, :]
    same = lambda w: (s // w) == (t // w)
    m = {"ident": s == t, "ones_d": np.full((P, P), 1.0 / D), "ones_dv": np.full((P, P), 1.0 / P),
         "pair": same(64), "pair_mean": same(64) / 64.0, "ones": np.ones((P, P)),
         "quad": same(4) & (s <= t), "strict": same(C) & (s < t), "incl": same(C) & (s <= t), "before": s < t}
    for b in LEVELS:
        m[f"lev{b}"] = same(2 * b) & (s % (2 * b) < b) & (t % (2 * b) >= b)
    own = np.where(s >= t, s - t, 1e33)
    dist = np.concatenate([own, s - t + P, own], 1)
    iota = np.broadcast_to(np.arange(1, CAP + 1), (P, CAP))
    j4 = np.arange(4)
    tie = np.broadcast_to((j4[None, :] < j4[:, None]).reshape(1, 16), (P, 16))
    return np.concatenate([np.asarray(x, np.float32) for x in
                           [m[n] for n in KEPT_MATS] + [iota, tie] + [m[n] for n in MIX_MATS] + [dist]], 1)


def kernel(**inputs):
    import numpy as np
    import concourse.bacc as bacc
    from concourse.bass_utils import run_bass_kernel_spmd

    a = {k: np.asarray(x) for k, x in inputs.items()}

    def by_channel(w):
        return w.reshape(-1, P, w.shape[-1])

    cols = lambda x: x.reshape(-1, P).T
    parts = {"c": a["c"], "b_ada": a["b_ada"], "hg_lb": a["hg_lb_logits"], "hg_norm": a["hg_norm_g"],
             "da_subln": a["da_subln_g"], "mu": a["rw_mu"], "w0": a["rw_w0"], "a0": a["rw_a0"], "k_k": a["rw_k_k"],
             "k_a": a["rw_k_a"], "r_k": a["rw_r_k"], "gn_g": a["rw_gn_g"], "gn_b": a["rw_gn_b"],
             "b_merge": a["b_merge"], "ln_g": a["ln_g"], "ln_b": a["ln_b"]}
    arrays = {
        "xt": by_channel(a["x"][0].T), "w_ada": by_channel(a["w_ada"][0]), "w_in": by_channel(a["w_in"][0]),
        "w_merge": a["w_merge"][0].reshape(3, KT, P, D), "w_branch": by_channel(a["w_branch"][0]),
        "w_out": by_channel(a["w_out"][0]), "w_router": by_channel(a["w_router"]),
        "w_gate": a["w_exp_gate"][0].reshape(E, KT, P, FE), "w_up": a["w_exp_up"][0].reshape(E, KT, P, FE),
        "w_down": a["w_exp_down"][0].reshape(E, FE // P, P, D),
        "vecs": np.concatenate([cols(parts[n]) for n, _ in VECS], 1), "consts": _constants(),
        "lam_row": a["da_lambda"].reshape(1, 256), "rbias_row": a["router_bias"].reshape(1, E),
        "rw_w_up": a["rw_w_up"][0], "rw_a_up": a["rw_a_up"][0], "rw_g_up": a["rw_g_up"][0],
    }
    arrays = {k: np.ascontiguousarray(x) for k, x in arrays.items()}
    nc = bacc.Bacc("TRN2", target_bir_lowering=False, num_devices=1)
    d = {n: nc.dram_tensor(f"in_{n}", arrays[n].shape, mybir.dt.from_np(arrays[n].dtype), kind="ExternalInput").ap()
         for n in _INS}
    for n in ("xt", "w_ada", "w_in", "w_branch", "w_out", "w_router"):
        d[n] = d[n].rearrange("k p c -> p k c")
    d["w_merge"] = d["w_merge"].rearrange("b k p c -> p b k c")
    for n in ("w_gate", "w_up", "w_down"):
        d[n] = d[n].rearrange("e k p c -> e p k c")
    out = nc.dram_tensor("out_t", (KT, P, T), F32, kind="ExternalOutput").ap().rearrange("k p c -> p k c")
    build(nc, out=out, **d)
    r = run_bass_kernel_spmd(nc, [{f"in_{n}": arrays[n] for n in _INS}], core_ids=[0])
    return np.ascontiguousarray(r.results[0]["out_t"].reshape(D, T).T).reshape(1, T, D)
```
